# Optimizing a Trainium2 kernel written in Bass

```python
import jax, jax.numpy as jnp
from jax import lax
import numpy as np

D_MODEL = 1024
BATCH = 1
SEQ = 256
DEPTH = 1
DEC_BATCH = 8
DEC_SEQ = 1
PAST_LEN = 2048
PAGE_SIZE = 128

N_META = 16
RET_HEADS = 4
RET_DK = 128
RET_DV = 256
RET_QK = RET_HEADS * RET_DK
RET_V = RET_HEADS * RET_DV
CHUNK = 128
LEAD_PAD = (-N_META) % CHUNK
ROPE_BASE = 10000.0
POOL_WINDOWS = (2, 4, 8, 16)
POOL_GROUPS = 4
POOL_GROUP_DIM = D_MODEL // 8
POOL_WIDTH = POOL_GROUPS * POOL_GROUP_DIM
POOL_BUF = max(POOL_WINDOWS) - 1
N_EXPERTS = 32
TOP_K = 4
D_FF = D_MODEL
SWIGLU_LIMIT = 7.0
SWIGLU_ALPHA = 1.702
MOE_BLOCK = 128
EPS = 1e-6
IN_WIDTHS = (RET_QK, RET_QK, RET_V, RET_V, POOL_WIDTH, D_MODEL, D_MODEL)
IN_TOTAL = sum(IN_WIDTHS)
IN_SPLITS = tuple(int(s) for s in np.cumsum(IN_WIDTHS)[:-1])

kernel_name = "gated_retention_pool_moe_step"

def rmsnorm(x, g):
    xf = x.astype(jnp.float32)
    y = xf * lax.rsqrt(jnp.mean(xf * xf, axis=-1, keepdims=True) + EPS)
    return (y * g.astype(jnp.float32)).astype(x.dtype)

def rotary(x, pos):
    d = x.shape[-1]
    inv = jnp.power(ROPE_BASE, -jnp.arange(0, d, 2, dtype=jnp.float32) / d)
    ang = pos[:, None] * inv[None, :]
    cos, sin = jnp.cos(ang), jnp.sin(ang)
    x1, x2 = x[..., : d // 2], x[..., d // 2:]
    return jnp.concatenate([x1 * cos - x2 * sin, x2 * cos + x1 * sin], axis=-1)

def retention(q, k, v, S0, chunk):
    B, H, T, dk = q.shape
    dv = v.shape[-1]
    nc = T // chunk
    log_g = jnp.log1p(-jnp.exp2(-5.0 - jnp.arange(H, dtype=jnp.float32)))
    i = jnp.arange(chunk, dtype=jnp.float32)
    diff = i[:, None] - i[None, :]
    mask = jnp.where(diff[None] >= 0, jnp.exp(jnp.maximum(diff, 0.0)[None] * log_g[:, None, None]), 0.0)
    q_dec = jnp.exp((i + 1.0)[None, :] * log_g[:, None])
    k_dec = jnp.exp((chunk - 1.0 - i)[None, :] * log_g[:, None])
    c_dec = jnp.exp(chunk * log_g)

    def to_chunks(a):
        return a.reshape(B, H, nc, chunk, a.shape[-1]).transpose(2, 0, 1, 3, 4)

    def step(S, xs):
        qc, kc, vc = xs
        scores = jnp.einsum('bhid,bhjd->bhij', qc, kc) * mask
        intra = jnp.einsum('bhij,bhjv->bhiv', scores, vc)
        cross = jnp.einsum('bhid,bhdv->bhiv', qc * q_dec[..., None], S)
        S_new = S * c_dec[:, None, None] + jnp.einsum('bhjd,bhjv->bhdv', kc * k_dec[..., None], vc)
        return S_new, intra + cross

    S_fin, o = lax.scan(step, S0, (to_chunks(q), to_chunks(k), to_chunks(v)))
    o = o.transpose(1, 2, 0, 3, 4).reshape(B, H, T, dv)
    return o, S_fin

def pool_mix(p, prev, pos0):
    B, T, W = p.shape
    ext = jnp.concatenate([prev.astype(p.dtype), p], axis=1)
    extf = ext.astype(jnp.float32)
    cs = jnp.concatenate([jnp.zeros((B, 1, W), jnp.float32), jnp.cumsum(extf, axis=1)], axis=1)
    pos = pos0 + jnp.arange(T, dtype=jnp.int32)
    outs = []
    for gi, w in enumerate(POOL_WINDOWS):
        sl = slice(gi * POOL_GROUP_DIM, (gi + 1) * POOL_GROUP_DIM)
        hi = cs[:, POOL_BUF + 1: POOL_BUF + 1 + T, sl]
        lo = cs[:, POOL_BUF + 1 - w: POOL_BUF + 1 - w + T, sl]
        cnt = jnp.minimum(pos + 1, w).astype(jnp.float32)
        outs.append((hi - lo) / cnt[None, :, None])
    pooled = jnp.concatenate(outs, axis=-1) - p.astype(jnp.float32)
    return pooled, ext[:, -POOL_BUF:]

def mixer(u, S0, pool_prev, pos0, lead_pad, chunk, w_in, ret_gn, pool_w, pool_scale,
          w_ret_branch, w_pool_branch, w_out):
    B, T, _ = u.shape
    proj = jnp.einsum('btd,de->bte', u, w_in)
    q, k, v, g, p, ga, gb = jnp.split(proj, IN_SPLITS, axis=-1)

    def heads(a, d):
        return a.reshape(B, T, RET_HEADS, d).transpose(0, 2, 1, 3).astype(jnp.float32)

    pos = (pos0 + jnp.arange(T, dtype=jnp.int32)).astype(jnp.float32)
    qh = rotary(heads(q, RET_DK), pos)
    kh = rotary(heads(k, RET_DK), pos) * (RET_DK ** -0.5)
    vh = heads(v, RET_DV)
    if lead_pad:
        padw = ((0, 0), (0, 0), (lead_pad, 0), (0, 0))
        qh, kh, vh = jnp.pad(qh, padw), jnp.pad(kh, padw), jnp.pad(vh, padw)
    o, S_new = retention(qh, kh, vh, S0.astype(jnp.float32), chunk)
    o = o[:, :, lead_pad:].transpose(0, 2, 1, 3)
    mu = jnp.mean(o, axis=-1, keepdims=True)
    var = jnp.mean(jnp.square(o - mu), axis=-1, keepdims=True)
    o = (o - mu) * lax.rsqrt(var + EPS) * ret_gn.astype(jnp.float32).reshape(RET_HEADS, RET_DV)
    o = o.reshape(B, T, RET_V).astype(u.dtype)
    ya = jnp.einsum('btc,cd->btd', jax.nn.silu(g) * o, w_ret_branch)

    pooled, pool_new = pool_mix(p, pool_prev, pos0)
    pooled = pooled.astype(u.dtype).reshape(B, T, POOL_GROUPS, POOL_GROUP_DIM)
    pooled = jnp.einsum('btgc,gce->btge', pooled, pool_w).reshape(B, T, POOL_WIDTH) * pool_scale
    yb = jnp.einsum('btc,cd->btd', pooled, w_pool_branch)

    merged = jax.nn.sigmoid(ga) * ya + jax.nn.sigmoid(gb) * yb
    return jnp.einsum('btd,de->bte', merged, w_out), S_new.astype(S0.dtype), pool_new

def moe(x, w_router, b_router, w_gate_up, b_gate_up, w_down, b_down):
    B, T, D = x.shape
    xt = x.reshape(B * T, D)
    NT = B * T
    NA = NT * TOP_K
    logits = jnp.einsum('td,de->te', xt, w_router).astype(jnp.float32) + b_router.astype(jnp.float32)
    top_val, top_idx = lax.top_k(logits, TOP_K)
    gates = jax.nn.softmax(top_val, axis=-1)
    flat_e = top_idx.reshape(-1)
    order = jnp.argsort(flat_e)
    sorted_e = flat_e[order]
    counts = jnp.bincount(flat_e, length=N_EXPERTS)
    padded = ((counts + MOE_BLOCK - 1) // MOE_BLOCK) * MOE_BLOCK
    pad_end = jnp.cumsum(padded)
    pad_start = pad_end - padded
    start = jnp.cumsum(counts) - counts
    dest = pad_start[sorted_e] + jnp.arange(NA, dtype=jnp.int32) - start[sorted_e]
    NB = (NA + MOE_BLOCK - 1) // MOE_BLOCK + N_EXPERTS
    row_tok = jnp.full((NB * MOE_BLOCK,), NT, jnp.int32).at[dest].set((order // TOP_K).astype(jnp.int32))
    block_e = jnp.minimum(jnp.searchsorted(pad_end, jnp.arange(NB, dtype=pad_end.dtype) * MOE_BLOCK, side='right'),
                          N_EXPERTS - 1)
    x_pad = jnp.concatenate([xt, jnp.zeros((1, D), xt.dtype)], axis=0)

    def expert_block(args):
        tok, e = args
        xb = x_pad[tok]
        h = jnp.einsum('rd,df->rf', xb, w_gate_up[e]) + b_gate_up[e]
        gate = jnp.minimum(h[:, :D_FF], SWIGLU_LIMIT)
        up = jnp.clip(h[:, D_FF:], -SWIGLU_LIMIT, SWIGLU_LIMIT)
        glu = gate * jax.nn.sigmoid(gate * SWIGLU_ALPHA)
        return jnp.einsum('rf,fd->rd', (up + 1.0) * glu, w_down[e]) + b_down[e]

    out_buf = lax.map(expert_block, (row_tok.reshape(NB, MOE_BLOCK), block_e)).reshape(NB * MOE_BLOCK, D)
    y_sorted = out_buf[dest]
    g_sorted = gates.reshape(-1)[order].astype(y_sorted.dtype)
    y = jnp.zeros((NT, D), y_sorted.dtype).at[order // TOP_K].add(y_sorted * g_sorted[:, None])
    return y.reshape(B, T, D).astype(x.dtype)

def setup_inputs(seed: int = 0) -> dict:
    key = jax.random.key(seed)
    ks = jax.random.split(key, 24)
    f32 = jnp.float32
    nrm = lambda k, shape, s: jax.random.normal(k, shape, f32) * s
    return {
        "x_prompt": nrm(ks[0], (BATCH, SEQ, D_MODEL), 1.0),
        "x_sample": nrm(ks[1], (DEC_BATCH, DEC_SEQ, D_MODEL), 1.0),
        "state_ret": nrm(ks[2], (DEPTH, DEC_BATCH, RET_HEADS, RET_DK, RET_DV), 0.5),
        "state_pool": nrm(ks[3], (DEPTH, DEC_BATCH, POOL_BUF, POOL_WIDTH), 1.0),
        "meta_tokens": nrm(ks[4], (N_META, D_MODEL), 1.0),
        "norm_mix": 1.0 + nrm(ks[5], (DEPTH, D_MODEL), 0.05),
        "w_in": nrm(ks[6], (DEPTH, D_MODEL, IN_TOTAL), D_MODEL ** -0.5),
        "ret_gn": 1.0 + nrm(ks[7], (DEPTH, RET_V), 0.05),
        "pool_w": nrm(ks[8], (DEPTH, POOL_GROUPS, POOL_GROUP_DIM, POOL_GROUP_DIM), POOL_GROUP_DIM ** -0.5),
        "pool_scale": 1.0 + nrm(ks[9], (DEPTH, POOL_WIDTH), 0.05),
        "w_ret_branch": nrm(ks[10], (DEPTH, RET_V, D_MODEL), RET_V ** -0.5),
        "w_pool_branch": nrm(ks[11], (DEPTH, POOL_WIDTH, D_MODEL), POOL_WIDTH ** -0.5),
        "w_out": nrm(ks[12], (DEPTH, D_MODEL, D_MODEL), D_MODEL ** -0.5),
        "norm_ffn": 1.0 + nrm(ks[13], (DEPTH, D_MODEL), 0.05),
        "w_router": nrm(ks[14], (DEPTH, D_MODEL, N_EXPERTS), D_MODEL ** -0.5),
        "b_router": nrm(ks[15], (DEPTH, N_EXPERTS), 0.01),
        "w_gate_up": nrm(ks[16], (DEPTH, N_EXPERTS, D_MODEL, 2 * D_FF), D_MODEL ** -0.5),
        "b_gate_up": nrm(ks[17], (DEPTH, N_EXPERTS, 2 * D_FF), 0.02),
        "w_down": nrm(ks[18], (DEPTH, N_EXPERTS, D_FF, D_MODEL), D_FF ** -0.5),
        "b_down": nrm(ks[19], (DEPTH, N_EXPERTS, D_MODEL), 0.02),
        "norm_final": 1.0 + nrm(ks[20], (D_MODEL,), 0.05),
    }

def reference(x_prompt, x_sample, state_ret, state_pool, meta_tokens, norm_mix, w_in, ret_gn, pool_w,
              pool_scale, w_ret_branch, w_pool_branch, w_out, norm_ffn, w_router, b_router, w_gate_up,
              b_gate_up, w_down, b_down, norm_final):
    B = x_prompt.shape[0]
    meta = jnp.broadcast_to(meta_tokens.astype(x_prompt.dtype)[None], (B, N_META, D_MODEL))
    hp = jnp.concatenate([meta, x_prompt], axis=1)
    hs = x_sample
    S0_p = jnp.zeros((B, RET_HEADS, RET_DK, RET_DV), state_ret.dtype)
    P0_p = jnp.zeros((B, POOL_BUF, POOL_WIDTH), x_prompt.dtype)
    rs_p, ps_p, rs_s, ps_s = [], [], [], []
    for l in range(DEPTH):
        mix_args = (w_in[l], ret_gn[l], pool_w[l], pool_scale[l], w_ret_branch[l], w_pool_branch[l], w_out[l])
        moe_args = (w_router[l], b_router[l], w_gate_up[l], b_gate_up[l], w_down[l], b_down[l])
        mp, Sp, Pp = mixer(rmsnorm(hp, norm_mix[l]), S0_p, P0_p, 0, LEAD_PAD, CHUNK, *mix_args)
        hp = hp + mp
        hp = hp + moe(rmsnorm(hp, norm_ffn[l]), *moe_args)
        ms, Ss, Ps = mixer(rmsnorm(hs, norm_mix[l]), state_ret[l], state_pool[l], PAST_LEN, 0, hs.shape[1],
                           *mix_args)
        hs = hs + ms
        hs = hs + moe(rmsnorm(hs, norm_ffn[l]), *moe_args)
        rs_p.append(Sp); ps_p.append(Pp); rs_s.append(Ss); ps_s.append(Ps)
    y_prompt = rmsnorm(hp[:, N_META:], norm_final)
    y_sample = rmsnorm(hs, norm_final)
    ret_state_prompt = jnp.stack(rs_p)
    pool_state_prompt = jnp.stack(ps_p)
    ret_state_sample = jnp.stack(rs_s)
    pool_state_sample = jnp.stack(ps_s)
    return (y_prompt, y_sample, ret_state_prompt, pool_state_prompt, ret_state_sample, pool_state_sample)


_drawn_inputs = setup_inputs


def setup_inputs(seed=0):
    import zlib

    import numpy as np

    out = dict(_drawn_inputs(seed))
    spreads = {}
    factors = {'b_gate_up': 5.648, 'b_down': 6.54}
    for name, (base, spread) in spreads.items():
        noise = np.random.default_rng([zlib.crc32(name.encode()), seed]).standard_normal(out[name].shape)
        drawn = base * np.exp(spread * noise) if base else spread * noise
        out[name] = __import__('jax').numpy.asarray(drawn.astype(out[name].dtype))
    for name, factor in factors.items():
        out[name] = (out[name] * factor).astype(out[name].dtype)
    return out
```

```python
from contextlib import ExitStack

import numpy as np

import concourse.bass as bass
from concourse import mybir

F32 = mybir.dt.float32
I32 = mybir.dt.int32
U32 = mybir.dt.uint32
ALU = mybir.AluOpType
ACT = mybir.ActivationFunctionType
AX = mybir.AxisListType

P = 128
D = 1024
KD = D // P
NPR, NS, NM = 256, 8, 16
NT = NPR + NS
NA = NT + NM
H, DK, DV = 4, 128, 256
PG = 4
WINDOWS = (2, 4, 8, 16)
PBUF = 15
NE = 32
TOPK = 4
CAP = 64
NPASS = -(-NT // CAP)
NPAIR = NE // 2
ALPHA, LIMIT = 1.702, 7.0
EPS = 1e-6
PAST = 2048
FAR = 4096.0
SLOT = 2048
RING = 12

V0, K0, Q0, P0, G0, GA0, GB0 = 0, 8, 12, 16, 20, 28, 36
PROJ = [*range(8, 16), *range(4, 8), *range(0, 4), *range(24, 28), *range(16, 24), *range(28, 36), *range(36, 44)]
N_IN = len(PROJ)
T_POOL, T_YB, T_YA, T_OUT, T_END = 44, 48, 56, 64, 72

AUX_BANKS = {}
AUX_AFTER = {n: [] for n in range(-1, T_END)}


def _aux(after, name, banks):
    AUX_BANKS[name] = banks
    AUX_AFTER[after].append(name)


for _j in range(8):
    _aux(_j + 1, ("v", _j), (4 + _j % 2,))
for _j in range(4):
    _aux(_j + 10, ("k", _j), (4 + _j % 2,))
_aux(9, ("hist",), (6,))
_aux(15, ("s_meta",), (6, 7))
_aux(17, ("score", 0), (4,))
_aux(18, ("score", 1), (5,))
_aux(19, ("s_next", 0), (6, 7))
_aux(20, ("o", 0), (6, 7))
_aux(21, ("s_next", 1), (4, 5))
_aux(22, ("o", 1), (6, 7))
_aux(23, ("ptok",), (4, 5))
for _b in range(NS):
    _aux(24 + _b, ("outer", _b), ((4, 5), (6, 7))[_b % 2])
_aux(34, ("o_turn",), (6, 7))
for _j in range(8):
    _aux(36 + _j, ("z", _j), (4 + _j % 2,))
AUX = [a for n in range(-1, T_END) for a in AUX_AFTER[n]]
AUX_AT = {a: i for i, a in enumerate(AUX)}


def bank_owner(i):
    last = 0
    for j in range(i):
        if set(AUX_BANKS[AUX[j]]) & set(AUX_BANKS[AUX[i]]):
            last = j + 1
    return last


CHUNKS = ([("in", n) for n in range(0, N_IN, 2)] + [("pb", c) for c in range(2)]
          + [("ret", c) for c in range(4)] + [("out", c) for c in range(4)])
MIX_SLOTS = 4
C_PB = N_IN // 2
C_RET, C_OUT = C_PB + 2, C_PB + 6


def last_tile(i):
    kind, c = CHUNKS[i]
    return {"in": c + 1, "pb": T_YB + 4 * c + 3, "ret": T_YA + 2 * c + 1, "out": T_OUT + 2 * c + 1}[kind]


ROOT_AFTER = {21: 0, 23: 1, 35: 2}

CONST = {}
_o = 0
for _n, _w in (("ident", 128), ("before", 128), ("ones", 128), ("iota", CAP), ("experts", NE), ("passes", 8),
               ("cos", NA), ("sin", NA), ("mask", H * P), ("q_dec", H * P), ("k_dec", H), ("k_dec_meta", H),
               ("eps", 1)):
    CONST[_n] = (_o, _w)
    _o += _w
N_CONST = _o + (-_o) % 4


def constants():
    c = np.zeros((P, N_CONST), np.float32)

    def put(name, v):
        o, w = CONST[name]
        c[:, o:o + w] = v

    i = np.arange(P, dtype=np.float32)
    put("ident", np.eye(P))
    put("before", np.triu(np.ones((P, P)), 1))
    put("ones", 1.0)
    put("iota", np.arange(CAP)[None])
    put("experts", np.arange(NE)[None])
    put("passes", (np.arange(8) * CAP + (np.arange(8) >= NPASS) * 1e6)[None])
    pos = np.concatenate([NM + np.arange(NPR), np.full(NS, PAST), np.arange(NM)]).astype(np.float32)
    inv = np.power(np.float32(10000.0), -np.arange(0, DK, 2, dtype=np.float32) / np.float32(DK)).astype(np.float32)
    ang = (pos[None, :] * np.concatenate([inv, inv])[:, None]).astype(np.float32)
    put("cos", np.cos(ang))
    put("sin", np.sin(ang) * np.where(np.arange(P) < DK // 2, -1.0, 1.0)[:, None])
    g = log_decay()
    diff = i[None, :] - i[:, None]
    mask = [np.where(diff >= 0, np.exp(np.maximum(diff, 0) * g[h]), 0.0) for h in range(H)]
    put("mask", np.concatenate(mask, 1))
    put("q_dec", np.concatenate([np.exp((i + 1) * g[h]) for h in range(H)])[None])
    put("k_dec", np.exp((P - 1 - i)[:, None] * g[None]))
    meta = np.zeros((P, H), np.float32)
    meta[32:32 + NM] = np.exp((NM - 1 - np.arange(NM, dtype=np.float32))[:, None] * g[None])
    put("k_dec_meta", meta)
    put("eps", EPS)
    return c


def log_decay():
    return np.log1p(-np.exp2(np.float32(-5.0) - np.arange(H, dtype=np.float32))).astype(np.float32)


CHUNK_DEC = [float(np.exp(np.float32(P) * g)) for g in log_decay()]
STEP_DEC = [float(np.exp(g)) for g in log_decay()]


def build(nc, ins, outs):
    x_prompt, x_sample, state_ret, state_pool, meta = (
        ins[n] for n in ("x_prompt", "x_sample", "state_ret", "state_pool", "meta_tokens"))
    y_prompt, y_sample, ret_prompt, pool_prompt, ret_sample, pool_sample = outs

    with ExitStack() as ctx:
        def sem(name):
            return ctx.enter_context(nc.semaphore(name))

        def sb(name, n, dt=F32):
            return ctx.enter_context(nc.sbuf_tensor(name, [P, n], dt))

        ring = sb("ring", RING * SLOT)

        def slot(s):
            return ring[:, s * SLOT:(s + 1) * SLOT]

        early = [4 * SLOT]

        def in_ring(n):
            o = early[0]
            early[0] += n
            assert early[0] <= 8 * SLOT
            return ring[:, o:o + n]

        state_s = in_ring(4 * H * DV).rearrange("p (s h v) -> p s h v", s=4, h=H)
        k_only = in_ring(2 * H * DK).rearrange("p (s h d) -> p s h d", s=2, h=H)
        rope_x = in_ring(2 * NA).rearrange("p (s t) -> p s t", s=2)
        rope_y = in_ring(2 * NA).rearrange("p (s t) -> p s t", s=2)
        v_T = in_ring(2 * NA).rearrange("p (s t) -> p s t", s=2)
        hist = in_ring(PG * P)

        consts = sb("consts", N_CONST)

        def const(name):
            o, w = CONST[name]
            return consts[:, o:o + w]

        ident, ones = const("ident"), const("ones")
        tok = sb("tok", 3 * D).rearrange("p (t d) -> p t d", t=3)
        normed = sb("normed", 3 * D).rearrange("p (t d) -> p t d", t=3)
        rows = normed[:, 0, :]
        u_T = sb("u_T", KD * NA).rearrange("p (k t) -> p k t", k=KD)
        params = sb("params", 28 + 16 * NE + KD * NE)
        norm_mix, gn_w, pool_scale, norm_ffn = (params[:, a:b] for a, b in ((0, 8), (8, 16), (16, 20), (20, 28)))
        b_gu = params[:, 28:28 + 16 * NE].rearrange("p (e m) -> p e m", e=NE)
        b_dn = params[:, 28 + 16 * NE:].rearrange("p (e m) -> p e m", e=NE)
        qk = sb("qk", H * NT + H * NA)
        q_T = qk[:, 0:H * NT].rearrange("p (h t) -> p h t", h=H)
        k_T = qk[:, H * NT:].rearrange("p (h t) -> p h t", h=H)
        gate_a = qk[:, 0:KD * NT].rearrange("p (k t) -> p k t", k=KD)
        xn_T = gate_a
        vk = sb("vk", 3 * D + 3 * H * DK)
        v_tok = vk[:, 0:2 * D].rearrange("p (t v) -> p t v", t=2)
        k_tok = vk[:, 2 * D:2 * D + 2 * H * DK].rearrange("p (t d) -> p t d", t=2)
        v_sm = vk[:, 2 * D + 2 * H * DK:3 * D + 2 * H * DK]
        k_sm = vk[:, 3 * D + 2 * H * DK:]
        gate_b = vk[:, 0:KD * NT].rearrange("p (k t) -> p k t", k=KD)
        q_s = sb("q_s", H * NS).rearrange("p (h b) -> p h b", h=H)
        z_T = sb("z_T", KD * NT).rearrange("p (k t) -> p k t", k=KD)
        y_T = z_T
        p_ext_all = sb("p_ext", PG * (NM + NPR))
        p_ext = p_ext_all.rearrange("p (g t) -> p g t", g=PG)
        p_s = sb("p_s", PG * NS).rearrange("p (g b) -> p g b", g=PG)
        hist_sum = sb("hist_sum", PG * NS).rearrange("p (g b) -> p g b", g=PG)
        win = sb("win", 2 * (NM + NPR)).rearrange("p (s t) -> p s t", s=2)
        pooled = sb("pooled", PG * NT).rearrange("p (g t) -> p g t", g=PG)
        rs = sb("rs", 2 * H * DV)
        ret_s = rs.rearrange("p (s h v) -> p s h v", s=2, h=H)
        sc = sb("sc", 2 * H * P)
        scores = sc.rearrange("p (c h i) -> p c h i", c=2, h=H)
        qd = sb("qd", 2 * H * P).rearrange("p (c h i) -> p c h i", c=2, h=H)
        pool_w = sb("pool_w", PG * P).rearrange("p (g e) -> p g e", g=PG)
        w_router = sb("w_router", KD * NE).rearrange("p (k e) -> p k e", k=KD)
        b_router = sb("b_router", NE)
        p_rows = sb("p_rows", PG * P)
        small = sb("small", 128)
        hs_T = sb("hs_T", 8 * NS).rearrange("p (m b) -> p m b", m=8)
        stats = small[:, 0:24].rearrange("p (h s) -> p h s", h=H)
        moments = small[:, 24:32].rearrange("p (h s) -> p h s", h=H)
        spread = small[:, 32:36]
        sumsq, rms, rstd = small[:, 40:43], small[:, 44:47], small[:, 48:51]
        top = small[:, 56:80].rearrange("p (t j) -> p t j", t=3)
        neg_top = small[:, 80:83]
        gate_sum, gate_rec = small[:, 84:87], small[:, 88:91]
        most = small[0:1, 92:93]
        beyond = small[0:1, 96:104]
        pairs_f = small[0:1, 104:105]
        top_i = sb("top_i", 24, U32).rearrange("p (t j) -> p t j", t=3)
        top_f = sb("top_f", 24).rearrange("p (t j) -> p t j", t=3)
        pairs_i = sb("pairs_i", 4, I32)
        route = p_ext_all[:, 3 * TOPK * NE:3 * TOPK * NE + 5 * 3 * NE].rearrange("p (a t e) -> p a t e", a=5, t=3)
        logits, expd, chosen, gates, place = (route[:, a] for a in range(5))

        xe = vk[:, 0:KD * P].rearrange("p (k c) -> p k c", k=KD)
        out_T = vk[:, KD * P:2 * KD * P].rearrange("p (k j c) -> p k j c", k=KD, j=2)
        out_pair = vk[:, 2 * KD * P:3 * KD * P]
        hg, hu, hs = (rs[:, i * KD * CAP:(i + 1) * KD * CAP].rearrange("p (m c) -> p m c", m=KD) for i in range(3))
        act = rs[:, 3 * KD * CAP:4 * KD * CAP].rearrange("p (m c) -> p m c", m=KD)
        one_hot = sc[:, 0:3 * P].rearrange("p (t j c) -> p t j c", t=3, j=2)
        gated = sc[:, 3 * P:6 * P].rearrange("p (t j c) -> p t j c", t=3, j=2)
        g_T = pooled[:, 0]
        match = p_ext_all[:, 0:3 * TOPK * NE].rearrange("p (a e) -> p a e", e=NE)
        w_final = qk[:, 0:D]
        squares = qk[:, D:2 * D]
        z_sq = rs[:, 0:D]

        psum = ctx.enter_context(nc.psum_tensor("psum", [P, 8, 512], F32))

        def banks(a, n=1):
            return psum[:, a:a + n].rearrange("p b c -> p (b c)")

        consts_in, x_in, rows_in, hist_in, misc_in, final_in = (
            sem(n) for n in ("consts_in", "x_in", "rows_in", "hist_in", "misc_in", "final_in"))
        wmix_in = [sem(f"wmix_in{s}") for s in range(MIX_SLOTS)]
        state_in = [sem(f"state_in{s}") for s in range(4)]
        state_out = [sem(f"state_out{s}") for s in range(4)]
        expert_in = [sem(f"expert_in{s}") for s in range(RING)]
        stored, y_out = sem("stored"), sem("y_out")
        cleared, x_scaled, sq_done, rms_done, rstd_done = (
            sem(n) for n in ("cleared", "x_scaled", "sq_done", "rms_done", "rstd_done"))
        params_turned, params_ready, x_turned, u_ready = (
            sem(n) for n in ("params_turned", "params_ready", "x_turned", "u_ready"))
        tile_done, act_took, dve_took = sem("tile_done"), sem("act_took"), sem("dve_took")
        aux_done, aux_took, roped = sem("aux_done"), sem("aux_took"), sem("roped")
        pooled_ready, k_only_ready, state_decayed, state_ready = (
            sem(n) for n in ("pooled_ready", "k_only_ready", "state_decayed", "state_ready"))
        outer_read, o_s_ready, ret_out = sem("outer_read"), sem("o_s_ready"), sem("ret_out")
        spread_ready, spread_rooted = sem("spread_ready"), sem("spread_rooted")
        zeroed = sem("zeroed")
        mix_turned, h_ready, xn_ready, xn_turned, xn_T_ready = (
            sem(n) for n in ("mix_turned", "h_ready", "xn_ready", "xn_turned", "xn_T_ready"))
        logits_done, neg_ready, exp_ready, chosen_ready, placed, pairs_ready, place_ready = (
            sem(n) for n in ("logits_done", "neg_ready", "exp_ready", "chosen_ready", "placed", "pairs_ready",
                             "place_ready"))
        dve_step, act_step, pool_step = sem("dve_step"), sem("act_step"), sem("pool_step")
        dve_loop = sem("dve_loop")
        slot_used, one_hot_ready, gated_ready, gathered, xe_dve, xe_act = (
            sem(n) for n in ("slot_used", "one_hot_ready", "gated_ready", "gathered", "xe_dve", "xe_act"))
        hidden_done, hidden_took, gate_clipped, sigmoid_ready, act_ready = (
            sem(n) for n in ("hidden_done", "hidden_took", "gate_clipped", "sigmoid_ready", "act_ready"))
        down_done, out_T_ready, out_turned, out_dve, out_act = (
            sem(n) for n in ("down_done", "out_T_ready", "out_turned", "out_dve", "out_act"))
        gates_turned, g_T_ready, scattered, y_added = (
            sem(n) for n in ("gates_turned", "g_T_ready", "scattered", "y_added"))
        y_turned, y_summed, y_sq, y_rms, y_rstd, y_ready = (
            sem(n) for n in ("y_turned", "y_summed", "y_sq", "y_rms", "y_rstd", "y_ready"))

        class Steps:

            def __init__(self, eng, s):
                self.eng, self.s, self.n, self.base = eng, s, 0, 0

            def __call__(self, ins):
                self.n += 1
                ins.then_inc(self.s, 1)
                return ins

            def wait(self):
                self.eng.wait_ge(self.s, self.n + self.base)

        def wait_taken(eng, n):
            if n < T_YB:
                eng.wait_ge(act_took, n + 1)
            elif n < T_OUT:
                eng.wait_ge(dve_took, n - T_YB + 1)
            else:
                eng.wait_ge(act_took, T_YB + n - T_OUT + 1)

        TILES = ((0, P), (P, P), (2 * P, NS))

        gu_w = ins["w_gate_up"].rearrange("l e (k p) f -> (l e) p k f", p=P)
        dn_w = ins["w_down"].rearrange("l e (k p) f -> (l e) p k f", p=P)

        def expert_chunk(sp, e, s):
            if s < 8:
                src = gu_w[bass.ds(e, 1), :, s, :].rearrange("a p f -> p (a f)")
                sp.dma_start(slot(s), src).then_inc(expert_in[s], 16)
            else:
                src = dn_w[bass.ds(e, 1), :, 2 * (s - 8):2 * (s - 8) + 2, :].rearrange("a p k f -> p (a k) f")
                sp.dma_start(slot(s).rearrange("p (k f) -> p k f", k=2), src).then_inc(expert_in[s], 16)

        block = ctx.enter_context(nc.Block())

        @block.sync
        def _(sp):
            w_in = ins["w_in"].rearrange("l (k p) n -> p (l k) n", p=P)
            w_pb = ins["w_pool_branch"].rearrange("l (k p) n -> p (l k) n", p=P)
            w_ret = ins["w_ret_branch"].rearrange("l (k p) n -> p (l k) n", p=P)
            w_out = ins["w_out"].rearrange("l (k p) n -> p (l k) n", p=P)

            sp.dma_start(tok[:, 0:2, :], x_prompt[0].rearrange("(t p) d -> p t d", p=P)).then_inc(x_in, 16)
            sp.wait_ge(cleared, 1)
            sp.dma_start(tok[0:NS, 2, :], x_sample.rearrange("b s d -> (b s) d")).then_inc(x_in, 16)
            sp.dma_start(tok[32:32 + NM, 2, :], meta).then_inc(x_in, 16)

            def mix_chunk(i):
                kind, c = CHUNKS[i]
                s = i % MIX_SLOTS
                if i >= MIX_SLOTS:
                    sp.wait_ge(tile_done, last_tile(i - MIX_SLOTS) + 1)
                dst = slot(8 + s)
                if kind == "in":
                    cols = PROJ[c] * P
                    src = w_in[:, :, cols:cols + 2 * P]
                    dst = dst.rearrange("p (k n) -> p k n", k=KD)
                elif kind == "pb":
                    src = w_pb[:, :, c * 512:c * 512 + 512]
                    dst = dst.rearrange("p (k n) -> p k n", k=PG)
                else:
                    src = (w_ret if kind == "ret" else w_out)[:, :, c * 256:c * 256 + 256]
                    dst = dst.rearrange("p (k n) -> p k n", k=KD)
                sp.dma_start(dst, src).then_inc(wmix_in[s], 16)

            for i in range(MIX_SLOTS):
                mix_chunk(i)
            for s in range(4):
                expert_chunk(sp, 0, s)
            for i in range(MIX_SLOTS, C_PB):
                mix_chunk(i)
            sp.wait_ge(aux_took, AUX_AT[("o_turn",)] + 1)
            for s in range(4):
                sp.wait_ge(state_out[s], 32)
            for s in range(4, 8):
                expert_chunk(sp, 0, s)
            for i in range(C_PB, len(CHUNKS)):
                mix_chunk(i)
            for s in range(MIX_SLOTS):
                sp.wait_ge(tile_done, last_tile(len(CHUNKS) - MIX_SLOTS + s) + 1)
                expert_chunk(sp, 0, 8 + s)

            def expert(e, n):
                for s in range(RING):
                    sp.wait_ge(slot_used, (n - 1) * RING + s + 1)
                    expert_chunk(sp, e, s)

            with sp.Fori(1, NE) as e:
                expert(e, e)
            sp.wait_ge(pairs_ready, 1)
            pairs = sp.value_load(pairs_i[0:1, 0:1], min_val=NPAIR, max_val=NPAIR * NPASS)
            with sp.Fori(1, NPASS) as r:
                with sp.If(pairs > r * NPAIR):
                    with sp.Fori(0, NE) as e:
                        expert(e, r * NE + e)

            for t, (c0, n) in enumerate(TILES):
                sp.wait_ge(y_ready, t + 1)
                dst = y_sample.rearrange("b s d -> (b s) d") if t == 2 else y_prompt[0, c0:c0 + n, :]
                sp.dma_start(dst, tok[0:n, t, :]).then_inc(y_out, 16)
            sp.wait_ge(y_out, 16 * 3)
            sp.wait_ge(stored, 16 * 3)
            sp.wait_ge(ret_out, 16)
            for s in range(4):
                sp.wait_ge(state_out[s], 32)

        @block.gpsimd
        def _(pool):
            step = Steps(pool, pool_step)
            nc.gpsimd.memset(tok[0:64, 2, :], 0.0).then_inc(cleared, 1)
            nc.gpsimd.dma_start(consts[:, :], ins["consts"]).then_inc(consts_in, 16)
            for o, name, n in ((0, "norm_mix", 8), (8, "ret_gn", 8), (16, "pool_scale", 4), (20, "norm_ffn", 8)):
                pool.dma_start(rows[o:o + n, 0:P], ins[name].rearrange("l (a p) -> (l a) p", p=P)).then_inc(rows_in, 16)
            bg = ins["b_gate_up"].rearrange("l e (m p) -> (l e m) p", p=P)
            bd = ins["b_down"].rearrange("l e (m p) -> (l e m) p", p=P)
            pool.dma_start(rows[:, P:5 * P].rearrange("r (c p) -> r c p", c=4),
                           bg.rearrange("(c r) p -> r c p", r=P)).then_inc(rows_in, 16)
            pool.dma_start(rows[:, 5 * P:7 * P].rearrange("r (c p) -> r c p", c=2),
                           bd.rearrange("(c r) p -> r c p", r=P)).then_inc(rows_in, 16)
            pool.dma_start(hist[0:NS * PBUF, :], state_pool.rearrange("l b t c -> (l b t) c")).then_inc(hist_in, 16)
            for b in range(4):
                pool.dma_start(state_s[:, b], state_ret[0, b].rearrange("h d v -> d h v")).then_inc(state_in[b], 16)
            pool.dma_start(pool_w, ins["pool_w"].rearrange("l g c e -> c (l g) e")).then_inc(misc_in, 16)
            pool.dma_start(w_router, ins["w_router"].rearrange("l (k p) e -> p (l k) e", p=P)).then_inc(misc_in, 16)
            pool.dma_start(b_router[:, :], ins["b_router"].broadcast_to([P, NE])).then_inc(misc_in, 16)
            pool.dma_start(pool_sample[0, :, 0:PBUF - 1, :], state_pool[0, :, 1:PBUF, :]).then_inc(stored, 16)

            def only_k(b):
                if b >= 2:
                    pool.wait_ge(aux_done, AUX_AT[("outer", b - 2)] + 1)
                nc.gpsimd.tensor_scalar(k_only[0:NS, b % 2].rearrange("p h d -> p (h d)"), k_sm[0:NS, :],
                                        ident[0:NS, b:b + 1], None, ALU.mult).then_inc(k_only_ready, 1)

            def decay_state(b):
                pool.wait_ge(state_in[b % 4], 16 * (b // 4 + 1))
                for h in range(H):
                    last = nc.gpsimd.tensor_scalar(state_s[:, b % 4, h], state_s[:, b % 4, h], STEP_DEC[h], None,
                                                   ALU.mult)
                last.then_inc(state_decayed, 1)

            for b in range(4):
                decay_state(b)

            n = NM + NPR
            for g, w in enumerate(WINDOWS):
                pool.wait_ge(act_took, P0 + g + 1)
                src, lag = p_ext[:, g], 1
                for i in range(g + 1):
                    dst = win[:, i % 2]
                    step(nc.gpsimd.tensor_tensor(dst[:, 2 * lag - 1:n], src[:, 2 * lag - 1:n],
                                                 src[:, lag - 1:n - lag], ALU.add))
                    step.wait()
                    src, lag = dst, 2 * lag
                step(nc.gpsimd.tensor_scalar(src[:, NM:n], src[:, NM:n], 1.0 / w, None, ALU.mult))
                pool.wait_ge(aux_took, AUX_AT[("hist",)] + 1)
                step(nc.gpsimd.tensor_tensor(hist_sum[:, g], hist_sum[:, g], p_s[:, g], ALU.add))
                step.wait()
                step(nc.gpsimd.tensor_scalar(hist_sum[:, g], hist_sum[:, g], 1.0 / w, None, ALU.mult))
                step(nc.gpsimd.tensor_tensor(pooled[:, g, 0:NPR], src[:, NM:n], p_ext[:, g, NM:n], ALU.subtract))
                step.wait()
                nc.gpsimd.tensor_tensor(pooled[:, g, NPR:NT], hist_sum[:, g], p_s[:, g],
                                        ALU.subtract).then_inc(pooled_ready, 1)

            pool.wait_ge(aux_took, AUX_AT[("k", 3)] + 1)
            only_k(0)
            only_k(1)
            for b in range(NS):
                pool.wait_ge(aux_took, AUX_AT[("outer", b)] + 1)
                pool.dma_start(ret_sample[0, b].rearrange("h d v -> d h v"), state_s[:, b % 4]).then_inc(
                    state_out[b % 4], 16)
                if b + 2 < NS:
                    only_k(b + 2)
                if 1 <= b <= 4:
                    s = b - 1
                    pool.wait_ge(state_out[s], 16)
                    pool.wait_ge(outer_read, s + 1)
                    pool.dma_start(state_s[:, s], state_ret[0, s + 4].rearrange("h d v -> d h v")).then_inc(
                        state_in[s], 16)
                if 2 <= b <= 5:
                    decay_state(b + 2)
            pool.dma_start(ret_prompt[0, 0].rearrange("h d v -> d h v"), ret_s[:, 0]).then_inc(ret_out, 16)
            pool.dma_start(pool_prompt[0, 0], p_rows[0:PBUF, :]).then_inc(stored, 16)
            pool.dma_start(pool_sample[0, :, PBUF - 1, :], p_rows[32:32 + NS, :]).then_inc(stored, 16)
            pool.wait_ge(dve_took, T_OUT - T_YB)
            nc.gpsimd.memset(y_T[:, :, :], 0.0).then_inc(y_added, KD)
            nc.gpsimd.memset(g_T, 0.0).then_inc(g_T_ready, 1)
            nc.gpsimd.memset(out_T[:, :, :, :], 0.0).then_inc(out_T_ready, 2)
            nc.gpsimd.memset(route[:, :, :, :], 0.0).then_inc(zeroed, 1)
            nc.gpsimd.memset(top_f[:, :, :], float(NE)).then_inc(zeroed, 1)
            pool.wait_ge(logits_done, 1)
            pool.dma_start(w_final, ins["norm_final"].rearrange("(a d) -> a d", a=1).broadcast_to([P, D])).then_inc(
                final_in, 16)

        @block.tensor
        def _(pe):
            mm = pe.matmul

            def aux(a):
                i = AUX_AT[a]
                if bank_owner(i):
                    pe.wait_ge(aux_took, bank_owner(i))
                kind, bank = a[0], AUX_BANKS[a][0]
                if kind == "v":
                    j = a[1]
                    pe.wait_ge(act_took, V0 + j + 1)
                    src = v_T[:, j % 2]
                    pe.transpose(banks(bank)[:, 0:P], src[:, 0:P], ident)
                    pe.transpose(banks(bank)[:, P:2 * P], src[:, P:2 * P], ident)
                    pe.transpose(banks(bank)[0:NS, 2 * P:3 * P], src[:, NPR:NT], ident)
                    last = pe.transpose(banks(bank)[0:NM, 3 * P:4 * P], src[:, NT:NA], ident)
                elif kind == "k":
                    j = a[1]
                    pe.wait_ge(roped, j + 1)
                    src = k_T[:, j]
                    pe.transpose(banks(bank)[:, 0:P], src[:, 0:P], ident)
                    pe.transpose(banks(bank)[:, P:2 * P], src[:, P:2 * P], ident)
                    pe.transpose(banks(bank)[0:NS, 2 * P:3 * P], src[:, NPR:NT], ident)
                    last = pe.transpose(banks(bank)[0:NM, 3 * P:4 * P], src[:, NT:NA], ident)
                elif kind == "hist":
                    pe.wait_ge(hist_in, 16)
                    n = NS * PBUF
                    for g in range(PG):
                        last = pe.transpose(banks(bank)[:, g * P:g * P + n], hist[0:n, g * P:(g + 1) * P],
                                            ident[0:n, 0:n])
                elif kind == "s_meta":
                    pe.wait_ge(aux_took, AUX_AT[("k", 3)] + 1)
                    for h in range(H):
                        last = mm(banks(bank, 2)[:, h * DV:(h + 1) * DV], k_sm[32:32 + NM, h * DK:(h + 1) * DK],
                                  v_sm[32:32 + NM, h * DV:(h + 1) * DV], start=True, stop=True)
                elif kind == "score":
                    c = a[1]
                    pe.wait_ge(roped, 8)
                    for h in range(H):
                        last = mm(banks(bank)[:, h * P:(h + 1) * P], k_T[:, h, c * P:(c + 1) * P],
                                  q_T[:, h, c * P:(c + 1) * P], start=True, stop=True)
                elif kind == "s_next":
                    c = a[1]
                    for h in range(H):
                        last = mm(banks(bank, 2)[:, h * DV:(h + 1) * DV], k_tok[:, c, h * DK:(h + 1) * DK],
                                  v_tok[:, c, h * DV:(h + 1) * DV], start=True, stop=True)
                elif kind == "o":
                    c = a[1]
                    before = ("s_meta",) if c == 0 else ("s_next", 0)
                    pe.wait_ge(aux_took, max(AUX_AT[("score", c)], AUX_AT[before]) + 1)
                    for h in range(H):
                        o = banks(bank, 2)[:, h * DV:(h + 1) * DV]
                        mm(o, scores[:, c, h], v_tok[:, c, h * DV:(h + 1) * DV], start=True, stop=False)
                        last = mm(o, qd[:, c, h], ret_s[:, c, h], start=False, stop=True)
                elif kind == "ptok":
                    pe.wait_ge(act_took, P0 + PG)
                    for g in range(PG):
                        pe.transpose(banks(bank)[0:PBUF, g * P:(g + 1) * P], p_ext[:, g, NM + NPR - PBUF:], ident)
                    for g in range(PG):
                        last = pe.transpose(banks(bank + 1)[0:NS, g * P:(g + 1) * P], p_s[:, g], ident)
                elif kind == "outer":
                    b = a[1]
                    pe.wait_ge(k_only_ready, b + 1)
                    for h in range(H):
                        last = mm(banks(bank, 2)[:, h * DV:(h + 1) * DV], k_only[0:NS, b % 2, h],
                                  v_sm[0:NS, h * DV:(h + 1) * DV], start=True, stop=True)
                elif kind == "o_turn":
                    pe.wait_ge(o_s_ready, 1)
                    for m in range(8):
                        last = pe.transpose(banks(bank, 2)[0:NS, m * P:(m + 1) * P], hs_T[:, m], ident)
                elif kind == "z":
                    j = a[1]
                    pe.wait_ge(aux_took, AUX_AT[("o_turn",)] + 1)
                    for t, (c0, n) in enumerate(TILES):
                        last = pe.transpose(banks(bank)[:, c0:c0 + n], normed[0:n, t, j * P:(j + 1) * P],
                                            ident[0:n, 0:n])
                last.then_inc(aux_done, 1)

            def read_state(b):
                pe.wait_ge(aux_took, AUX_AT[("outer", b)] + 1)
                for h in range(H):
                    for v in range(2):
                        m = 2 * h + v
                        last = mm(psum[:, 3, m * NS + b:m * NS + b + 1], state_s[:, b % 4, h, v * P:(v + 1) * P],
                                  q_s[:, h, b:b + 1], start=True, stop=True)
                last.then_inc(outer_read, 1)

            pe.wait_ge(consts_in, 16)
            pe.wait_ge(rows_in, 6 * 16)
            pe.transpose(psum[:, 0, 0:28], rows[0:28, 0:P], ident[0:28, 0:28])
            for c in range(4):
                pe.transpose(psum[:, 1, c * P:(c + 1) * P], rows[:, (1 + c) * P:(2 + c) * P], ident)
            for c in range(2):
                last = pe.transpose(psum[:, 2, c * P:(c + 1) * P], rows[:, (5 + c) * P:(6 + c) * P], ident)
            last.then_inc(params_turned, 1)
            for k in range(KD):
                if k == 0:
                    pe.wait_ge(x_scaled, 3)
                if k >= 4:
                    pe.wait_ge(u_ready, 2 * (k - 3))
                for t, n in enumerate((P, P, 48)):
                    last = pe.transpose(psum[:, 4 + k % 4, t * P:t * P + n], normed[0:n, t, k * P:(k + 1) * P],
                                        ident[0:n, 0:n])
                last.then_inc(x_turned, 1)
            pe.wait_ge(u_ready, 2 * KD)
            pe.wait_ge(params_ready, 3)

            for n in range(T_END):
                if n >= 3:
                    wait_taken(pe, n - 3)
                o = psum[:, n % 3]
                if n < N_IN:
                    i, width = n // 2, (NA if n < G0 else NT)
                    w = slot(8 + i % MIX_SLOTS).rearrange("p (k n) -> p k n", k=KD)
                    cols = (n % 2) * P
                    x, nk = u_T, KD
                elif n < T_YB:
                    width, nk = NT, 1
                    if n == T_POOL:
                        pe.wait_ge(misc_in, 3 * 16)
                    g = n - T_POOL
                    pe.wait_ge(pooled_ready, g + 1)
                    mm(o[:, 0:NT], pool_w[:, g], pooled[:, g], start=True, stop=True).then_inc(tile_done, 1)
                    continue
                elif n < T_YA:
                    d = n - T_YB
                    i, cols, x, width, nk = C_PB + d // 4, (d % 4) * P, pooled, NT, PG
                    w = slot(8 + i % MIX_SLOTS).rearrange("p (k n) -> p k n", k=PG)
                    if d == 0:
                        pe.wait_ge(act_took, T_YB)
                else:
                    d = n - (T_YA if n < T_OUT else T_OUT)
                    i = (C_RET if n < T_OUT else C_OUT) + d // 2
                    cols, width, nk = (d % 2) * P, NT, KD
                    x = z_T if n < T_OUT else gate_a
                    w = slot(8 + i % MIX_SLOTS).rearrange("p (k n) -> p k n", k=KD)
                    if n == T_YA:
                        pe.wait_ge(aux_took, AUX_AT[("z", 7)] + 1)
                    if n == T_OUT:
                        pe.wait_ge(dve_took, T_OUT - T_YB)
                pe.wait_ge(wmix_in[i % MIX_SLOTS], 16 * (i // MIX_SLOTS + 1))
                for k in range(nk):
                    last = mm(o[:, 0:width], w[:, k, cols:cols + P], x[:, k, 0:width], start=k == 0, stop=k == nk - 1)
                last.then_inc(tile_done, 1)
                for a in AUX_AFTER[n]:
                    aux(a)
                if 25 <= n < 25 + NS:
                    read_state(n - 25)

            for t, (c0, n) in enumerate(TILES):
                bank = (4, 6, 3)[t]
                if t == 0:
                    wait_taken(pe, T_END - 1)
                for d in range(KD):
                    o = banks(bank, 2)[0:n, d * P:(d + 1) * P] if t < 2 else psum[0:n, 3 if d < 4 else 0,
                                                                                 (d % 4) * P:(d % 4 + 1) * P]
                    last = pe.transpose(o, u_T[:, d, c0:c0 + n], ident)
                last.then_inc(mix_turned, 1)
            for k in range(KD):
                if k == 0:
                    pe.wait_ge(xn_ready, 3)
                if k >= 2:
                    pe.wait_ge(xn_T_ready, k - 1)
                for t, (c0, n) in enumerate(TILES):
                    last = pe.transpose(psum[:, 1 + k % 2, c0:c0 + n], normed[0:n, t, k * P:(k + 1) * P],
                                        ident[0:n, 0:n])
                last.then_inc(xn_turned, 1)
            pe.wait_ge(xn_T_ready, KD)
            for t, (c0, n) in enumerate(TILES):
                for k in range(KD):
                    last = mm(psum[0:n, 4, t * NE:(t + 1) * NE], xn_T[:, k, c0:c0 + n], w_router[:, k],
                              start=k == 0, stop=k == KD - 1)
            last.then_inc(logits_done, 1)
            pe.wait_ge(chosen_ready, 1)
            before = const("before")
            for t, (_, n) in enumerate(TILES):
                for s in range(t):
                    mm(psum[0:n, 5, t * NE:(t + 1) * NE], ones[:, 0:n], chosen[:, s], start=s == 0, stop=False)
                mm(psum[0:n, 5, t * NE:(t + 1) * NE], before[0:n, 0:n], chosen[0:n, t], start=t == 0, stop=True)
            for t, (_, n) in enumerate(TILES):
                last = mm(psum[:, 5, 3 * NE:4 * NE], ones[0:n, :], chosen[0:n, t], start=t == 0, stop=t == 2)
            last.then_inc(placed, 1)

            def turn_out(it):
                pe.wait_ge(out_T_ready, 2 * it + 2)
                pe.wait_ge(y_added, KD * it + KD)
                for d in range(KD):
                    last = pe.transpose(banks(5, 2)[:, d * P:(d + 1) * P],
                                        out_T[:, d].rearrange("p j c -> p (j c)"), ident)
                last.then_inc(out_turned, 1)

            def scatter(it, tiles):
                for d in tiles:
                    if d == 0:
                        pe.wait_ge(out_act, it + 1)
                        pe.wait_ge(out_dve, it + 1)
                        pe.wait_ge(g_T_ready, it + 1)
                    if d >= 3:
                        pe.wait_ge(y_added, KD * (it + 1) + d - 2)
                    mm(psum[:, 5 + d % 3, 0:NT], out_pair[:, d * P:(d + 1) * P], g_T, start=True,
                       stop=True).then_inc(scattered, 1)

            def gate_up(it, j):
                pe.wait_ge(hidden_took, 2 * (2 * it + j + 1))
                for k in range(KD):
                    pe.wait_ge(expert_in[k], 16 * (2 * it + j + 1))
                    if j == 0 and k == 0:
                        pe.wait_ge(xe_dve, it + 1)
                    if j == 0 and k == 4:
                        pe.wait_ge(xe_act, it + 1)
                    w = slot(k)
                    for m in range(16):
                        last = mm(psum[:, m // 8, (m % 8) * CAP:(m % 8 + 1) * CAP], w[:, m * P:(m + 1) * P],
                                  xe[:, k, j * CAP:(j + 1) * CAP], start=k == 0 and m % 8 == 0, stop=k == KD - 1,
                                  skip_group_check=True)
                    last.then_inc(slot_used, 1)

            def down(it, j):
                pe.wait_ge(act_ready, 2 * it + j + 1)
                if j == 0:
                    pe.wait_ge(g_T_ready, it + 1)
                pe.wait_ge(out_T_ready, 2 * it + j + 2)
                if j == 1:
                    pe.wait_ge(g_T_ready, it + 2)
                for f in range(KD):
                    s = 8 + f // 2
                    if f % 2 == 0:
                        pe.wait_ge(expert_in[s], 16 * (2 * it + j + 1))
                    w = slot(s)[:, (f % 2) * D:(f % 2 + 1) * D]
                    for d in range(KD):
                        last = mm(psum[:, 2, d * CAP:(d + 1) * CAP], w[:, d * P:(d + 1) * P], act[:, f],
                                  start=f == 0 and d == 0, stop=f == KD - 1, skip_group_check=True)
                    if f % 2:
                        last.then_inc(slot_used, 1)

            def pair(it):
                pe.wait_ge(one_hot_ready, it + 1)
                for k in range(KD):
                    for t, (_, n) in enumerate(TILES):
                        last = mm(psum[:, 3 + k // 4, (k % 4) * P:(k % 4 + 1) * P], normed[0:n, t, k * P:(k + 1) * P],
                                  one_hot[0:n, t].rearrange("p j c -> p (j c)"), start=t == 0, stop=t == 2)
                last.then_inc(gathered, 1)
                turn_out(it)
                gate_up(it, 0)
                scatter(it, (0, 1, 2))
                down(it, 0)
                scatter(it, (3, 4, 5))
                gate_up(it, 1)
                scatter(it, (6, 7))
                pe.wait_ge(gated_ready, it + 1)
                pe.wait_ge(out_T_ready, 2 * it + 3)
                for t, (c0, n) in enumerate(TILES):
                    last = pe.transpose(psum[:, 2, c0:c0 + n], gated[0:n, t].rearrange("p j c -> p (j c)"),
                                        ident[0:n, 0:n])
                last.then_inc(gates_turned, 1)
                down(it, 1)

            pe.wait_ge(pairs_ready, 1)
            pe.wait_ge(zeroed, 2)
            pairs = pe.value_load(pairs_i[0:1, 0:1], min_val=NPAIR, max_val=NPAIR * NPASS)
            with pe.Fori(0, NPASS) as r:
                with pe.If(pairs > r * NPAIR):
                    with pe.Fori(0, NPAIR) as p:
                        pair(r * NPAIR + p)
            turn_out(pairs)
            scatter(pairs, range(KD))

            pe.wait_ge(y_added, KD * pairs + 2 * KD)
            for t, (c0, n) in enumerate(TILES):
                for d in range(KD):
                    last = pe.transpose(banks(2 * t, 2)[0:n, d * P:(d + 1) * P], y_T[:, d, c0:c0 + n], ident)
                last.then_inc(y_turned, 1)

        @block.scalar
        def _(act_e):
            step = Steps(act_e, act_step)
            A = nc.scalar.activation
            act_e.wait_ge(x_in, 48)
            act_e.wait_ge(consts_in, 16)
            for t, n in enumerate((P, P, 48)):
                step(A(squares[0:n], tok[0:n, t], ACT.Square, accum_out=sumsq[0:n, t:t + 1]))
                step.wait()
            for t, n in enumerate((P, P, 48)):
                A(rms[0:n, t:t + 1], sumsq[0:n, t:t + 1], ACT.Sqrt, bias=const("eps")[0:n], scale=1.0 / D).then_inc(
                    rms_done, 1)
            act_e.wait_ge(params_ready, 3)
            for k in range(KD):
                act_e.wait_ge(x_turned, k + 1)
                A(u_T[:, k, 0:NT], psum[:, 4 + k % 4, 0:NT], ACT.Copy, scale=norm_mix[:, k:k + 1]).then_inc(u_ready, 1)
                A(u_T[:, k, NT:NA], psum[:, 4 + k % 4, 288:304], ACT.Copy, scale=norm_mix[:, k:k + 1]).then_inc(
                    u_ready, 1)
            for n in range(T_YB):
                act_e.wait_ge(tile_done, n + 1)
                ps = psum[:, n % 3]
                if n < K0:
                    if n >= 2:
                        act_e.wait_ge(aux_done, AUX_AT[("v", n - 2)] + 1)
                    last = nc.scalar.copy(v_T[:, n % 2], ps[:, 0:NA])
                elif n < P0:
                    j = n - K0
                    if j >= 2:
                        act_e.wait_ge(roped, j - 1)
                    nc.scalar.copy(rope_y[0:64, j % 2], ps[64:128, 0:NA])
                    nc.scalar.copy(rope_y[64:128, j % 2], ps[0:64, 0:NA])
                    last = nc.scalar.copy(rope_x[:, j % 2], ps[:, 0:NA])
                elif n < G0:
                    g = n - P0
                    nc.scalar.copy(p_ext[:, g, 0:NM], ps[:, NT:NA])
                    nc.scalar.copy(p_s[:, g], ps[:, NPR:NT])
                    last = nc.scalar.copy(p_ext[:, g, NM:], ps[:, 0:NPR])
                elif n < GA0:
                    last = A(z_T[:, n - G0], ps[:, 0:NT], ACT.Silu)
                elif n < GB0:
                    if n == GA0:
                        act_e.wait_ge(aux_took, AUX_AT[("o", 1)] + 1)
                    last = A(gate_a[:, n - GA0], ps[:, 0:NT], ACT.Sigmoid)
                elif n < N_IN:
                    if n == GB0:
                        act_e.wait_ge(aux_done, AUX_AT[("outer", NS - 1)] + 1)
                    last = A(gate_b[:, n - GB0], ps[:, 0:NT], ACT.Sigmoid)
                else:
                    g = n - T_POOL
                    last = A(pooled[:, g], ps[:, 0:NT], ACT.Copy, scale=pool_scale[:, g:g + 1])
                last.then_inc(act_took, 1)
                if n in ROOT_AFTER:
                    i = ROOT_AFTER[n]
                    rows_n = NS if i == 2 else P
                    act_e.wait_ge(spread_ready, i + 1)
                    A(spread[0:rows_n], moments[0:rows_n, :, 1], ACT.Sqrt, bias=const("eps")[0:rows_n]).then_inc(
                        spread_rooted, 1)
            for n in range(T_OUT, T_END):
                act_e.wait_ge(tile_done, n + 1)
                nc.scalar.copy(u_T[:, n - T_OUT, 0:NT], psum[:, n % 3, 0:NT]).then_inc(act_took, 1)
            act_e.wait_ge(ret_out, 16)
            for t, (_, n) in enumerate(TILES):
                act_e.wait_ge(h_ready, t + 1)
                A(z_sq[0:n], tok[0:n, t], ACT.Square, accum_out=sumsq[0:n, t:t + 1]).then_inc(sq_done, 1)
                act_e.wait_ge(sq_done, t + 1)
            for t, (_, n) in enumerate(TILES):
                A(rms[0:n, t:t + 1], sumsq[0:n, t:t + 1], ACT.Sqrt, bias=const("eps")[0:n], scale=1.0 / D).then_inc(
                    rms_done, 1)
            for k in range(KD):
                act_e.wait_ge(xn_turned, k + 1)
                A(xn_T[:, k], psum[:, 1 + k % 2, 0:NT], ACT.Copy, scale=norm_ffn[:, k:k + 1]).then_inc(xn_T_ready, 1)
            act_e.wait_ge(neg_ready, 1)
            act_e.wait_ge(zeroed, 2)
            for t, (_, n) in enumerate(TILES):
                A(expd[0:n, t], logits[0:n, t], ACT.Exp, bias=neg_top[0:n, t:t + 1]).then_inc(exp_ready, 1)

            def pair(it):
                act_e.wait_ge(gathered, it + 1)
                for k in range(4, KD):
                    last = A(xe[:, k], psum[:, 4, (k - 4) * P:(k - 3) * P], ACT.Copy, scale=norm_ffn[:, k:k + 1])
                last.then_inc(xe_act, 1)
                take_turned(it)
                for j in range(2):
                    act_e.wait_ge(gate_clipped, 2 * it + j + 1)
                    A(hs[:, :, :], hg[:, :, :], ACT.Sigmoid, scale=ALPHA).then_inc(sigmoid_ready, 1)
                act_e.wait_ge(gates_turned, it + 1)
                nc.scalar.copy(g_T, psum[:, 2, 0:NT]).then_inc(g_T_ready, 1)

            def take_turned(it):
                act_e.wait_ge(out_turned, it + 1)
                nc.scalar.copy(out_pair[:, 0:512], psum[:, 5]).then_inc(out_act, 1)

            act_e.wait_ge(pairs_ready, 1)
            pairs = act_e.value_load(pairs_i[0:1, 0:1], min_val=NPAIR, max_val=NPAIR * NPASS)
            with act_e.Fori(0, NPASS) as r:
                with act_e.If(pairs > r * NPAIR):
                    with act_e.Fori(0, NPAIR) as p:
                        pair(r * NPAIR + p)
            take_turned(pairs)

            for t, (_, n) in enumerate(TILES):
                act_e.wait_ge(y_summed, t + 1)
                A(squares[0:n], tok[0:n, t], ACT.Square, accum_out=sumsq[0:n, t:t + 1]).then_inc(y_sq, 1)
                act_e.wait_ge(y_sq, t + 1)
            for t, (_, n) in enumerate(TILES):
                A(rms[0:n, t:t + 1], sumsq[0:n, t:t + 1], ACT.Sqrt, bias=const("eps")[0:n], scale=1.0 / D).then_inc(
                    y_rms, 1)

        @block.vector
        def _(dve):
            V = nc.vector
            step = Steps(dve, dve_step)

            def aux(a):
                i = AUX_AT[a]
                dve.wait_ge(aux_done, i + 1)
                kind, bank = a[0], AUX_BANKS[a][0]
                ps = banks(bank)
                if kind == "v":
                    c = slice(a[1] * P, (a[1] + 1) * P)
                    V.tensor_copy(v_tok[:, :, c], ps[:, 0:2 * P].rearrange("p (t c) -> p t c", t=2))
                    V.tensor_copy(v_sm[0:NS, c], ps[0:NS, 2 * P:3 * P])
                    last = V.tensor_copy(v_sm[32:32 + NM, c], ps[0:NM, 3 * P:4 * P])
                elif kind == "k":
                    j = a[1]
                    c = slice(j * P, (j + 1) * P)
                    V.tensor_scalar(k_tok[:, :, c], ps[:, 0:2 * P].rearrange("p (t c) -> p t c", t=2),
                                    const("k_dec")[:, j:j + 1], None, ALU.mult)
                    V.tensor_copy(k_sm[0:NS, c], ps[0:NS, 2 * P:3 * P])
                    step(V.tensor_copy(k_sm[32:32 + NM, c], ps[0:NM, 3 * P:4 * P]))
                    step.wait()
                    last = V.tensor_scalar(k_sm[32:32 + NM, c], k_sm[32:32 + NM, c],
                                           const("k_dec_meta")[32:32 + NM, j:j + 1], None, ALU.mult)
                elif kind == "hist":
                    for g, w in enumerate(WINDOWS):
                        rows_g = ps[:, g * P:g * P + NS * PBUF].rearrange("p (b t) -> p b t", b=NS)
                        last = V.tensor_reduce(hist_sum[:, g], rows_g[:, :, PBUF - w + 1:], AX.X, ALU.add)
                elif kind == "s_meta":
                    last = V.tensor_copy(ret_s[:, 0].rearrange("p h v -> p (h v)"), banks(bank, 2))
                elif kind == "score":
                    c = a[1]
                    V.tensor_tensor(qd[:, c], q_T[:, :, c * P:(c + 1) * P],
                                    const("q_dec").rearrange("p (h i) -> p h i", h=H), ALU.mult)
                    last = V.tensor_tensor(scores[:, c].rearrange("p h i -> p (h i)"), ps, const("mask"), ALU.mult)
                elif kind == "s_next":
                    c = a[1]
                    for h in range(H):
                        last = V.scalar_tensor_tensor(ret_s[:, 1 - c, h], ret_s[:, c, h], CHUNK_DEC[h],
                                                      banks(bank, 2)[:, h * DV:(h + 1) * DV], ALU.mult, ALU.add)
                elif kind == "o":
                    group_norm(a[1], P, banks(bank, 2))
                    last = None
                elif kind == "ptok":
                    V.tensor_copy(p_rows[0:PBUF, :], ps[0:PBUF])
                    last = V.tensor_copy(p_rows[32:32 + NS, :], banks(bank + 1)[0:NS])
                elif kind == "outer":
                    b = a[1]
                    dve.wait_ge(state_decayed, b + 1)
                    s = state_s[:, b % 4].rearrange("p h v -> p (h v)")
                    last = V.tensor_tensor(s, s, banks(bank, 2), ALU.add)
                elif kind == "o_turn":
                    group_norm(2, NS, banks(bank, 2))
                    last = None
                elif kind == "z":
                    j = a[1]
                    dve.wait_ge(act_took, GA0)
                    last = V.scalar_tensor_tensor(z_T[:, j], ps[:, 0:NT], gn_w[:, j:j + 1], z_T[:, j], ALU.mult,
                                                  ALU.mult)
                if last is not None:
                    last.then_inc(aux_took, 1)

            def group_norm(i, n, ps):
                for h in range(H):
                    step(V.bn_stats(stats[0:n, h], ps[0:n, h * DV:(h + 1) * DV]))
                step.wait()
                for h in range(H):
                    last = V.bn_aggr(moments[0:n, h], stats[0:n, h])
                last.then_inc(spread_ready, 1)
                dve.wait_ge(spread_rooted, i + 1)
                step(V.reciprocal(spread[0:n], spread[0:n]))
                step.wait()
                for h in range(H):
                    last = V.tensor_scalar(normed[0:n, i, h * DV:(h + 1) * DV], ps[0:n, h * DV:(h + 1) * DV],
                                           moments[0:n, h, 0:1], spread[0:n, h:h + 1], ALU.subtract, ALU.mult)
                last.then_inc(aux_took, 1)

            dve.wait_ge(rms_done, 3)
            dve.wait_ge(params_turned, 1)
            V.tensor_copy(params[:, 0:28], psum[:, 0, 0:28]).then_inc(params_ready, 1)
            V.tensor_copy(params[:, 28:28 + 512], psum[:, 1]).then_inc(params_ready, 1)
            V.tensor_copy(params[:, 28 + 512:], psum[:, 2, 0:256]).then_inc(params_ready, 1)
            for t, n in enumerate((P, P, 48)):
                step(V.reciprocal(rstd[0:n, t:t + 1], rms[0:n, t:t + 1]))
            step.wait()
            for t, n in enumerate((P, P, 48)):
                V.tensor_scalar(normed[0:n, t], tok[0:n, t], rstd[0:n, t:t + 1], None, ALU.mult).then_inc(x_scaled, 1)

            for n in range(T_OUT):
                if K0 <= n < P0:
                    j = n - K0
                    dve.wait_ge(act_took, n + 1)
                    s = DK ** -0.5 if j < H else 1.0
                    x, y = rope_x[:, j % 2], rope_y[:, j % 2]
                    step(V.scalar_tensor_tensor(x, x, s, const("cos"), ALU.mult, ALU.mult))
                    step(V.scalar_tensor_tensor(y, y, s, const("sin"), ALU.mult, ALU.mult))
                    step.wait()
                    if j < H:
                        V.tensor_tensor(k_T[:, j], x, y, ALU.add).then_inc(roped, 1)
                    else:
                        h = j - H
                        step(V.tensor_tensor(q_s[:, h], x[:, NPR:NT], y[:, NPR:NT], ALU.add))
                        V.tensor_tensor(q_T[:, h], x[:, 0:NT], y[:, 0:NT], ALU.add).then_inc(roped, 1)
                        if h == H - 1:
                            dve.wait_ge(roped, 8)
                elif T_YB <= n < T_YA:
                    d = n - T_YB
                    dve.wait_ge(tile_done, n + 1)
                    dve.wait_ge(act_took, N_IN)
                    V.tensor_tensor(gate_b[:, d], psum[:, n % 3, 0:NT], gate_b[:, d], ALU.mult).then_inc(dve_took, 1)
                elif T_YA <= n:
                    d = n - T_YA
                    dve.wait_ge(tile_done, n + 1)
                    if d == 0:
                        dve.wait_ge(dve_took, T_YA - T_YB)
                    step(V.tensor_tensor(gate_a[:, d], psum[:, n % 3, 0:NT], gate_a[:, d], ALU.mult))
                    step.wait()
                    V.tensor_tensor(gate_a[:, d], gate_a[:, d], gate_b[:, d], ALU.add).then_inc(dve_took, 1)
                for a in AUX_AFTER[n]:
                    aux(a)
                if n == 33:
                    dve.wait_ge(outer_read, NS)
                    V.tensor_copy(hs_T.rearrange("p m b -> p (m b)"), psum[:, 3, 0:8 * NS]).then_inc(o_s_ready, 1)

            for t, (_, n) in enumerate(TILES):
                dve.wait_ge(mix_turned, t + 1)
                if t < 2:
                    V.tensor_tensor(tok[0:n, t], banks((4, 6)[t], 2)[0:n], tok[0:n, t], ALU.add).then_inc(h_ready, 1)
                else:
                    step(V.tensor_tensor(tok[0:n, t, 0:512], psum[0:n, 3], tok[0:n, t, 0:512], ALU.add))
                    step.wait()
                    V.tensor_tensor(tok[0:n, t, 512:], psum[0:n, 0], tok[0:n, t, 512:], ALU.add).then_inc(h_ready, 1)
            dve.wait_ge(rms_done, 6)
            for t, (_, n) in enumerate(TILES):
                step(V.reciprocal(rstd[0:n, t:t + 1], rms[0:n, t:t + 1]))
            step.wait()
            for t, (_, n) in enumerate(TILES):
                V.tensor_scalar(normed[0:n, t], tok[0:n, t], rstd[0:n, t:t + 1], None, ALU.mult).then_inc(xn_ready, 1)

            dve.wait_ge(logits_done, 1)
            dve.wait_ge(zeroed, 2)
            for t, (_, n) in enumerate(TILES):
                step(V.tensor_tensor(logits[0:n, t], psum[0:n, 4, t * NE:(t + 1) * NE], b_router[0:n, :], ALU.add))
            step.wait()
            for t, (_, n) in enumerate(TILES):
                step(V.max(top[0:n, t], logits[0:n, t]))
            step.wait()
            for t, (_, n) in enumerate(TILES):
                last = V.tensor_scalar(neg_top[0:n, t:t + 1], top[0:n, t, 0:1], -1.0, None, ALU.mult)
            last.then_inc(neg_ready, 1)
            for t, (_, n) in enumerate(TILES):
                step(V.max_index(top_i[0:n, t], top[0:n, t], logits[0:n, t]))
            step.wait()
            for t, (_, n) in enumerate(TILES):
                step(V.tensor_copy(top_f[0:n, t], top_i[0:n, t]))
            step.wait()
            for t in range(3):
                step(V.tensor_tensor(match[:, 4 * t:4 * t + 4],
                                     const("experts").rearrange("p (a e) -> p a e", a=1).broadcast_to([P, TOPK, NE]),
                                     top_f[:, t, 0:TOPK].rearrange("p (j a) -> p j a", a=1).broadcast_to(
                                         [P, TOPK, NE]), ALU.is_equal))
            step.wait()
            for t in range(3):
                last = V.tensor_reduce(chosen[:, t], match[:, 4 * t:4 * t + 4].rearrange("p j e -> p e j"), AX.X,
                                       ALU.add)
                if t == 2:
                    last.then_inc(chosen_ready, 1)
            dve.wait_ge(exp_ready, 3)
            dve.wait_ge(chosen_ready, 1)
            step(V.tensor_tensor(gates[:, :, :], expd[:, :, :], chosen[:, :, :], ALU.mult))
            step.wait()
            step(V.tensor_reduce(gate_sum, gates[:, :, :], AX.X, ALU.add))
            step.wait()
            step(V.tensor_scalar(gate_sum, gate_sum, 1e-30, None, ALU.max))
            step.wait()
            step(V.reciprocal(gate_rec, gate_sum))
            step.wait()
            step(V.tensor_tensor(gates[:, :, :], gates[:, :, :],
                                 gate_rec.rearrange("p (t a) -> p t a", a=1).broadcast_to([P, 3, NE]), ALU.mult))
            step(V.tensor_scalar(place[:, :, :], chosen[:, :, :], -FAR, FAR, ALU.mult, ALU.add))
            step.wait()
            dve.wait_ge(placed, 1)
            step(V.tensor_tensor(place[:, 0:2], place[:, 0:2],
                                 psum[:, 5, 0:2 * NE].rearrange("p (t e) -> p t e", t=2), ALU.add))
            V.tensor_tensor(place[0:NS, 2], place[0:NS, 2], psum[0:NS, 5, 2 * NE:3 * NE], ALU.add).then_inc(
                place_ready, 1)
            step(V.tensor_reduce(most, psum[0:1, 5, 3 * NE:4 * NE], AX.X, ALU.max))
            step.wait()
            step(V.tensor_scalar(beyond, const("passes")[0:1], most, float(NPAIR), ALU.is_lt, ALU.mult))
            step.wait()
            V.tensor_reduce(pairs_f, beyond, AX.X, ALU.add).then_inc(hidden_took, 2)
            dve.wait_ge(hidden_took, 2)
            V.tensor_copy(pairs_i[0:1, 0:1], pairs_f).then_inc(pairs_ready, 1)

            loop = Steps(dve, dve_loop)
            iota = const("iota").rearrange("p (t j c) -> p t j c", t=1, j=1).broadcast_to([P, 3, 2, CAP])
            nf = norm_ffn[:, 0:4].rearrange("p (k c) -> p k c", c=1).broadcast_to([P, 4, P])

            def per_pair(table, p):
                return table[:, :, bass.ds(2 * p, 2)].rearrange("p t (j c) -> p t j c", c=1).broadcast_to(
                    [P, 3, 2, CAP])

            def bias(table, e, m0):
                return table[:, bass.ds(e, 1), m0:m0 + KD].rearrange("p a (m c) -> p (a m) c", c=1).broadcast_to(
                    [P, KD, CAP])

            def add_scattered(it, tiles):
                for d in tiles:
                    dve.wait_ge(scattered, KD * it + d + 1)
                    V.tensor_tensor(y_T[:, d], y_T[:, d], psum[:, 5 + d % 3, 0:NT], ALU.add).then_inc(y_added, 1)

            def take_turned(it):
                dve.wait_ge(out_turned, it + 1)
                V.tensor_copy(out_pair[:, 512:], psum[:, 6]).then_inc(out_dve, 1)

            def swiglu(it, j, e):
                dve.wait_ge(slot_used, (2 * it + j) * RING + KD)
                n = 2 * it + j
                V.tensor_tensor(hg, psum[:, 0].rearrange("p (m c) -> p m c", m=KD), bias(b_gu, e, 0),
                                ALU.add).then_inc(hidden_took, 1)
                dve.wait_ge(hidden_took, 2 * n + 3)
                V.tensor_scalar(hg, hg, LIMIT, None, ALU.min).then_inc(gate_clipped, 1)
                V.tensor_tensor(hu, psum[:, 1].rearrange("p (m c) -> p m c", m=KD), bias(b_gu, e, KD),
                                ALU.add).then_inc(hidden_took, 1)
                dve.wait_ge(hidden_took, 2 * n + 4)
                loop(V.tensor_scalar(hu, hu, LIMIT, -LIMIT, ALU.min, ALU.max))
                loop.wait()
                dve.wait_ge(gate_clipped, n + 1)
                loop(V.scalar_tensor_tensor(hu, hu, 1.0, hg, ALU.add, ALU.mult))
                loop.wait()
                dve.wait_ge(sigmoid_ready, 2 * it + j + 1)
                V.tensor_tensor(act, hu, hs, ALU.mult).then_inc(act_ready, 1)

            def take_down(it, j, e):
                dve.wait_ge(slot_used, (2 * it + j + 1) * RING)
                V.tensor_tensor(out_T[:, :, j], psum[:, 2].rearrange("p (m c) -> p m c", m=KD), bias(b_dn, e, 0),
                                ALU.add).then_inc(out_T_ready, 1)

            LOOP_STEPS = 4

            def pair(r, p):
                it = r * NPAIR + p
                loop.base, loop.n = it * LOOP_STEPS, 0
                dve.wait_ge(place_ready, r + 1)
                V.tensor_tensor(one_hot, iota, per_pair(place, p), ALU.is_equal).then_inc(one_hot_ready, 1)
                dve.wait_ge(one_hot_ready, it + 1)
                V.tensor_tensor(gated, one_hot, per_pair(gates, p), ALU.mult).then_inc(gated_ready, 1)
                dve.wait_ge(gathered, it + 1)
                V.tensor_tensor(xe[:, 0:4], psum[:, 3].rearrange("p (k c) -> p k c", k=4), nf, ALU.mult).then_inc(
                    xe_dve, 1)
                take_turned(it)
                swiglu(it, 0, 2 * p)
                add_scattered(it, (0, 1, 2))
                take_down(it, 0, 2 * p)
                add_scattered(it, (3, 4, 5))
                swiglu(it, 1, 2 * p + 1)
                add_scattered(it, (6, 7))
                take_down(it, 1, 2 * p + 1)
                assert loop.n == LOOP_STEPS

            dve.wait_ge(pairs_ready, 1)
            pairs = dve.value_load(pairs_i[0:1, 0:1], min_val=NPAIR, max_val=NPAIR * NPASS)
            with dve.Fori(0, NPASS) as r:
                with dve.If(pairs > r * NPAIR):
                    with dve.Fori(0, NPAIR) as p:
                        pair(r, p)
                    V.tensor_scalar(place[:, :, :], place[:, :, :], float(CAP), None, ALU.subtract).then_inc(
                        place_ready, 1)
            take_turned(pairs)
            add_scattered(pairs, range(KD))

            dve.wait_ge(final_in, 16)
            for t, (_, n) in enumerate(TILES):
                dve.wait_ge(y_turned, t + 1)
                V.tensor_tensor(tok[0:n, t], banks(2 * t, 2)[0:n], tok[0:n, t], ALU.add).then_inc(y_summed, 1)
            dve.wait_ge(y_rms, 3)
            for t, (_, n) in enumerate(TILES):
                V.reciprocal(rstd[0:n, t:t + 1], rms[0:n, t:t + 1]).then_inc(y_rstd, 1)
            dve.wait_ge(y_rstd, 3)
            for t, (_, n) in enumerate(TILES):
                V.scalar_tensor_tensor(tok[0:n, t], tok[0:n, t], rstd[0:n, t:t + 1], w_final[0:n], ALU.mult,
                                       ALU.mult).then_inc(y_ready, 1)


_INS = ["x_prompt", "x_sample", "state_ret", "state_pool", "meta_tokens", "norm_mix", "w_in", "ret_gn", "pool_w",
        "pool_scale", "w_ret_branch", "w_pool_branch", "w_out", "norm_ffn", "w_router", "b_router", "w_gate_up",
        "b_gate_up", "w_down", "b_down", "norm_final"]
_OUTS = [(1, NPR, D), (NS, 1, D), (1, 1, H, DK, DV), (1, 1, PBUF, PG * P), (1, NS, H, DK, DV), (1, NS, PBUF, PG * P)]


def kernel(**inputs):
    import numpy as _np
    import concourse.bacc as _bacc
    from concourse.bass_utils import run_bass_kernel_spmd as _run

    nc = _bacc.Bacc("TRN2", target_bir_lowering=False, num_devices=1)
    arrays = {f"in_{n}": _np.ascontiguousarray(inputs[n]) for n in _INS}
    arrays["in_consts"] = constants()
    ins = {n[3:]: nc.dram_tensor(n, a.shape, F32, kind="ExternalInput").ap() for n, a in arrays.items()}
    outs = [nc.dram_tensor(f"out_{i}", s, F32, kind="ExternalOutput").ap() for i, s in enumerate(_OUTS)]
    build(nc, ins, outs)
    r = _run(nc, [arrays], core_ids=[0])
    return tuple(r.results[0][f"out_{i}"] for i in range(len(_OUTS)))
```

```python
from contextlib import ExitStack

import numpy as np

import concourse.bass as bass
from concourse import mybir

F32 = mybir.dt.float32
F32R = mybir.dt.float32r
I32 = mybir.dt.int32
U32 = mybir.dt.uint32
ALU = mybir.AluOpType
ACT = mybir.ActivationFunctionType
AX = mybir.AxisListType

P = 128
D = 1024
KD = D // P
NPR, NS, NM = 256, 8, 16
NT = NPR + NS
NA = NT + NM
H, DK, DV = 4, 128, 256
PG = 4
WINDOWS = (2, 4, 8, 16)
PBUF = 15
NE = 32
TOPK = 4
CAP = 64
NPASS = -(-NT // CAP)
NPAIR = NE // 2
ALPHA, LIMIT = 1.702, 7.0
EPS = 1e-6
PAST = 2048
FAR = 4096.0
SLOT = 2048
RING = 12
STAGE = 8
HALF = SLOT // 2
ORDER = ([(0, "gu", k) for k in range(8)] + [(1, "gu", k) for k in range(2)] + [(0, "dn", k) for k in range(4)]
         + [(1, "gu", k) for k in range(2, 8)] + [(1, "dn", k) for k in range(4)])
NCH = len(ORDER)
UNITS = [(*c, h) for c in ORDER for h in range(2)]
NU = len(UNITS)


WHOLE = set()
SPLITS = [u for u in range(NU) if UNITS[u][0:3] not in WHOLE]
NSPLIT = len(SPLITS)


def ends_banks(u):
    return UNITS[u][1:3] == ("gu", KD - 1) or UNITS[u][1:] == ("dn", 3, 1)


SCATTER_AFTER = 2
COUNTED = [u for u in range(NU) if not ends_banks(u)]
LEAD = 4
S_AT = {UNITS[u][0:3]: i for i, u in reversed(list(enumerate(SPLITS)))}
D0_END = S_AT[0, "dn", 3] + 2
SWIGLU_AT = (S_AT[1, "gu", 0] + 4, S_AT[1, "dn", 0] + 4)

V0, K0, Q0, P0, G0, GA0, GB0 = 0, 8, 12, 16, 20, 28, 36
PROJ = [*range(8, 16), *range(4, 8), *range(0, 4), *range(24, 28), *range(16, 24), *range(28, 36), *range(36, 44)]
N_IN = len(PROJ)
T_POOL, T_YB, T_YA, T_OUT, T_END = 44, 48, 56, 64, 72

AUX_BANKS = {}
AUX_AFTER = {n: [] for n in range(-1, T_END)}


def _aux(after, name, banks):
    AUX_BANKS[name] = banks
    AUX_AFTER[after].append(name)


for _j in range(8):
    _aux(_j + 1, ("v", _j), (4 + _j % 2,))
for _j in range(4):
    _aux(_j + 10, ("k", _j), (4 + _j % 2,))
_aux(9, ("hist",), (6,))
_aux(15, ("s_meta",), (6, 7))
_aux(17, ("score", 0), (4,))
_aux(18, ("score", 1), (5,))
_aux(19, ("s_next", 0), (6, 7))
_aux(20, ("o", 0), (6, 7))
_aux(21, ("s_next", 1), (4, 5))
_aux(22, ("o", 1), (6, 7))
_aux(23, ("ptok",), (4, 5))
for _b in range(NS):
    _aux(24 + _b, ("outer", _b), ((4, 5), (6, 7))[_b % 2])
_aux(34, ("o_turn",), (6, 7))
for _j in range(8):
    _aux(36 + _j, ("z", _j), (4 + _j % 2,))
AUX = [a for n in range(-1, T_END) for a in AUX_AFTER[n]]
AUX_AT = {a: i for i, a in enumerate(AUX)}


def bank_owner(i):
    last = 0
    for j in range(i):
        if set(AUX_BANKS[AUX[j]]) & set(AUX_BANKS[AUX[i]]):
            last = j + 1
    return last


CHUNKS = ([("in", n) for n in range(0, N_IN, 2)] + [("pb", c) for c in range(2)]
          + [("ret", c) for c in range(4)] + [("out", c) for c in range(4)])
MIX_SLOTS = 4
C_PB = N_IN // 2
C_RET, C_OUT = C_PB + 2, C_PB + 6


def last_tile(i):
    kind, c = CHUNKS[i]
    return {"in": c + 1, "pb": T_YB + 4 * c + 3, "ret": T_YA + 2 * c + 1, "out": T_OUT + 2 * c + 1}[kind]


ROOT_AFTER = {21: 0, 23: 1, 35: 2}

CONST = {}
_o = 0
for _n, _w in (("ident", 128), ("before", 128), ("ones", 128), ("twin", CAP), ("iota", CAP), ("experts", NE), ("passes", 8),
               ("cos", NA), ("sin", NA), ("mask", H * P), ("q_dec", H * P), ("k_dec", H), ("k_dec_meta", H),
               ("eps", 1)):
    CONST[_n] = (_o, _w)
    _o += _w
N_CONST = _o + (-_o) % 4


def constants():
    c = np.zeros((P, N_CONST), np.float32)

    def put(name, v):
        o, w = CONST[name]
        c[:, o:o + w] = v

    i = np.arange(P, dtype=np.float32)
    put("ident", np.eye(P))
    put("before", np.triu(np.ones((P, P)), 1))
    put("ones", 1.0)
    put("twin", np.concatenate([np.eye(CAP), np.eye(CAP)]))
    put("iota", np.arange(CAP)[None])
    put("experts", np.arange(NE)[None])
    put("passes", (np.arange(8) * CAP + (np.arange(8) >= NPASS) * 1e6)[None])
    pos = np.concatenate([NM + np.arange(NPR), np.full(NS, PAST), np.arange(NM)]).astype(np.float32)
    inv = np.power(np.float32(10000.0), -np.arange(0, DK, 2, dtype=np.float32) / np.float32(DK)).astype(np.float32)
    ang = (pos[None, :] * np.concatenate([inv, inv])[:, None]).astype(np.float32)
    put("cos", np.cos(ang))
    put("sin", np.sin(ang) * np.where(np.arange(P) < DK // 2, -1.0, 1.0)[:, None])
    g = log_decay()
    diff = i[None, :] - i[:, None]
    mask = [np.where(diff >= 0, np.exp(np.maximum(diff, 0) * g[h]), 0.0) for h in range(H)]
    put("mask", np.concatenate(mask, 1))
    put("q_dec", np.concatenate([np.exp((i + 1) * g[h]) for h in range(H)])[None])
    put("k_dec", np.exp((P - 1 - i)[:, None] * g[None]))
    meta = np.zeros((P, H), np.float32)
    meta[32:32 + NM] = np.exp((NM - 1 - np.arange(NM, dtype=np.float32))[:, None] * g[None])
    put("k_dec_meta", meta)
    put("eps", EPS)
    return c


def log_decay():
    return np.log1p(-np.exp2(np.float32(-5.0) - np.arange(H, dtype=np.float32))).astype(np.float32)


CHUNK_DEC = [float(np.exp(np.float32(P) * g)) for g in log_decay()]
STEP_DEC = [float(np.exp(g)) for g in log_decay()]


def build(nc, ins, outs):
    x_prompt, x_sample, state_ret, state_pool, meta = (
        ins[n] for n in ("x_prompt", "x_sample", "state_ret", "state_pool", "meta_tokens"))
    y_prompt, y_sample, ret_prompt, pool_prompt, ret_sample, pool_sample = outs

    with ExitStack() as ctx:
        def sem(name):
            return ctx.enter_context(nc.semaphore(name))

        mixer_only = ExitStack()

        def sb(name, n, dt=F32, where=ctx):
            return where.enter_context(nc.sbuf_tensor(name, [P, n], dt))

        def msb(name, n):
            return sb(name, n, F32, mixer_only)

        with ExitStack() as twice:
            ring_r = sb("ring_r", RING * SLOT, F32R, twice)
        ring = sb("ring", RING * SLOT)

        def slot(s):
            return ring[:, s * SLOT:(s + 1) * SLOT]

        def raw_half(u):
            o = (u // 2) % RING * SLOT + u % 2 * HALF
            return ring[:, o:o + HALF]

        def lo_half(u):
            o = (u // 2) % RING * SLOT + u % 2 * HALF
            return ring_r[:, o:o + HALF]

        early = [4 * SLOT]

        def in_ring(n):
            o = early[0]
            early[0] += n
            assert early[0] <= 8 * SLOT
            return ring[:, o:o + n]

        state_s = in_ring(4 * H * DV).rearrange("p (s h v) -> p s h v", s=4, h=H)
        k_only = in_ring(2 * H * DK).rearrange("p (s h d) -> p s h d", s=2, h=H)
        rope_x = in_ring(2 * NA).rearrange("p (s t) -> p s t", s=2)
        rope_y = in_ring(2 * NA).rearrange("p (s t) -> p s t", s=2)
        v_T = in_ring(2 * NA).rearrange("p (s t) -> p s t", s=2)
        hist = in_ring(PG * P)
        p_rows = in_ring(PG * P)
        q_s = in_ring(H * NS).rearrange("p (h b) -> p h b", h=H)
        hs_T = in_ring(8 * NS).rearrange("p (m b) -> p m b", m=8)
        p_s = in_ring(PG * NS).rearrange("p (g b) -> p g b", g=PG)
        hist_sum = in_ring(PG * NS).rearrange("p (g b) -> p g b", g=PG)

        consts = sb("consts", N_CONST)

        def const(name):
            o, w = CONST[name]
            return consts[:, o:o + w]

        ident, ones = const("ident"), const("ones")
        z_T = sb("z_T", KD * NT).rearrange("p (k t) -> p k t", k=KD)
        y_T = z_T
        normed = sb("normed", 3 * D).rearrange("p (t d) -> p t d", t=3)
        rows = normed[:, 0, :]
        params = sb("params", 28 + 16 * NE)
        norm_mix, gn_w, pool_scale, norm_ffn = (params[:, a:b] for a, b in ((0, 8), (8, 16), (16, 20), (20, 28)))
        b_gu = params[:, 28:28 + 16 * NE].rearrange("p (e m) -> p e m", e=NE)
        small = sb("small", 128)
        stats = small[:, 0:24].rearrange("p (h s) -> p h s", h=H)
        moments = small[:, 24:32].rearrange("p (h s) -> p h s", h=H)
        spread = small[:, 32:36]
        sumsq, rms, rstd = small[:, 40:43], small[:, 44:47], small[:, 48:51]
        top = small[:, 56:80].rearrange("p (t j) -> p t j", t=3)
        neg_top = small[:, 80:83]
        gate_sum, gate_rec = small[:, 84:87], small[:, 88:91]
        most = small[0:1, 92:93]
        beyond = small[0:1, 96:104]
        pairs_f = small[0:1, 104:105]
        top_i = sb("top_i", 24, U32).rearrange("p (t j) -> p t j", t=3)
        top_f = sb("top_f", 24).rearrange("p (t j) -> p t j", t=3)
        pairs_i = sb("pairs_i", 4, I32)
        route = sb("route", 5 * 3 * NE).rearrange("p (a t e) -> p a t e", a=5, t=3)
        logits, expd, chosen, gates, gates_s = (route[:, a] for a in range(5))
        place = sb("place", 3 * (NE + 2)).rearrange("p (t e) -> p t e", t=3)
        tok = msb("tok", 3 * D).rearrange("p (t d) -> p t d", t=3)
        u_T = msb("u_T", KD * NA).rearrange("p (k t) -> p k t", k=KD)
        qk = msb("qk", H * NT + H * NA)
        q_T = qk[:, 0:H * NT].rearrange("p (h t) -> p h t", h=H)
        k_T = qk[:, H * NT:].rearrange("p (h t) -> p h t", h=H)
        gate_a = qk[:, 0:KD * NT].rearrange("p (k t) -> p k t", k=KD)
        xn_T = gate_a
        vk = msb("vk", 3 * D + 3 * H * DK)
        v_tok = vk[:, 0:2 * D].rearrange("p (t v) -> p t v", t=2)
        k_tok = vk[:, 2 * D:2 * D + 2 * H * DK].rearrange("p (t d) -> p t d", t=2)
        v_sm = vk[:, 2 * D + 2 * H * DK:3 * D + 2 * H * DK]
        k_sm = vk[:, 3 * D + 2 * H * DK:]
        gate_b = vk[:, 0:KD * NT].rearrange("p (k t) -> p k t", k=KD)
        p_ext_all = msb("p_ext", PG * (NM + NPR))
        p_ext = p_ext_all.rearrange("p (g t) -> p g t", g=PG)
        win = msb("win", 2 * (NM + NPR)).rearrange("p (s t) -> p s t", s=2)
        pooled = msb("pooled", PG * NT).rearrange("p (g t) -> p g t", g=PG)
        rs = msb("rs", 2 * H * DV)
        ret_s = rs.rearrange("p (s h v) -> p s h v", s=2, h=H)
        sc = msb("sc", 2 * H * P)
        scores = sc.rearrange("p (c h i) -> p c h i", c=2, h=H)
        qd_all = msb("qd", 2 * H * P)
        qd = qd_all.rearrange("p (c h i) -> p c h i", c=2, h=H)
        match = qd_all[:, 0:3 * TOPK * NE].rearrange("p (a e) -> p a e", e=NE)
        pool_w = msb("pool_w", PG * P).rearrange("p (g e) -> p g e", g=PG)
        w_router = msb("w_router", KD * NE).rearrange("p (k e) -> p k e", k=KD)
        b_router = msb("b_router", NE)
        squares = qk[:, D:2 * D]
        z_sq = rs[:, 0:D]
        w_ffn = rs[:, D:2 * D]
        mixer_only.close()

        stage_hi = [sb(f"stage_hi{i}", HALF, F32R) for i in range(STAGE)]
        x_parts = sb("x_parts", KD * 2 * P, F32R).rearrange("p (k j s c) -> p k j s c", k=KD, j=2, s=2)
        act_parts = sb("act_parts", KD * P, F32R).rearrange("p (k s c) -> p k s c", k=KD, s=2)
        h_raw = sb("h_raw", 2 * D)
        hg, hu, hs = (sb(n, KD * CAP).rearrange("p (m c) -> p m c", m=KD) for n in ("hg", "hu", "hs"))
        out_sb = sb("out_sb", 2 * D).rearrange("p (j d) -> p j d", j=2)
        one_hot = sb("one_hot", 3 * P).rearrange("p (t j c) -> p t j c", t=3, j=2)
        gated = sb("gated", 6 * P).rearrange("p (t j s c) -> p t j s c", t=3, j=2, s=2)
        w_final = sb("w_final", D)
        g_T = sb("g_T", 2 * NT).rearrange("p (j t) -> p j t", j=2)
        out_sq = h_raw[:, 0:D]

        psum = ctx.enter_context(nc.psum_tensor("psum", [P, 8, 512], F32))

        def banks(a, n=1):
            return psum[:, a:a + n].rearrange("p b c -> p (b c)")

        consts_in, x_in, rows_in, hist_in, misc_in, final_in = (
            sem(n) for n in ("consts_in", "x_in", "rows_in", "hist_in", "misc_in", "final_in"))
        wmix_in = [sem(f"wmix_in{s}") for s in range(MIX_SLOTS)]
        state_in = [sem(f"state_in{s}") for s in range(4)]
        state_out = [sem(f"state_out{s}") for s in range(4)]
        expert_in = [sem(f"expert_in{s}") for s in range(RING)]
        stored, y_out = sem("stored"), sem("y_out")
        cleared, x_scaled, sq_done, rms_done, rstd_done = (
            sem(n) for n in ("cleared", "x_scaled", "sq_done", "rms_done", "rstd_done"))
        params_turned, params_ready, x_turned, u_ready = (
            sem(n) for n in ("params_turned", "params_ready", "x_turned", "u_ready"))
        tile_done, act_took, dve_took = sem("tile_done"), sem("act_took"), sem("dve_took")
        aux_done, aux_took, roped = sem("aux_done"), sem("aux_took"), sem("roped")
        pooled_ready, k_only_ready, state_decayed, state_ready = (
            sem(n) for n in ("pooled_ready", "k_only_ready", "state_decayed", "state_ready"))
        outer_read, o_s_ready, ret_out = sem("outer_read"), sem("o_s_ready"), sem("ret_out")
        spread_ready, spread_rooted = sem("spread_ready"), sem("spread_rooted")
        zeroed = sem("zeroed")
        mix_turned, h_ready, xn_ready, xn_turned, xn_T_ready = (
            sem(n) for n in ("mix_turned", "h_ready", "xn_ready", "xn_turned", "xn_T_ready"))
        logits_done, neg_ready, exp_ready, chosen_ready, placed, pairs_ready, place_ready = (
            sem(n) for n in ("logits_done", "neg_ready", "exp_ready", "chosen_ready", "placed", "pairs_ready",
                             "place_ready"))
        dve_step, act_step, pool_step = sem("dve_step"), sem("act_step"), sem("pool_step")
        dve_loop = sem("dve_loop")
        half_used, split_hi, split_lo = sem("half_used"), sem("split_hi"), sem("split_lo")
        one_hot_ready, gated_ready, gathered, x_hi, x_lo = (
            sem(n) for n in ("one_hot_ready", "gated_ready", "gathered", "x_hi", "x_lo"))
        gu_done, raw_ready, hidden_turned, hidden_took, gate_clipped, silu_ready, act_ready = (
            sem(n) for n in ("gu_done", "raw_ready", "hidden_turned", "hidden_took", "gate_clipped", "silu_ready",
                             "act_ready"))
        down_done, out_ready, gates_turned, g_T_ready, scattered, y_added = (
            sem(n) for n in ("down_done", "out_ready", "gates_turned", "g_T_ready", "scattered", "y_added"))
        h_turned, h_T_ready, bias_in = sem("h_turned"), sem("h_T_ready"), sem("bias_in")
        ffn_in, ffn_scaled = sem("ffn_in"), sem("ffn_scaled")
        y_turned, y_taken, y_sq, y_rms, y_rstd, y_ready = (
            sem(n) for n in ("y_turned", "y_taken", "y_sq", "y_rms", "y_rstd", "y_ready"))

        class Steps:

            def __init__(self, eng, s):
                self.eng, self.s, self.n, self.base = eng, s, 0, 0

            def __call__(self, ins):
                self.n += 1
                ins.then_inc(self.s, 1)
                return ins

            def wait(self):
                self.eng.wait_ge(self.s, self.n + self.base)

        def wait_taken(eng, n):
            if n < T_YB:
                eng.wait_ge(act_took, n + 1)
            elif n < T_OUT:
                eng.wait_ge(dve_took, n - T_YB + 1)
            else:
                eng.wait_ge(act_took, T_YB + n - T_OUT + 1)

        TILES = ((0, P), (P, P), (2 * P, NS))

        gu_w = ins["w_gate_up"].rearrange("l e (k p) f -> (l e) p k f", p=P)
        dn_w = ins["w_down"].rearrange("l e (k p) f -> (l e) p k f", p=P)

        def wait_used(eng, it, u):
            if u < 0:
                it, u = it - 1, u + NU
            j, part, _, h = UNITS[u]
            if ends_banks(u) and part == "gu":
                eng.wait_ge(gu_done, 4 * (2 * it + j) + 2 * h + 2)
            elif ends_banks(u):
                eng.wait_ge(down_done, 2 * (2 * it + j) + 4)
            else:
                eng.wait_ge(half_used, len(COUNTED) * it + COUNTED.index(u) + 1 + STAGE)

        def wait_staged(eng, it, i):
            if i >= STAGE:
                wait_used(eng, it, SPLITS[i - STAGE])
            else:
                wait_used(eng, it, SPLITS[i - STAGE + NSPLIT] - NU)

        def load_chunk(sp, p, i):
            j, part, k = ORDER[i]
            e, s = 2 * p + j, i % RING
            if part == "gu":
                src = gu_w[bass.ds(e, 1), :, k, :].rearrange("a p f -> p (a f)")
                sp.dma_start(slot(s), src).then_inc(expert_in[s], 16)
            else:
                src = dn_w[bass.ds(e, 1), :, 2 * k:2 * k + 2, :].rearrange("a p k f -> p (a k) f")
                sp.dma_start(slot(s).rearrange("p (k f) -> p k f", k=2), src).then_inc(expert_in[s], 16)

        block = ctx.enter_context(nc.Block())

        @block.sync
        def _(sp):
            w_in = ins["w_in"].rearrange("l (k p) n -> p (l k) n", p=P)
            w_pb = ins["w_pool_branch"].rearrange("l (k p) n -> p (l k) n", p=P)
            w_ret = ins["w_ret_branch"].rearrange("l (k p) n -> p (l k) n", p=P)
            w_out = ins["w_out"].rearrange("l (k p) n -> p (l k) n", p=P)

            sp.dma_start(tok[:, 0:2, :], x_prompt[0].rearrange("(t p) d -> p t d", p=P)).then_inc(x_in, 16)
            sp.wait_ge(cleared, 1)
            sp.dma_start(tok[0:NS, 2, :], x_sample.rearrange("b s d -> (b s) d")).then_inc(x_in, 16)
            sp.dma_start(tok[32:32 + NM, 2, :], meta).then_inc(x_in, 16)

            def mix_chunk(i):
                kind, c = CHUNKS[i]
                s = i % MIX_SLOTS
                if i >= MIX_SLOTS:
                    sp.wait_ge(tile_done, last_tile(i - MIX_SLOTS) + 1)
                dst = slot(8 + s)
                if kind == "in":
                    cols = PROJ[c] * P
                    src = w_in[:, :, cols:cols + 2 * P]
                    dst = dst.rearrange("p (k n) -> p k n", k=KD)
                elif kind == "pb":
                    src = w_pb[:, :, c * 512:c * 512 + 512]
                    dst = dst.rearrange("p (k n) -> p k n", k=PG)
                else:
                    src = (w_ret if kind == "ret" else w_out)[:, :, c * 256:c * 256 + 256]
                    dst = dst.rearrange("p (k n) -> p k n", k=KD)
                sp.dma_start(dst, src).then_inc(wmix_in[s], 16)

            for i in range(MIX_SLOTS):
                mix_chunk(i)
            for s in range(4):
                load_chunk(sp, 0, s)
            for i in range(MIX_SLOTS, C_PB):
                mix_chunk(i)
            sp.wait_ge(aux_took, AUX_AT[("o_turn",)] + 1)
            for s in range(4):
                sp.wait_ge(state_out[s], 32)
            sp.wait_ge(stored, 16 * 3)
            for s in range(4, 8):
                load_chunk(sp, 0, s)
            for i in range(C_PB, len(CHUNKS)):
                mix_chunk(i)
            for s in range(MIX_SLOTS):
                sp.wait_ge(tile_done, last_tile(len(CHUNKS) - MIX_SLOTS + s) + 1)
                load_chunk(sp, 0, 8 + s)

            def pair(it, p, first=0):
                for i in range(first, NCH):
                    wait_used(sp, it, 2 * (i - RING) + 1)
                    load_chunk(sp, p, i)

            pair(0, 0, RING)
            with sp.Fori(1, NPAIR) as p:
                pair(p, p)
            sp.wait_ge(pairs_ready, 1)
            pairs = sp.value_load(pairs_i[0:1, 0:1], min_val=NPAIR, max_val=NPAIR * NPASS)
            with sp.Fori(1, NPASS) as r:
                with sp.If(pairs > r * NPAIR):
                    with sp.Fori(0, NPAIR) as p:
                        pair(r * NPAIR + p, p)
            for t, (c0, n) in enumerate(TILES):
                sp.wait_ge(y_ready, t + 1)
                dst = y_sample.rearrange("b s d -> (b s) d") if t == 2 else y_prompt[0, c0:c0 + n, :]
                sp.dma_start(dst, normed[0:n, t, :]).then_inc(y_out, 16)
            sp.wait_ge(y_out, 16 * 3)
            sp.wait_ge(stored, 16 * 3)
            sp.wait_ge(ret_out, 16)
            for s in range(4):
                sp.wait_ge(state_out[s], 32)

        @block.gpsimd
        def _(pool):
            step = Steps(pool, pool_step)
            nc.gpsimd.memset(tok[0:64, 2, :], 0.0).then_inc(cleared, 1)
            nc.gpsimd.dma_start(consts[:, :], ins["consts"]).then_inc(consts_in, 16)
            for o, name, n in ((0, "norm_mix", 8), (8, "ret_gn", 8), (16, "pool_scale", 4), (20, "norm_ffn", 8)):
                pool.dma_start(rows[o:o + n, 0:P], ins[name].rearrange("l (a p) -> (l a) p", p=P)).then_inc(rows_in, 16)
            bg = ins["b_gate_up"].rearrange("l e (m p) -> (l e m) p", p=P)
            pool.dma_start(rows[:, P:5 * P].rearrange("r (c p) -> r c p", c=4),
                           bg.rearrange("(c r) p -> r c p", r=P)).then_inc(rows_in, 16)
            pool.dma_start(hist[0:NS * PBUF, :], state_pool.rearrange("l b t c -> (l b t) c")).then_inc(hist_in, 16)
            for b in range(4):
                pool.dma_start(state_s[:, b], state_ret[0, b].rearrange("h d v -> d h v")).then_inc(state_in[b], 16)
            pool.dma_start(pool_w, ins["pool_w"].rearrange("l g c e -> c (l g) e")).then_inc(misc_in, 16)
            pool.dma_start(w_router, ins["w_router"].rearrange("l (k p) e -> p (l k) e", p=P)).then_inc(misc_in, 16)
            pool.dma_start(b_router[:, :], ins["b_router"].broadcast_to([P, NE])).then_inc(misc_in, 16)
            pool.dma_start(pool_sample[0, :, 0:PBUF - 1, :], state_pool[0, :, 1:PBUF, :]).then_inc(stored, 16)

            def only_k(b):
                if b >= 2:
                    pool.wait_ge(aux_done, AUX_AT[("outer", b - 2)] + 1)
                nc.gpsimd.tensor_scalar(k_only[0:NS, b % 2].rearrange("p h d -> p (h d)"), k_sm[0:NS, :],
                                        ident[0:NS, b:b + 1], None, ALU.mult).then_inc(k_only_ready, 1)

            def decay_state(b):
                pool.wait_ge(state_in[b % 4], 16 * (b // 4 + 1))
                for h in range(H):
                    last = nc.gpsimd.tensor_scalar(state_s[:, b % 4, h], state_s[:, b % 4, h], STEP_DEC[h], None,
                                                   ALU.mult)
                last.then_inc(state_decayed, 1)

            for b in range(4):
                decay_state(b)

            n = NM + NPR
            for g, w in enumerate(WINDOWS):
                pool.wait_ge(act_took, P0 + g + 1)
                src, lag = p_ext[:, g], 1
                for i in range(g + 1):
                    dst = win[:, i % 2]
                    step(nc.gpsimd.tensor_tensor(dst[:, 2 * lag - 1:n], src[:, 2 * lag - 1:n],
                                                 src[:, lag - 1:n - lag], ALU.add))
                    step.wait()
                    src, lag = dst, 2 * lag
                step(nc.gpsimd.tensor_scalar(src[:, NM:n], src[:, NM:n], 1.0 / w, None, ALU.mult))
                pool.wait_ge(aux_took, AUX_AT[("hist",)] + 1)
                step(nc.gpsimd.tensor_tensor(hist_sum[:, g], hist_sum[:, g], p_s[:, g], ALU.add))
                step.wait()
                step(nc.gpsimd.tensor_scalar(hist_sum[:, g], hist_sum[:, g], 1.0 / w, None, ALU.mult))
                step(nc.gpsimd.tensor_tensor(pooled[:, g, 0:NPR], src[:, NM:n], p_ext[:, g, NM:n], ALU.subtract))
                step.wait()
                nc.gpsimd.tensor_tensor(pooled[:, g, NPR:NT], hist_sum[:, g], p_s[:, g],
                                        ALU.subtract).then_inc(pooled_ready, 1)

            only_k(0)
            only_k(1)
            pool.wait_ge(aux_took, AUX_AT[("o", 1)] + 1)
            pool.dma_start(w_ffn, ins["norm_ffn"].broadcast_to([P, D])).then_inc(ffn_in, 16)
            for b in range(NS):
                pool.wait_ge(aux_took, AUX_AT[("outer", b)] + 1)
                pool.dma_start(ret_sample[0, b].rearrange("h d v -> d h v"), state_s[:, b % 4]).then_inc(
                    state_out[b % 4], 16)
                if b + 2 < NS:
                    only_k(b + 2)
                if 1 <= b <= 4:
                    s = b - 1
                    pool.wait_ge(state_out[s], 16)
                    pool.wait_ge(outer_read, s + 1)
                    pool.dma_start(state_s[:, s], state_ret[0, s + 4].rearrange("h d v -> d h v")).then_inc(
                        state_in[s], 16)
                if 2 <= b <= 5:
                    decay_state(b + 2)
            pool.dma_start(ret_prompt[0, 0].rearrange("h d v -> d h v"), ret_s[:, 0]).then_inc(ret_out, 16)
            pool.dma_start(pool_prompt[0, 0], p_rows[0:PBUF, :]).then_inc(stored, 16)
            pool.dma_start(pool_sample[0, :, PBUF - 1, :], p_rows[32:32 + NS, :]).then_inc(stored, 16)
            nc.gpsimd.memset(route[:, :, :, :], 0.0).then_inc(zeroed, 1)
            nc.gpsimd.memset(top_f[:, :, :], float(NE)).then_inc(zeroed, 1)
            pool.wait_ge(h_T_ready, KD)
            pool.wait_ge(chosen_ready, 1)
            pool.wait_ge(ffn_scaled, 3)
            pool.dma_start(w_final[0:NE, :], ins["b_down"].rearrange("l e d -> (l e) d")).then_inc(bias_in, 16)
            nc.gpsimd.memset(g_T[:, :, :], 0.0).then_inc(half_used, STAGE)
            nc.gpsimd.memset(out_sb[:, 0, :], 0.0).then_inc(out_ready, 2)
            pool.wait_ge(down_done, 2)
            pool.dma_start(w_final[:, :], ins["norm_final"].rearrange("(a d) -> a d", a=1).broadcast_to([P, D])).then_inc(
                final_in, 16)

        @block.tensor
        def _(pe):
            mm = pe.matmul

            def aux(a):
                i = AUX_AT[a]
                if bank_owner(i):
                    pe.wait_ge(aux_took, bank_owner(i))
                kind, bank = a[0], AUX_BANKS[a][0]
                if kind == "v":
                    j = a[1]
                    pe.wait_ge(act_took, V0 + j + 1)
                    src = v_T[:, j % 2]
                    pe.transpose(banks(bank)[:, 0:P], src[:, 0:P], ident)
                    pe.transpose(banks(bank)[:, P:2 * P], src[:, P:2 * P], ident)
                    pe.transpose(banks(bank)[0:NS, 2 * P:3 * P], src[:, NPR:NT], ident)
                    last = pe.transpose(banks(bank)[0:NM, 3 * P:4 * P], src[:, NT:NA], ident)
                elif kind == "k":
                    j = a[1]
                    pe.wait_ge(roped, j + 1)
                    src = k_T[:, j]
                    pe.transpose(banks(bank)[:, 0:P], src[:, 0:P], ident)
                    pe.transpose(banks(bank)[:, P:2 * P], src[:, P:2 * P], ident)
                    pe.transpose(banks(bank)[0:NS, 2 * P:3 * P], src[:, NPR:NT], ident)
                    last = pe.transpose(banks(bank)[0:NM, 3 * P:4 * P], src[:, NT:NA], ident)
                elif kind == "hist":
                    pe.wait_ge(hist_in, 16)
                    n = NS * PBUF
                    for g in range(PG):
                        last = pe.transpose(banks(bank)[:, g * P:g * P + n], hist[0:n, g * P:(g + 1) * P],
                                            ident[0:n, 0:n])
                elif kind == "s_meta":
                    pe.wait_ge(aux_took, AUX_AT[("k", 3)] + 1)
                    for h in range(H):
                        last = mm(banks(bank, 2)[:, h * DV:(h + 1) * DV], k_sm[32:32 + NM, h * DK:(h + 1) * DK],
                                  v_sm[32:32 + NM, h * DV:(h + 1) * DV], start=True, stop=True)
                elif kind == "score":
                    c = a[1]
                    pe.wait_ge(roped, 8)
                    for h in range(H):
                        last = mm(banks(bank)[:, h * P:(h + 1) * P], k_T[:, h, c * P:(c + 1) * P],
                                  q_T[:, h, c * P:(c + 1) * P], start=True, stop=True)
                elif kind == "s_next":
                    c = a[1]
                    for h in range(H):
                        last = mm(banks(bank, 2)[:, h * DV:(h + 1) * DV], k_tok[:, c, h * DK:(h + 1) * DK],
                                  v_tok[:, c, h * DV:(h + 1) * DV], start=True, stop=True)
                elif kind == "o":
                    c = a[1]
                    before = ("s_meta",) if c == 0 else ("s_next", 0)
                    pe.wait_ge(aux_took, max(AUX_AT[("score", c)], AUX_AT[before]) + 1)
                    for h in range(H):
                        o = banks(bank, 2)[:, h * DV:(h + 1) * DV]
                        mm(o, scores[:, c, h], v_tok[:, c, h * DV:(h + 1) * DV], start=True, stop=False)
                        last = mm(o, qd[:, c, h], ret_s[:, c, h], start=False, stop=True)
                elif kind == "ptok":
                    pe.wait_ge(act_took, P0 + PG)
                    for g in range(PG):
                        pe.transpose(banks(bank)[0:PBUF, g * P:(g + 1) * P], p_ext[:, g, NM + NPR - PBUF:], ident)
                    for g in range(PG):
                        last = pe.transpose(banks(bank + 1)[0:NS, g * P:(g + 1) * P], p_s[:, g], ident)
                elif kind == "outer":
                    b = a[1]
                    pe.wait_ge(k_only_ready, b + 1)
                    for h in range(H):
                        last = mm(banks(bank, 2)[:, h * DV:(h + 1) * DV], k_only[0:NS, b % 2, h],
                                  v_sm[0:NS, h * DV:(h + 1) * DV], start=True, stop=True)
                elif kind == "o_turn":
                    pe.wait_ge(o_s_ready, 1)
                    for m in range(8):
                        last = pe.transpose(banks(bank, 2)[0:NS, m * P:(m + 1) * P], hs_T[:, m], ident)
                elif kind == "z":
                    j = a[1]
                    pe.wait_ge(aux_took, AUX_AT[("o_turn",)] + 1)
                    for t, (c0, n) in enumerate(TILES):
                        last = pe.transpose(banks(bank)[:, c0:c0 + n], normed[0:n, t, j * P:(j + 1) * P],
                                            ident[0:n, 0:n])
                last.then_inc(aux_done, 1)

            def read_state(b):
                pe.wait_ge(aux_took, AUX_AT[("outer", b)] + 1)
                for h in range(H):
                    for v in range(2):
                        m = 2 * h + v
                        last = mm(psum[:, 3, m * NS + b:m * NS + b + 1], state_s[:, b % 4, h, v * P:(v + 1) * P],
                                  q_s[:, h, b:b + 1], start=True, stop=True)
                last.then_inc(outer_read, 1)

            pe.wait_ge(consts_in, 16)
            pe.wait_ge(rows_in, 5 * 16)
            pe.transpose(psum[:, 0, 0:28], rows[0:28, 0:P], ident[0:28, 0:28])
            for c in range(4):
                last = pe.transpose(psum[:, 1, c * P:(c + 1) * P], rows[:, (1 + c) * P:(2 + c) * P], ident)
            last.then_inc(params_turned, 1)
            for k in range(KD):
                if k == 0:
                    pe.wait_ge(x_scaled, 3)
                if k >= 4:
                    pe.wait_ge(u_ready, 2 * (k - 3))
                for t, n in enumerate((P, P, 48)):
                    last = pe.transpose(psum[:, 4 + k % 4, t * P:t * P + n], normed[0:n, t, k * P:(k + 1) * P],
                                        ident[0:n, 0:n])
                last.then_inc(x_turned, 1)
            pe.wait_ge(u_ready, 2 * KD)
            pe.wait_ge(params_ready, 2)

            for n in range(T_END):
                if n >= 3:
                    wait_taken(pe, n - 3)
                o = psum[:, n % 3]
                if n < N_IN:
                    i, width = n // 2, (NA if n < G0 else NT)
                    w = slot(8 + i % MIX_SLOTS).rearrange("p (k n) -> p k n", k=KD)
                    cols = (n % 2) * P
                    x, nk = u_T, KD
                elif n < T_YB:
                    width, nk = NT, 1
                    if n == T_POOL:
                        pe.wait_ge(misc_in, 3 * 16)
                    g = n - T_POOL
                    pe.wait_ge(pooled_ready, g + 1)
                    mm(o[:, 0:NT], pool_w[:, g], pooled[:, g], start=True, stop=True).then_inc(tile_done, 1)
                    continue
                elif n < T_YA:
                    d = n - T_YB
                    i, cols, x, width, nk = C_PB + d // 4, (d % 4) * P, pooled, NT, PG
                    w = slot(8 + i % MIX_SLOTS).rearrange("p (k n) -> p k n", k=PG)
                    if d == 0:
                        pe.wait_ge(act_took, T_YB)
                else:
                    d = n - (T_YA if n < T_OUT else T_OUT)
                    i = (C_RET if n < T_OUT else C_OUT) + d // 2
                    cols, width, nk = (d % 2) * P, NT, KD
                    x = z_T if n < T_OUT else gate_a
                    w = slot(8 + i % MIX_SLOTS).rearrange("p (k n) -> p k n", k=KD)
                    if n == T_YA:
                        pe.wait_ge(aux_took, AUX_AT[("z", 7)] + 1)
                    if n == T_OUT:
                        pe.wait_ge(dve_took, T_OUT - T_YB)
                pe.wait_ge(wmix_in[i % MIX_SLOTS], 16 * (i // MIX_SLOTS + 1))
                for k in range(nk):
                    last = mm(o[:, 0:width], w[:, k, cols:cols + P], x[:, k, 0:width], start=k == 0, stop=k == nk - 1)
                last.then_inc(tile_done, 1)
                for a in AUX_AFTER[n]:
                    aux(a)
                if 25 <= n < 25 + NS:
                    read_state(n - 25)

            for t, (c0, n) in enumerate(TILES):
                bank = (4, 6, 3)[t]
                if t == 0:
                    wait_taken(pe, T_END - 1)
                for d in range(KD):
                    o = banks(bank, 2)[0:n, d * P:(d + 1) * P] if t < 2 else psum[0:n, 3 if d < 4 else 0,
                                                                                 (d % 4) * P:(d % 4 + 1) * P]
                    last = pe.transpose(o, u_T[:, d, c0:c0 + n], ident)
                last.then_inc(mix_turned, 1)
            for k in range(KD):
                if k == 0:
                    pe.wait_ge(xn_ready, 3)
                if k >= 2:
                    pe.wait_ge(xn_T_ready, k - 1)
                for t, (c0, n) in enumerate(TILES):
                    last = pe.transpose(psum[:, 1 + k % 2, c0:c0 + n], normed[0:n, t, k * P:(k + 1) * P],
                                        ident[0:n, 0:n])
                last.then_inc(xn_turned, 1)
            pe.wait_ge(xn_T_ready, KD)
            for t, (c0, n) in enumerate(TILES):
                for k in range(KD):
                    last = mm(psum[0:n, 4, t * NE:(t + 1) * NE], xn_T[:, k, c0:c0 + n], w_router[:, k],
                              start=k == 0, stop=k == KD - 1)
            last.then_inc(logits_done, 1)
            for k in range(KD):
                if k >= 2:
                    pe.wait_ge(h_T_ready, k - 1)
                for t, (c0, n) in enumerate(TILES):
                    last = pe.transpose(psum[:, 6 + k % 2, c0:c0 + n], tok[0:n, t, k * P:(k + 1) * P],
                                        ident[0:n, 0:n])
                last.then_inc(h_turned, 1)
            pe.wait_ge(chosen_ready, 1)
            before = const("before")
            for t, (_, n) in enumerate(TILES):
                for s in range(t):
                    mm(psum[0:n, 5, t * NE:(t + 1) * NE], ones[:, 0:n], chosen[:, s], start=s == 0, stop=False)
                mm(psum[0:n, 5, t * NE:(t + 1) * NE], before[0:n, 0:n], chosen[0:n, t], start=t == 0, stop=True)
            for t, (_, n) in enumerate(TILES):
                last = mm(psum[:, 5, 3 * NE:4 * NE], ones[0:n, :], chosen[0:n, t], start=t == 0, stop=t == 2)
            last.then_inc(placed, 1)

            pe.wait_ge(gated_ready, 1)
            for t, (c0, n) in enumerate(TILES):
                last = pe.transpose(psum[0:NE, 3, c0:c0 + n], gates[0:n, t], ident[0:n, 0:n])
            last.then_inc(gates_turned, 1)

            def scatter(it, d):
                if d == 0:
                    pe.wait_ge(out_ready, 4 * it + 4)
                    pe.wait_ge(g_T_ready, 2 * it + 2)
                if d >= 2:
                    pe.wait_ge(y_added, KD * it + d - 1)
                for j in range(2):
                    last = mm(psum[:, 6 + d % 2, 0:NT], out_sb[:, j, d * P:(d + 1) * P], g_T[:, j], start=j == 0,
                              stop=j == 1)
                last.then_inc(scattered, 1)

            def gather(it):
                pe.wait_ge(one_hot_ready, it + 1)
                for k in range(KD):
                    for t, (_, n) in enumerate(TILES):
                        last = mm(psum[:, k // 4, (k % 4) * P:(k % 4 + 1) * P], normed[0:n, t, k * P:(k + 1) * P],
                                  one_hot[0:n, t].rearrange("p j c -> p (j c)"), start=t == 0, stop=t == 2)
                last.then_inc(gathered, 1)

            def use(it, u):
                j, part, k, h = UNITS[u]
                if part == "gu":
                    x = x_parts[:, k, j].rearrange("p s c -> p (s c)")
                    if u == 0:
                        pe.wait_ge(x_lo, it + 1)
                    bank, first, last_k, done = 2 * h, k == 0, k == KD - 1, gu_done
                else:
                    f = 2 * k + h
                    if f == 0:
                        pe.wait_ge(act_ready, 2 * it + j + 1)
                        if j == 1:
                            pe.wait_ge(g_T_ready, 2 * it + 4)
                    x = act_parts[:, f].rearrange("p s c -> p (s c)")
                    bank, first, last_k, done = 4, f == 0, f == KD - 1, down_done
                if (j, part, k) in WHOLE:
                    i = u // 2
                    pe.wait_ge(expert_in[i % RING], 16 * (2 * it + i // RING + 1))
                    for n in range(2):
                        c = h * HALF + n * 512
                        last = mm(psum[0:CAP, bank + n], hg[:, f], slot(i % RING)[:, c:c + 512], start=False, stop=False)
                else:
                    s = SPLITS.index(u)
                    hi, lo = stage_hi[s % STAGE], lo_half(u)
                    pe.wait_ge(split_lo, NSPLIT * it + s + 1)
                    for n in range(2):
                        mm(psum[:, bank + n], x, hi[:, n * 512:(n + 1) * 512], start=first, stop=False)
                        last = mm(psum[:, bank + n], x, lo[:, n * 512:(n + 1) * 512], start=False, stop=last_k)
                        if last_k:
                            last.then_inc(done, 1)
                if not last_k:
                    last.then_inc(half_used, 1)

            def turn_hidden(it, j):
                e = 2 * it + j
                if j == 0:
                    pe.wait_ge(y_added, KD * it + KD)
                for m in range(16):
                    if m % 4 == 0:
                        pe.wait_ge(raw_ready, 4 * e + 1 + m // 4)
                    last = mm(psum[:, 6 + m // 8, (m % 8) * CAP:(m % 8 + 1) * CAP], h_raw[:, m * P:(m + 1) * P],
                              const("twin"), start=True, stop=True)
                    if m % 8 == 7:
                        last.then_inc(hidden_turned, 1)

            def pair(it):
                for u in range(NU):
                    if UNITS[u] == (1, "gu", 0, 0):
                        turn_hidden(it, 0)
                    if UNITS[u] == (1, "dn", 0, 0):
                        turn_hidden(it, 1)
                        gather(it + 1)
                        pe.wait_ge(gated_ready, it + 2)
                        pe.wait_ge(out_ready, 4 * it + 6)
                        for j in range(2):
                            for t, (c0, n) in enumerate(TILES):
                                last = pe.transpose(psum[:, 4 + j, c0:c0 + n],
                                                    gated[0:n, t, j].rearrange("p s c -> p (s c)"), ident[0:n, 0:n])
                        last.then_inc(gates_turned, 1)
                    use(it, u)
                    if SCATTER_AFTER <= u < SCATTER_AFTER + KD:
                        scatter(it, u - SCATTER_AFTER)

            pe.wait_ge(pairs_ready, 1)
            gather(0)
            pe.wait_ge(bias_in, 16)
            for n in range(2):
                mm(psum[:, 4 + n], ident[0:NE, :], w_final[0:NE, n * 512:(n + 1) * 512], start=True,
                   stop=True).then_inc(down_done, 1)
            pe.wait_ge(h_T_ready, KD)
            pairs = pe.value_load(pairs_i[0:1, 0:1], min_val=NPAIR, max_val=NPAIR * NPASS)
            with pe.Fori(0, NPASS) as r:
                with pe.If(pairs > r * NPAIR):
                    with pe.Fori(0, NPAIR) as p:
                        pair(r * NPAIR + p)
            for d in range(KD):
                scatter(pairs, d)

            pe.wait_ge(y_added, KD * pairs + KD)
            for t, (c0, n) in enumerate(TILES):
                for d in range(KD):
                    last = pe.transpose(banks(2 * t, 2)[0:n, d * P:(d + 1) * P], y_T[:, d, c0:c0 + n], ident)
                last.then_inc(y_turned, 1)

        @block.scalar
        def _(act_e):
            step = Steps(act_e, act_step)
            A = nc.scalar.activation
            act_e.wait_ge(x_in, 48)
            act_e.wait_ge(consts_in, 16)
            for t, n in enumerate((P, P, 48)):
                step(A(squares[0:n], tok[0:n, t], ACT.Square, accum_out=sumsq[0:n, t:t + 1]))
                step.wait()
            for t, n in enumerate((P, P, 48)):
                A(rms[0:n, t:t + 1], sumsq[0:n, t:t + 1], ACT.Sqrt, bias=const("eps")[0:n], scale=1.0 / D).then_inc(
                    rms_done, 1)
            act_e.wait_ge(params_ready, 2)
            for k in range(KD):
                act_e.wait_ge(x_turned, k + 1)
                A(u_T[:, k, 0:NT], psum[:, 4 + k % 4, 0:NT], ACT.Copy, scale=norm_mix[:, k:k + 1]).then_inc(u_ready, 1)
                A(u_T[:, k, NT:NA], psum[:, 4 + k % 4, 288:304], ACT.Copy, scale=norm_mix[:, k:k + 1]).then_inc(
                    u_ready, 1)
            for n in range(T_YB):
                act_e.wait_ge(tile_done, n + 1)
                ps = psum[:, n % 3]
                if n < K0:
                    if n >= 2:
                        act_e.wait_ge(aux_done, AUX_AT[("v", n - 2)] + 1)
                    last = nc.scalar.copy(v_T[:, n % 2], ps[:, 0:NA])
                elif n < P0:
                    j = n - K0
                    if j >= 2:
                        act_e.wait_ge(roped, j - 1)
                    nc.scalar.copy(rope_y[0:64, j % 2], ps[64:128, 0:NA])
                    nc.scalar.copy(rope_y[64:128, j % 2], ps[0:64, 0:NA])
                    last = nc.scalar.copy(rope_x[:, j % 2], ps[:, 0:NA])
                elif n < G0:
                    g = n - P0
                    nc.scalar.copy(p_ext[:, g, 0:NM], ps[:, NT:NA])
                    nc.scalar.copy(p_s[:, g], ps[:, NPR:NT])
                    last = nc.scalar.copy(p_ext[:, g, NM:], ps[:, 0:NPR])
                elif n < GA0:
                    last = A(z_T[:, n - G0], ps[:, 0:NT], ACT.Silu)
                elif n < GB0:
                    if n == GA0:
                        act_e.wait_ge(aux_took, AUX_AT[("o", 1)] + 1)
                    last = A(gate_a[:, n - GA0], ps[:, 0:NT], ACT.Sigmoid)
                elif n < N_IN:
                    if n == GB0:
                        act_e.wait_ge(aux_done, AUX_AT[("outer", NS - 1)] + 1)
                    last = A(gate_b[:, n - GB0], ps[:, 0:NT], ACT.Sigmoid)
                else:
                    g = n - T_POOL
                    last = A(pooled[:, g], ps[:, 0:NT], ACT.Copy, scale=pool_scale[:, g:g + 1])
                last.then_inc(act_took, 1)
                if n in ROOT_AFTER:
                    i = ROOT_AFTER[n]
                    rows_n = NS if i == 2 else P
                    act_e.wait_ge(spread_ready, i + 1)
                    A(spread[0:rows_n], moments[0:rows_n, :, 1], ACT.Sqrt, bias=const("eps")[0:rows_n]).then_inc(
                        spread_rooted, 1)
            for n in range(T_OUT, T_END):
                act_e.wait_ge(tile_done, n + 1)
                nc.scalar.copy(u_T[:, n - T_OUT, 0:NT], psum[:, n % 3, 0:NT]).then_inc(act_took, 1)
            act_e.wait_ge(ret_out, 16)
            for t, (_, n) in enumerate(TILES):
                act_e.wait_ge(h_ready, t + 1)
                A(z_sq[0:n], tok[0:n, t], ACT.Square, accum_out=sumsq[0:n, t:t + 1]).then_inc(sq_done, 1)
                act_e.wait_ge(sq_done, t + 1)
            for t, (_, n) in enumerate(TILES):
                A(rms[0:n, t:t + 1], sumsq[0:n, t:t + 1], ACT.Sqrt, bias=const("eps")[0:n], scale=1.0 / D).then_inc(
                    rms_done, 1)
            for k in range(KD):
                act_e.wait_ge(xn_turned, k + 1)
                A(xn_T[:, k], psum[:, 1 + k % 2, 0:NT], ACT.Copy, scale=norm_ffn[:, k:k + 1]).then_inc(xn_T_ready, 1)
            act_e.wait_ge(neg_ready, 1)
            act_e.wait_ge(zeroed, 2)
            for t, (_, n) in enumerate(TILES):
                A(expd[0:n, t], logits[0:n, t], ACT.Exp, bias=neg_top[0:n, t:t + 1]).then_inc(exp_ready, 1)

            for k in range(KD):
                act_e.wait_ge(h_turned, k + 1)
                nc.scalar.copy(y_T[:, k], psum[:, 6 + k % 2, 0:NT]).then_inc(h_T_ready, 1)
            act_e.wait_ge(gates_turned, 1)
            act_e.wait_ge(half_used, STAGE)
            A(sumsq[0:1, 0:1], sumsq[0:1, 0:1], ACT.Silu)
            nc.scalar.copy(g_T[0:NE, 1], psum[0:NE, 3, 0:NT]).then_inc(g_T_ready, 2)

            def split(it, *places):
                for i in places:
                    c, h = SPLITS[i] // 2, SPLITS[i] % 2
                    if h == 0:
                        act_e.wait_ge(expert_in[c % RING], 16 * (2 * it + c // RING + 1))
                    wait_staged(act_e, it, i)
                    nc.scalar.copy(stage_hi[i % STAGE][:, :], raw_half(SPLITS[i])).then_inc(split_hi, 1)

            def take_hidden(it, j):
                e = 2 * it + j
                for n in range(4):
                    act_e.wait_ge(gu_done, 4 * e + n + 1)
                    nc.scalar.copy(h_raw[:, n * 512:(n + 1) * 512], psum[:, n]).then_inc(raw_ready, 1)

            def take_down(n, j):
                for b in range(2):
                    act_e.wait_ge(down_done, 2 * n + 3 + b)
                    nc.scalar.copy(out_sb[:, j, b * 512:(b + 1) * 512], psum[:, 4 + b]).then_inc(out_ready, 1)

            def take_tokens(it):
                act_e.wait_ge(gathered, it + 1)
                nc.scalar.copy(x_parts[:, :, :, 0].rearrange("p k j c -> p (k j) c"),
                               banks(0, 2).rearrange("p (k c) -> p k c", c=CAP)).then_inc(x_hi, 1)

            def silu(it, j):
                act_e.wait_ge(gate_clipped, 2 * it + j + 1)
                A(hs[:, :, :], hg[:, :, :], ACT.Silu, scale=ALPHA).then_inc(silu_ready, 1)

            def pair(it):
                split(it, 0, 1)
                take_down(2 * it - 1, 1)
                split(it, *range(2, S_AT[1, "gu", 0] + LEAD))
                take_hidden(it, 0)
                split(it, *range(S_AT[1, "gu", 0] + LEAD, SWIGLU_AT[0] + 2))
                silu(it, 0)
                split(it, *range(SWIGLU_AT[0] + 2, D0_END + LEAD))
                take_down(2 * it, 0)
                split(it, *range(D0_END + LEAD, S_AT[1, "dn", 0] + LEAD))
                take_hidden(it, 1)
                split(it, *range(S_AT[1, "dn", 0] + LEAD, SWIGLU_AT[1] + 2))
                silu(it, 1)
                take_tokens(it + 1)
                act_e.wait_ge(gates_turned, it + 2)
                for j in range(2):
                    nc.scalar.copy(g_T[:, j], psum[:, 4 + j, 0:NT]).then_inc(g_T_ready, 1)
                split(it, *range(SWIGLU_AT[1] + 2, NSPLIT))

            take_tokens(0)
            act_e.wait_ge(pairs_ready, 1)
            pairs = act_e.value_load(pairs_i[0:1, 0:1], min_val=NPAIR, max_val=NPAIR * NPASS)
            with act_e.Fori(0, NPASS) as r:
                with act_e.If(pairs > r * NPAIR):
                    with act_e.Fori(0, NPAIR) as p:
                        pair(r * NPAIR + p)

            take_down(2 * pairs - 1, 1)

            for t, (_, n) in enumerate(TILES):
                act_e.wait_ge(y_taken, t + 1)
                A(out_sq[0:n], normed[0:n, t], ACT.Square, accum_out=sumsq[0:n, t:t + 1]).then_inc(y_sq, 1)
                act_e.wait_ge(y_sq, t + 1)
            for t, (_, n) in enumerate(TILES):
                A(rms[0:n, t:t + 1], sumsq[0:n, t:t + 1], ACT.Sqrt, bias=const("eps")[0:n], scale=1.0 / D).then_inc(
                    y_rms, 1)

        @block.vector
        def _(dve):
            V = nc.vector
            step = Steps(dve, dve_step)

            def aux(a):
                i = AUX_AT[a]
                dve.wait_ge(aux_done, i + 1)
                kind, bank = a[0], AUX_BANKS[a][0]
                ps = banks(bank)
                if kind == "v":
                    c = slice(a[1] * P, (a[1] + 1) * P)
                    V.tensor_copy(v_tok[:, :, c], ps[:, 0:2 * P].rearrange("p (t c) -> p t c", t=2))
                    V.tensor_copy(v_sm[0:NS, c], ps[0:NS, 2 * P:3 * P])
                    last = V.tensor_copy(v_sm[32:32 + NM, c], ps[0:NM, 3 * P:4 * P])
                elif kind == "k":
                    j = a[1]
                    c = slice(j * P, (j + 1) * P)
                    V.tensor_scalar(k_tok[:, :, c], ps[:, 0:2 * P].rearrange("p (t c) -> p t c", t=2),
                                    const("k_dec")[:, j:j + 1], None, ALU.mult)
                    V.tensor_copy(k_sm[0:NS, c], ps[0:NS, 2 * P:3 * P])
                    step(V.tensor_copy(k_sm[32:32 + NM, c], ps[0:NM, 3 * P:4 * P]))
                    step.wait()
                    last = V.tensor_scalar(k_sm[32:32 + NM, c], k_sm[32:32 + NM, c],
                                           const("k_dec_meta")[32:32 + NM, j:j + 1], None, ALU.mult)
                elif kind == "hist":
                    for g, w in enumerate(WINDOWS):
                        rows_g = ps[:, g * P:g * P + NS * PBUF].rearrange("p (b t) -> p b t", b=NS)
                        last = V.tensor_reduce(hist_sum[:, g], rows_g[:, :, PBUF - w + 1:], AX.X, ALU.add)
                elif kind == "s_meta":
                    last = V.tensor_copy(ret_s[:, 0].rearrange("p h v -> p (h v)"), banks(bank, 2))
                elif kind == "score":
                    c = a[1]
                    V.tensor_tensor(qd[:, c], q_T[:, :, c * P:(c + 1) * P],
                                    const("q_dec").rearrange("p (h i) -> p h i", h=H), ALU.mult)
                    last = V.tensor_tensor(scores[:, c].rearrange("p h i -> p (h i)"), ps, const("mask"), ALU.mult)
                elif kind == "s_next":
                    c = a[1]
                    for h in range(H):
                        last = V.scalar_tensor_tensor(ret_s[:, 1 - c, h], ret_s[:, c, h], CHUNK_DEC[h],
                                                      banks(bank, 2)[:, h * DV:(h + 1) * DV], ALU.mult, ALU.add)
                elif kind == "o":
                    group_norm(a[1], P, banks(bank, 2))
                    last = None
                elif kind == "ptok":
                    V.tensor_copy(p_rows[0:PBUF, :], ps[0:PBUF])
                    last = V.tensor_copy(p_rows[32:32 + NS, :], banks(bank + 1)[0:NS])
                elif kind == "outer":
                    b = a[1]
                    dve.wait_ge(state_decayed, b + 1)
                    s = state_s[:, b % 4].rearrange("p h v -> p (h v)")
                    last = V.tensor_tensor(s, s, banks(bank, 2), ALU.add)
                elif kind == "o_turn":
                    group_norm(2, NS, banks(bank, 2))
                    last = None
                elif kind == "z":
                    j = a[1]
                    dve.wait_ge(act_took, GA0)
                    last = V.scalar_tensor_tensor(z_T[:, j], ps[:, 0:NT], gn_w[:, j:j + 1], z_T[:, j], ALU.mult,
                                                  ALU.mult)
                if last is not None:
                    last.then_inc(aux_took, 1)

            def group_norm(i, n, ps):
                for h in range(H):
                    step(V.bn_stats(stats[0:n, h], ps[0:n, h * DV:(h + 1) * DV]))
                step.wait()
                for h in range(H):
                    last = V.bn_aggr(moments[0:n, h], stats[0:n, h])
                last.then_inc(spread_ready, 1)
                dve.wait_ge(spread_rooted, i + 1)
                step(V.reciprocal(spread[0:n], spread[0:n]))
                step.wait()
                for h in range(H):
                    last = V.tensor_scalar(normed[0:n, i, h * DV:(h + 1) * DV], ps[0:n, h * DV:(h + 1) * DV],
                                           moments[0:n, h, 0:1], spread[0:n, h:h + 1], ALU.subtract, ALU.mult)
                last.then_inc(aux_took, 1)

            dve.wait_ge(rms_done, 3)
            dve.wait_ge(params_turned, 1)
            V.tensor_copy(params[:, 0:28], psum[:, 0, 0:28]).then_inc(params_ready, 1)
            V.tensor_copy(params[:, 28:28 + 512], psum[:, 1]).then_inc(params_ready, 1)
            for t, n in enumerate((P, P, 48)):
                step(V.reciprocal(rstd[0:n, t:t + 1], rms[0:n, t:t + 1]))
            step.wait()
            for t, n in enumerate((P, P, 48)):
                V.tensor_scalar(normed[0:n, t], tok[0:n, t], rstd[0:n, t:t + 1], None, ALU.mult).then_inc(x_scaled, 1)

            for n in range(T_OUT):
                if K0 <= n < P0:
                    j = n - K0
                    dve.wait_ge(act_took, n + 1)
                    s = DK ** -0.5 if j < H else 1.0
                    x, y = rope_x[:, j % 2], rope_y[:, j % 2]
                    step(V.scalar_tensor_tensor(x, x, s, const("cos"), ALU.mult, ALU.mult))
                    step(V.scalar_tensor_tensor(y, y, s, const("sin"), ALU.mult, ALU.mult))
                    step.wait()
                    if j < H:
                        V.tensor_tensor(k_T[:, j], x, y, ALU.add).then_inc(roped, 1)
                    else:
                        h = j - H
                        step(V.tensor_tensor(q_s[:, h], x[:, NPR:NT], y[:, NPR:NT], ALU.add))
                        V.tensor_tensor(q_T[:, h], x[:, 0:NT], y[:, 0:NT], ALU.add).then_inc(roped, 1)
                        if h == H - 1:
                            dve.wait_ge(roped, 8)
                elif T_YB <= n < T_YA:
                    d = n - T_YB
                    dve.wait_ge(tile_done, n + 1)
                    dve.wait_ge(act_took, N_IN)
                    V.tensor_tensor(gate_b[:, d], psum[:, n % 3, 0:NT], gate_b[:, d], ALU.mult).then_inc(dve_took, 1)
                elif T_YA <= n:
                    d = n - T_YA
                    dve.wait_ge(tile_done, n + 1)
                    if d == 0:
                        dve.wait_ge(dve_took, T_YA - T_YB)
                    step(V.tensor_tensor(gate_a[:, d], psum[:, n % 3, 0:NT], gate_a[:, d], ALU.mult))
                    step.wait()
                    V.tensor_tensor(gate_a[:, d], gate_a[:, d], gate_b[:, d], ALU.add).then_inc(dve_took, 1)
                for a in AUX_AFTER[n]:
                    aux(a)
                if n == 33:
                    dve.wait_ge(outer_read, NS)
                    V.tensor_copy(hs_T.rearrange("p m b -> p (m b)"), psum[:, 3, 0:8 * NS]).then_inc(o_s_ready, 1)

            for t, (_, n) in enumerate(TILES):
                dve.wait_ge(mix_turned, t + 1)
                if t < 2:
                    V.tensor_tensor(tok[0:n, t], banks((4, 6)[t], 2)[0:n], tok[0:n, t], ALU.add).then_inc(h_ready, 1)
                else:
                    step(V.tensor_tensor(tok[0:n, t, 0:512], psum[0:n, 3], tok[0:n, t, 0:512], ALU.add))
                    step.wait()
                    V.tensor_tensor(tok[0:n, t, 512:], psum[0:n, 0], tok[0:n, t, 512:], ALU.add).then_inc(h_ready, 1)
            dve.wait_ge(rms_done, 6)
            for t, (_, n) in enumerate(TILES):
                step(V.reciprocal(rstd[0:n, t:t + 1], rms[0:n, t:t + 1]))
            step.wait()
            for t, (_, n) in enumerate(TILES):
                V.tensor_scalar(normed[0:n, t], tok[0:n, t], rstd[0:n, t:t + 1], None, ALU.mult).then_inc(xn_ready, 1)

            dve.wait_ge(xn_turned, KD)
            dve.wait_ge(ffn_in, 16)
            dve.wait_ge(xn_ready, 3)
            for t, (_, n) in enumerate(TILES):
                V.tensor_tensor(normed[0:n, t], normed[0:n, t], w_ffn[0:n], ALU.mult).then_inc(ffn_scaled, 1)

            dve.wait_ge(logits_done, 1)
            dve.wait_ge(zeroed, 2)
            for t, (_, n) in enumerate(TILES):
                step(V.tensor_tensor(logits[0:n, t], psum[0:n, 4, t * NE:(t + 1) * NE], b_router[0:n, :], ALU.add))
            step.wait()
            for t, (_, n) in enumerate(TILES):
                step(V.max(top[0:n, t], logits[0:n, t]))
            step.wait()
            for t, (_, n) in enumerate(TILES):
                last = V.tensor_scalar(neg_top[0:n, t:t + 1], top[0:n, t, 0:1], -1.0, None, ALU.mult)
            last.then_inc(neg_ready, 1)
            for t, (_, n) in enumerate(TILES):
                step(V.max_index(top_i[0:n, t], top[0:n, t], logits[0:n, t]))
            step.wait()
            for t, (_, n) in enumerate(TILES):
                step(V.tensor_copy(top_f[0:n, t], top_i[0:n, t]))
            step.wait()
            for t in range(3):
                step(V.tensor_tensor(match[:, 4 * t:4 * t + 4],
                                     const("experts").rearrange("p (a e) -> p a e", a=1).broadcast_to([P, TOPK, NE]),
                                     top_f[:, t, 0:TOPK].rearrange("p (j a) -> p j a", a=1).broadcast_to(
                                         [P, TOPK, NE]), ALU.is_equal))
            step.wait()
            for t in range(3):
                last = V.tensor_reduce(chosen[:, t], match[:, 4 * t:4 * t + 4].rearrange("p j e -> p e j"), AX.X,
                                       ALU.add)
                if t == 2:
                    last.then_inc(chosen_ready, 1)
            dve.wait_ge(exp_ready, 3)
            dve.wait_ge(chosen_ready, 1)
            step(V.tensor_tensor(gates[:, :, :], expd[:, :, :], chosen[:, :, :], ALU.mult))
            step.wait()
            step(V.tensor_reduce(gate_sum, gates[:, :, :], AX.X, ALU.add))
            step.wait()
            step(V.tensor_scalar(gate_sum, gate_sum, 1e-30, None, ALU.max))
            step.wait()
            step(V.reciprocal(gate_rec, gate_sum))
            step.wait()
            V.tensor_tensor(gates[:, :, :], gates[:, :, :],
                            gate_rec.rearrange("p (t a) -> p t a", a=1).broadcast_to([P, 3, NE]),
                            ALU.mult).then_inc(gated_ready, 1)
            dve.wait_ge(gated_ready, 1)
            step(V.tensor_scalar(gates_s[:, :, :], gates[:, :, :], 1.0 / ALPHA, None, ALU.mult))
            step(V.tensor_scalar(place[:, :, 0:NE], chosen[:, :, :], -FAR, FAR, ALU.mult, ALU.add))
            step.wait()
            dve.wait_ge(placed, 1)
            step(V.tensor_tensor(place[:, 0:2, 0:NE], place[:, 0:2, 0:NE],
                                 psum[:, 5, 0:2 * NE].rearrange("p (t e) -> p t e", t=2), ALU.add))
            step(V.tensor_tensor(place[0:NS, 2, 0:NE], place[0:NS, 2, 0:NE], psum[0:NS, 5, 2 * NE:3 * NE], ALU.add))
            step.wait()
            V.tensor_scalar(place[:, :, NE:NE + 2], place[:, :, 0:2], float(CAP), None, ALU.subtract).then_inc(
                place_ready, 1)
            step(V.tensor_reduce(most, psum[0:1, 5, 3 * NE:4 * NE], AX.X, ALU.max))
            step.wait()
            step(V.tensor_scalar(beyond, const("passes")[0:1], most, float(NPAIR), ALU.is_lt, ALU.mult))
            step.wait()
            step(V.tensor_reduce(pairs_f, beyond, AX.X, ALU.add))
            step.wait()
            V.tensor_copy(pairs_i[0:1, 0:1], pairs_f).then_inc(pairs_ready, 1)

            loop = Steps(dve, dve_loop)
            iota = const("iota").rearrange("p (t j c) -> p t j c", t=1, j=1).broadcast_to([P, 3, 2, CAP])

            def bias(e, m0):
                return b_gu[:, bass.ds(e, 1), m0:m0 + KD].rearrange("p a (m c) -> p (a m) c", c=1).broadcast_to(
                    [P, KD, CAP])

            def split(it, *places):
                for i in places:
                    dve.wait_ge(split_hi, NSPLIT * it + i + 1)
                    V.tensor_tensor(lo_half(SPLITS[i]), raw_half(SPLITS[i]), stage_hi[i % STAGE][:, :].bitcast(F32), ALU.subtract).then_inc(split_lo, 1)

            def choose(r, p2):
                dve.wait_ge(place_ready, r + 1)
                V.tensor_tensor(one_hot, iota, place[:, :, bass.ds(p2, 2)].rearrange(
                    "p t (j c) -> p t j c", c=1).broadcast_to([P, 3, 2, CAP]), ALU.is_equal).then_inc(one_hot_ready, 1)

            def take_tokens(it):
                dve.wait_ge(x_hi, it + 1)
                V.tensor_tensor(x_parts[:, :, :, 1].rearrange("p k j c -> p (k j) c"),
                                banks(0, 2).rearrange("p (k c) -> p k c", c=CAP),
                                x_parts[:, :, :, 0].bitcast(F32).rearrange("p k j c -> p (k j) c"),
                                ALU.subtract).then_inc(x_lo, 1)

            def add_scattered(it, tiles):
                for d in tiles:
                    dve.wait_ge(scattered, KD * it + d + 1)
                    V.tensor_tensor(y_T[:, d], y_T[:, d], psum[:, 6 + d % 2, 0:NT], ALU.add).then_inc(y_added, 1)

            def swiglu(it, j, p):
                e, n = 2 * p + j, 2 * it + j
                dve.wait_ge(hidden_turned, 2 * n + 1)
                V.tensor_tensor(hg, psum[:, 6].rearrange("p (m c) -> p m c", m=KD), bias(e, 0),
                                ALU.add).then_inc(hidden_took, 1)
                dve.wait_ge(hidden_took, 2 * n + 1)
                V.tensor_scalar(hg, hg, LIMIT, None, ALU.min).then_inc(gate_clipped, 1)
                split(it, SWIGLU_AT[j])
                dve.wait_ge(hidden_turned, 2 * n + 2)
                V.tensor_tensor(hu, psum[:, 7].rearrange("p (m c) -> p m c", m=KD), bias(e, KD),
                                ALU.add).then_inc(hidden_took, 1)
                dve.wait_ge(hidden_took, 2 * n + 2)
                loop(V.tensor_scalar(hu, hu, LIMIT, -LIMIT, ALU.min, ALU.max))
                split(it, SWIGLU_AT[j] + 1)
                loop.wait()
                dve.wait_ge(silu_ready, n + 1)
                loop(V.scalar_tensor_tensor(hg, hu, 1.0, hs, ALU.add, ALU.mult))
                loop.wait()
                loop(V.tensor_copy(act_parts[:, :, 0], hg))
                loop.wait()
                V.tensor_tensor(act_parts[:, :, 1], hg, act_parts[:, :, 0].bitcast(F32), ALU.subtract).then_inc(
                    act_ready, 1)

            LOOP_STEPS = 6

            def pair(r, p):
                it = r * NPAIR + p
                loop.base, loop.n = it * LOOP_STEPS, 0
                split(it, 0, 1)
                dve.wait_ge(one_hot_ready, it + 1)
                for j in range(2):
                    last = V.tensor_tensor(
                        gated[:, :, j], one_hot[:, :, j].rearrange("p t (s c) -> p t s c", s=1).broadcast_to(
                            [P, 3, 2, CAP]),
                        gates_s[:, :, bass.ds(2 * p + j, 1)].rearrange("p t (s c) -> p t s c", s=1).broadcast_to(
                            [P, 3, 2, CAP]), ALU.mult)
                last.then_inc(gated_ready, 1)
                dve.wait_ge(gated_ready, it + 2)
                choose(r, 2 * p + 2)
                for i in range(2, SWIGLU_AT[0]):
                    split(it, i)
                    if SCATTER_AFTER < i <= SCATTER_AFTER + KD:
                        add_scattered(it, (i - SCATTER_AFTER - 1,))
                swiglu(it, 0, p)
                split(it, *range(SWIGLU_AT[0] + 2, SWIGLU_AT[1]))
                swiglu(it, 1, p)
                take_tokens(it + 1)
                split(it, *range(SWIGLU_AT[1] + 2, NSPLIT))
                assert loop.n == LOOP_STEPS

            choose(0, 0)
            take_tokens(0)
            dve.wait_ge(pairs_ready, 1)
            pairs = dve.value_load(pairs_i[0:1, 0:1], min_val=NPAIR, max_val=NPAIR * NPASS)
            with dve.Fori(0, NPASS) as r:
                with dve.If(pairs > r * NPAIR):
                    with dve.Fori(0, NPAIR) as p:
                        pair(r, p)
                    dve.wait_ge(one_hot_ready, (r + 1) * NPAIR + 1)
                    V.tensor_scalar(place[:, :, :], place[:, :, :], float(CAP), None, ALU.subtract).then_inc(
                        place_ready, 1)
            add_scattered(pairs, range(KD))

            for t, (_, n) in enumerate(TILES):
                dve.wait_ge(y_turned, t + 1)
                V.tensor_copy(normed[0:n, t], banks(2 * t, 2)[0:n]).then_inc(y_taken, 1)
            dve.wait_ge(y_rms, 3)
            for t, (_, n) in enumerate(TILES):
                V.reciprocal(rstd[0:n, t:t + 1], rms[0:n, t:t + 1]).then_inc(y_rstd, 1)
            dve.wait_ge(y_rstd, 3)
            dve.wait_ge(final_in, 16)
            for t, (_, n) in enumerate(TILES):
                V.scalar_tensor_tensor(normed[0:n, t], normed[0:n, t], rstd[0:n, t:t + 1], w_final[0:n], ALU.mult,
                                       ALU.mult).then_inc(y_ready, 1)


_INS = ["x_prompt", "x_sample", "state_ret", "state_pool", "meta_tokens", "norm_mix", "w_in", "ret_gn", "pool_w",
        "pool_scale", "w_ret_branch", "w_pool_branch", "w_out", "norm_ffn", "w_router", "b_router", "w_gate_up",
        "b_gate_up", "w_down", "b_down", "norm_final"]
_OUTS = [(1, NPR, D), (NS, 1, D), (1, 1, H, DK, DV), (1, 1, PBUF, PG * P), (1, NS, H, DK, DV), (1, NS, PBUF, PG * P)]


def kernel(**inputs):
    import numpy as _np
    import concourse.bacc as _bacc
    from concourse.bass_utils import run_bass_kernel_spmd as _run

    nc = _bacc.Bacc("TRN2", target_bir_lowering=False, num_devices=1)
    arrays = {f"in_{n}": _np.ascontiguousarray(inputs[n]) for n in _INS}
    arrays["in_consts"] = constants()
    ins = {n[3:]: nc.dram_tensor(n, a.shape, F32, kind="ExternalInput").ap() for n, a in arrays.items()}
    outs = [nc.dram_tensor(f"out_{i}", s, F32, kind="ExternalOutput").ap() for i, s in enumerate(_OUTS)]
    build(nc, ins, outs)
    r = _run(nc, [arrays], core_ids=[0])
    return tuple(r.results[0][f"out_{i}"] for i in range(len(_OUTS)))
```

```python
from contextlib import ExitStack

import numpy as np

import concourse.bass as bass
from concourse import mybir

F32 = mybir.dt.float32
F32R = mybir.dt.float32r
I32 = mybir.dt.int32
U32 = mybir.dt.uint32
ALU = mybir.AluOpType
ACT = mybir.ActivationFunctionType
AX = mybir.AxisListType

P = 128
D = 1024
KD = D // P
NPR, NS, NM = 256, 8, 16
NT = NPR + NS
NA = NT + NM
H, DK, DV = 4, 128, 256
PG = 4
WINDOWS = (2, 4, 8, 16)
PBUF = 15
NE = 32
TOPK = 4
CAP = 64
NPASS = -(-NT // CAP)
NPAIR = NE // 2
ALPHA, LIMIT = 1.702, 7.0
EPS = 1e-6
PAST = 2048
FAR = 4096.0
SLOT = 2048
RING = 12
STAGE = 8
HALF = SLOT // 2
ORDER = ([(0, "gu", k) for k in range(8)] + [(1, "gu", k) for k in range(2)] + [(0, "dn", k) for k in range(4)]
         + [(1, "gu", k) for k in range(2, 8)] + [(1, "dn", k) for k in range(4)])
NCH = len(ORDER)
UNITS = [(*c, h) for c in ORDER for h in range(2)]
NU = len(UNITS)


def ends_banks(u):
    return UNITS[u][1:3] == ("gu", KD - 1) or UNITS[u][1:] == ("dn", 3, 1)


COUNTED = [u for u in range(NU) if not ends_banks(u)]
SCATTER_AFTER = (3, 5, 6, 8, 9, 11, 12, 14)
LEAD = 4
AT = {(j, part, k): u for u, (j, part, k, h) in enumerate(UNITS) if h == 0}
D0_END = AT[0, "dn", 3] + 2
SWIGLU_AT = (AT[1, "gu", 0] + 4, AT[1, "dn", 0] + 4)

V0, K0, Q0, P0, G0, GA0, GB0 = 0, 8, 12, 16, 20, 28, 36
PROJ = [*range(8, 16), *range(4, 8), *range(0, 4), *range(24, 28), *range(16, 24), *range(28, 36), *range(36, 44)]
N_IN = len(PROJ)
T_POOL, T_YB, T_YA, T_OUT, T_END = 44, 48, 56, 64, 72

AUX_BANKS = {}
AUX_AFTER = {n: [] for n in range(-1, T_END)}


def _aux(after, name, banks):
    AUX_BANKS[name] = banks
    AUX_AFTER[after].append(name)


for _j in range(8):
    _aux(_j + 1, ("v", _j), (4 + _j % 2,))
for _j in range(4):
    _aux(_j + 10, ("k", _j), (4 + _j % 2,))
_aux(9, ("hist",), (6,))
_aux(15, ("s_meta",), (6, 7))
_aux(17, ("score", 0), (4,))
_aux(18, ("score", 1), (5,))
_aux(19, ("s_next", 0), (6, 7))
_aux(20, ("o", 0), (6, 7))
_aux(21, ("s_next", 1), (4, 5))
_aux(22, ("o", 1), (6, 7))
_aux(23, ("ptok",), (4, 5))
for _b in range(NS):
    _aux(24 + _b, ("outer", _b), ((4, 5), (6, 7))[_b % 2])
_aux(34, ("o_turn",), (6, 7))
for _j in range(8):
    _aux(36 + _j, ("z", _j), (4 + _j % 2,))
AUX = [a for n in range(-1, T_END) for a in AUX_AFTER[n]]
AUX_AT = {a: i for i, a in enumerate(AUX)}


def bank_owner(i):
    last = 0
    for j in range(i):
        if set(AUX_BANKS[AUX[j]]) & set(AUX_BANKS[AUX[i]]):
            last = j + 1
    return last


CHUNKS = ([("in", n) for n in range(0, N_IN, 2)] + [("pb", c) for c in range(2)]
          + [("ret", c) for c in range(4)] + [("out", c) for c in range(4)])
MIX_SLOTS = 4
C_PB = N_IN // 2
C_RET, C_OUT = C_PB + 2, C_PB + 6


def last_tile(i):
    kind, c = CHUNKS[i]
    return {"in": c + 1, "pb": T_YB + 4 * c + 3, "ret": T_YA + 2 * c + 1, "out": T_OUT + 2 * c + 1}[kind]


ROOT_AFTER = {21: 0, 23: 1, 35: 2}

CONST = {}
_o = 0
for _n, _w in (("ident", 128), ("before", 128), ("ones", 128), ("twin", CAP), ("iota", CAP), ("experts", NE), ("passes", 8),
               ("cos", NA), ("sin", NA), ("mask", H * P), ("q_dec", H * P), ("k_dec", H), ("k_dec_meta", H),
               ("eps", 1)):
    CONST[_n] = (_o, _w)
    _o += _w
N_CONST = _o + (-_o) % 4


def constants():
    c = np.zeros((P, N_CONST), np.float32)

    def put(name, v):
        o, w = CONST[name]
        c[:, o:o + w] = v

    i = np.arange(P, dtype=np.float32)
    put("ident", np.eye(P))
    put("before", np.triu(np.ones((P, P)), 1))
    put("ones", 1.0)
    put("twin", np.concatenate([np.eye(CAP), np.eye(CAP)]))
    put("iota", np.arange(CAP)[None])
    put("experts", np.arange(NE)[None])
    put("passes", (np.arange(8) * CAP + (np.arange(8) >= NPASS) * 1e6)[None])
    pos = np.concatenate([NM + np.arange(NPR), np.full(NS, PAST), np.arange(NM)]).astype(np.float32)
    inv = np.power(np.float32(10000.0), -np.arange(0, DK, 2, dtype=np.float32) / np.float32(DK)).astype(np.float32)
    ang = (pos[None, :] * np.concatenate([inv, inv])[:, None]).astype(np.float32)
    put("cos", np.cos(ang))
    put("sin", np.sin(ang) * np.where(np.arange(P) < DK // 2, -1.0, 1.0)[:, None])
    g = log_decay()
    diff = i[None, :] - i[:, None]
    mask = [np.where(diff >= 0, np.exp(np.maximum(diff, 0) * g[h]), 0.0) for h in range(H)]
    put("mask", np.concatenate(mask, 1))
    put("q_dec", np.concatenate([np.exp((i + 1) * g[h]) for h in range(H)])[None])
    put("k_dec", np.exp((P - 1 - i)[:, None] * g[None]))
    meta = np.zeros((P, H), np.float32)
    meta[32:32 + NM] = np.exp((NM - 1 - np.arange(NM, dtype=np.float32))[:, None] * g[None])
    put("k_dec_meta", meta)
    put("eps", EPS)
    return c


def log_decay():
    return np.log1p(-np.exp2(np.float32(-5.0) - np.arange(H, dtype=np.float32))).astype(np.float32)


CHUNK_DEC = [float(np.exp(np.float32(P) * g)) for g in log_decay()]
STEP_DEC = [float(np.exp(g)) for g in log_decay()]


def build(nc, ins, outs):
    x_prompt, x_sample, state_ret, state_pool, meta = (
        ins[n] for n in ("x_prompt", "x_sample", "state_ret", "state_pool", "meta_tokens"))
    y_prompt, y_sample, ret_prompt, pool_prompt, ret_sample, pool_sample = outs

    with ExitStack() as ctx:
        def sem(name):
            return ctx.enter_context(nc.semaphore(name))

        mixer_only = ExitStack()

        def sb(name, n, dt=F32, where=ctx):
            return where.enter_context(nc.sbuf_tensor(name, [P, n], dt))

        def msb(name, n):
            return sb(name, n, F32, mixer_only)

        with ExitStack() as twice:
            ring_r = sb("ring_r", RING * SLOT, F32R, twice)
        ring = sb("ring", RING * SLOT)

        def slot(s):
            return ring[:, s * SLOT:(s + 1) * SLOT]

        def raw_half(u):
            o = (u // 2) % RING * SLOT + u % 2 * HALF
            return ring[:, o:o + HALF]

        def lo_half(u):
            o = (u // 2) % RING * SLOT + u % 2 * HALF
            return ring_r[:, o:o + HALF]

        early = [4 * SLOT]

        def in_ring(n):
            o = early[0]
            early[0] += n
            assert early[0] <= 8 * SLOT
            return ring[:, o:o + n]

        state_s = in_ring(4 * H * DV).rearrange("p (s h v) -> p s h v", s=4, h=H)
        k_only = in_ring(2 * H * DK).rearrange("p (s h d) -> p s h d", s=2, h=H)
        rope_x = in_ring(2 * NA).rearrange("p (s t) -> p s t", s=2)
        rope_y = in_ring(2 * NA).rearrange("p (s t) -> p s t", s=2)
        v_T = in_ring(2 * NA).rearrange("p (s t) -> p s t", s=2)
        hist = in_ring(PG * P)
        p_rows = in_ring(PG * P)
        q_s = in_ring(H * NS).rearrange("p (h b) -> p h b", h=H)
        hs_T = in_ring(8 * NS).rearrange("p (m b) -> p m b", m=8)
        p_s = in_ring(PG * NS).rearrange("p (g b) -> p g b", g=PG)
        hist_sum = in_ring(PG * NS).rearrange("p (g b) -> p g b", g=PG)

        consts = sb("consts", N_CONST)

        def const(name):
            o, w = CONST[name]
            return consts[:, o:o + w]

        ident, ones = const("ident"), const("ones")
        z_T = sb("z_T", KD * NT).rearrange("p (k t) -> p k t", k=KD)
        y_T = z_T
        normed = sb("normed", 3 * D).rearrange("p (t d) -> p t d", t=3)
        params = sb("params", 28 + 16 * NE)
        norm_mix, gn_w, pool_scale, norm_ffn = (params[:, a:b] for a, b in ((0, 8), (8, 16), (16, 20), (20, 28)))
        b_gu = params[:, 28:28 + 16 * NE].rearrange("p (e m) -> p e m", e=NE)
        small = sb("small", 128)
        stats = small[:, 0:24].rearrange("p (h s) -> p h s", h=H)
        moments = small[:, 24:32].rearrange("p (h s) -> p h s", h=H)
        spread = small[:, 32:36]
        sumsq, rms, rstd = small[:, 40:44], small[:, 44:47], small[:, 48:51]
        top = small[:, 56:80].rearrange("p (t j) -> p t j", t=3)
        neg_top = small[:, 80:83]
        gate_sum, gate_rec = small[:, 84:87], small[:, 88:91]
        most = small[0:1, 92:93]
        beyond = small[0:1, 96:104]
        pairs_f = small[0:1, 104:105]
        top_i = sb("top_i", 24, U32).rearrange("p (t j) -> p t j", t=3)
        top_f = sb("top_f", 24).rearrange("p (t j) -> p t j", t=3)
        pairs_i = sb("pairs_i", 4, I32)
        route = sb("route", 5 * 3 * NE).rearrange("p (a t e) -> p a t e", a=5, t=3)
        logits, expd, chosen, gates, gates_s = (route[:, a] for a in range(5))
        place = sb("place", 3 * (NE + 2)).rearrange("p (t e) -> p t e", t=3)
        tok = msb("tok", 3 * D).rearrange("p (t d) -> p t d", t=3)
        u_T = msb("u_T", KD * NA).rearrange("p (k t) -> p k t", k=KD)
        xn_T = u_T[:, :, 0:NT]
        qk = msb("qk", H * NT + H * NA)
        q_T = qk[:, 0:H * NT].rearrange("p (h t) -> p h t", h=H)
        k_T = qk[:, H * NT:].rearrange("p (h t) -> p h t", h=H)
        gate_a = qk[:, 0:KD * NT].rearrange("p (k t) -> p k t", k=KD)
        vk = msb("vk", 3 * D + 3 * H * DK)
        v_tok = vk[:, 0:2 * D].rearrange("p (t v) -> p t v", t=2)
        k_tok = vk[:, 2 * D:2 * D + 2 * H * DK].rearrange("p (t d) -> p t d", t=2)
        v_sm = vk[:, 2 * D + 2 * H * DK:3 * D + 2 * H * DK]
        k_sm = vk[:, 3 * D + 2 * H * DK:]
        gate_b = vk[:, 0:KD * NT].rearrange("p (k t) -> p k t", k=KD)
        p_ext_all = msb("p_ext", PG * (NM + NPR))
        p_ext = p_ext_all.rearrange("p (g t) -> p g t", g=PG)
        win = msb("win", 2 * (NM + NPR)).rearrange("p (s t) -> p s t", s=2)
        pooled = msb("pooled", PG * NT).rearrange("p (g t) -> p g t", g=PG)
        rs = msb("rs", 2 * H * DV)
        rows = rs[:, 0:D]
        ret_s = rs.rearrange("p (s h v) -> p s h v", s=2, h=H)
        sc = msb("sc", 2 * H * P)
        scores = sc.rearrange("p (c h i) -> p c h i", c=2, h=H)
        qd_all = msb("qd", 2 * H * P)
        qd = qd_all.rearrange("p (c h i) -> p c h i", c=2, h=H)
        match = qd_all[:, 0:3 * TOPK * NE].rearrange("p (a e) -> p a e", e=NE)
        pool_w = msb("pool_w", PG * P).rearrange("p (g e) -> p g e", g=PG)
        w_router = msb("w_router", KD * NE).rearrange("p (k e) -> p k e", k=KD)
        b_router = msb("b_router", NE)
        squares = qk[:, D:2 * D]
        z_sq = rs[:, 0:D]
        w_ffn = rs[:, D:2 * D]
        mixer_only.close()

        stage_hi = [sb(f"stage_hi{i}", HALF, F32R) for i in range(STAGE)]
        x_parts = sb("x_parts", KD * 2 * P, F32R).rearrange("p (k j s c) -> p k j s c", k=KD, j=2, s=2)
        act_parts = sb("act_parts", KD * P, F32R).rearrange("p (k s c) -> p k s c", k=KD, s=2)
        h_raw = sb("h_raw", 2 * D)
        hg, hu, hs = (sb(n, KD * CAP).rearrange("p (m c) -> p m c", m=KD) for n in ("hg", "hu", "hs"))
        out_sb = sb("out_sb", 2 * D).rearrange("p (j d) -> p j d", j=2)
        one_hot = sb("one_hot", 3 * P).rearrange("p (t j c) -> p t j c", t=3, j=2)
        gated = sb("gated", 6 * P).rearrange("p (t j s c) -> p t j s c", t=3, j=2, s=2)
        w_final = sb("w_final", D)
        g_T = sb("g_T", 2 * NT).rearrange("p (j t) -> p j t", j=2)
        out_sq = h_raw[:, 0:D]

        psum = ctx.enter_context(nc.psum_tensor("psum", [P, 8, 512], F32))

        def banks(a, n=1):
            return psum[:, a:a + n].rearrange("p b c -> p (b c)")

        def h_tok(t):
            return banks((4, 6)[t], 2)

        consts_in, x_in, rows_in, hist_in, misc_in, final_in = (
            sem(n) for n in ("consts_in", "x_in", "rows_in", "hist_in", "misc_in", "final_in"))
        wmix_in = [sem(f"wmix_in{s}") for s in range(MIX_SLOTS)]
        state_in = [sem(f"state_in{s}") for s in range(4)]
        state_out = [sem(f"state_out{s}") for s in range(4)]
        expert_in = [sem(f"expert_in{s}") for s in range(RING)]
        stored, y_out = sem("stored"), sem("y_out")
        cleared, x_scaled, sq_done, rms_done = (
            sem(n) for n in ("cleared", "x_scaled", "sq_done", "rms_done"))
        params_turned, params_ready, x_turned, u_ready = (
            sem(n) for n in ("params_turned", "params_ready", "x_turned", "u_ready"))
        tile_done, act_took, dve_took = sem("tile_done"), sem("act_took"), sem("dve_took")
        aux_done, aux_took, roped = sem("aux_done"), sem("aux_took"), sem("roped")
        pooled_ready, k_only_ready, state_decayed = (
            sem(n) for n in ("pooled_ready", "k_only_ready", "state_decayed"))
        outer_read, o_s_ready, ret_out = sem("outer_read"), sem("o_s_ready"), sem("ret_out")
        spread_ready, spread_rooted = sem("spread_ready"), sem("spread_rooted")
        zeroed = sem("zeroed")
        h_turned, xn_ready = sem("h_turned"), sem("xn_ready")
        logits_done, neg_ready, exp_ready, chosen_ready, placed, pairs_ready, place_ready = (
            sem(n) for n in ("logits_done", "neg_ready", "exp_ready", "chosen_ready", "placed", "pairs_ready",
                             "place_ready"))
        dve_step, act_step, pool_step = sem("dve_step"), sem("act_step"), sem("pool_step")
        dve_loop = sem("dve_loop")
        half_used, split_hi, split_lo = sem("half_used"), sem("split_hi"), sem("split_lo")
        one_hot_ready, gated_ready, gathered, x_hi, x_lo = (
            sem(n) for n in ("one_hot_ready", "gated_ready", "gathered", "x_hi", "x_lo"))
        gu_done, raw_ready, hidden_turned, hidden_took, gate_clipped, silu_ready, act_ready = (
            sem(n) for n in ("gu_done", "raw_ready", "hidden_turned", "hidden_took", "gate_clipped", "silu_ready",
                             "act_ready"))
        down_done, out_ready, gates_turned, g_T_ready, scattered, y_added = (
            sem(n) for n in ("down_done", "out_ready", "gates_turned", "g_T_ready", "scattered", "y_added"))
        bias_in = sem("bias_in")
        ffn_in, b_gu_in, gates_ready = (sem(n) for n in ("ffn_in", "b_gu_in", "gates_ready"))
        y_turned, y_sq, y_rms, y_rstd, y_ready = (
            sem(n) for n in ("y_turned", "y_sq", "y_rms", "y_rstd", "y_ready"))

        class Steps:

            def __init__(self, eng, s):
                self.eng, self.s, self.n, self.base = eng, s, 0, 0

            def __call__(self, ins):
                self.n += 1
                ins.then_inc(self.s, 1)
                return ins

            def wait(self):
                self.eng.wait_ge(self.s, self.n + self.base)

        def wait_taken(eng, n):
            if n < T_YB:
                eng.wait_ge(act_took, n + 1)
            elif n < T_OUT:
                eng.wait_ge(dve_took, n - T_YB + 1)
            else:
                eng.wait_ge(act_took, T_YB + n - T_OUT + 1)

        TILES = ((0, P), (P, P), (2 * P, NS))

        gu_w = ins["w_gate_up"].rearrange("l e (k p) f -> (l e) p k f", p=P)
        dn_w = ins["w_down"].rearrange("l e (k p) f -> (l e) p k f", p=P)

        def wait_used(eng, it, u):
            if u < 0:
                it, u = it - 1, u + NU
            j, part, _, h = UNITS[u]
            if ends_banks(u) and part == "gu":
                eng.wait_ge(gu_done, 4 * (2 * it + j) + 2 * h + 2)
            elif ends_banks(u):
                eng.wait_ge(down_done, 2 * (2 * it + j) + 4)
            else:
                eng.wait_ge(half_used, len(COUNTED) * it + COUNTED.index(u) + 1 + STAGE)

        def load_chunk(sp, p, i):
            j, part, k = ORDER[i]
            e, s = 2 * p + j, i % RING
            if part == "gu":
                src = gu_w[bass.ds(e, 1), :, k, :].rearrange("a p f -> p (a f)")
                sp.dma_start(slot(s), src).then_inc(expert_in[s], 16)
            else:
                src = dn_w[bass.ds(e, 1), :, 2 * k:2 * k + 2, :].rearrange("a p k f -> p (a k) f")
                sp.dma_start(slot(s).rearrange("p (k f) -> p k f", k=2), src).then_inc(expert_in[s], 16)

        block = ctx.enter_context(nc.Block())

        @block.sync
        def _(sp):
            w_in = ins["w_in"].rearrange("l (k p) n -> p (l k) n", p=P)
            w_pb = ins["w_pool_branch"].rearrange("l (k p) n -> p (l k) n", p=P)
            w_ret = ins["w_ret_branch"].rearrange("l (k p) n -> p (l k) n", p=P)
            w_out = ins["w_out"].rearrange("l (k p) n -> p (l k) n", p=P)

            sp.dma_start(tok[:, 0:2, :], x_prompt[0].rearrange("(t p) d -> p t d", p=P)).then_inc(x_in, 16)
            sp.dma_start(consts[:, :], ins["consts"]).then_inc(consts_in, 16)
            sp.wait_ge(cleared, 1)
            sp.dma_start(tok[0:NS, 2, :], x_sample.rearrange("b s d -> (b s) d")).then_inc(x_in, 16)
            sp.dma_start(tok[32:32 + NM, 2, :], meta).then_inc(x_in, 16)

            def mix_chunk(i):
                kind, c = CHUNKS[i]
                s = i % MIX_SLOTS
                if i >= MIX_SLOTS:
                    sp.wait_ge(tile_done, last_tile(i - MIX_SLOTS) + 1)
                dst = slot(8 + s)
                if kind == "in":
                    cols = PROJ[c] * P
                    src = w_in[:, :, cols:cols + 2 * P]
                    dst = dst.rearrange("p (k n) -> p k n", k=KD)
                elif kind == "pb":
                    src = w_pb[:, :, c * 512:c * 512 + 512]
                    dst = dst.rearrange("p (k n) -> p k n", k=PG)
                else:
                    src = (w_ret if kind == "ret" else w_out)[:, :, c * 256:c * 256 + 256]
                    dst = dst.rearrange("p (k n) -> p k n", k=KD)
                sp.dma_start(dst, src).then_inc(wmix_in[s], 16)

            sp.wait_ge(rows_in, 4 * 16)
            for i in range(C_PB):
                mix_chunk(i)
                if MIX_SLOTS + 2 <= i < MIX_SLOTS + 6:
                    load_chunk(sp, 0, i - MIX_SLOTS - 2)
            sp.wait_ge(aux_took, AUX_AT[("o_turn",)] + 1)
            for s in range(4):
                sp.wait_ge(state_out[s], 32)
            sp.wait_ge(stored, 16 * 3)
            for s in range(4, 8):
                load_chunk(sp, 0, s)
            for i in range(C_PB, len(CHUNKS)):
                mix_chunk(i)
            for s in range(MIX_SLOTS):
                sp.wait_ge(tile_done, last_tile(len(CHUNKS) - MIX_SLOTS + s) + 1)
                load_chunk(sp, 0, 8 + s)

            def pair(it, p, first=0):
                for i in range(first, NCH):
                    wait_used(sp, it, 2 * (i - RING) + 1)
                    load_chunk(sp, p, i)

            pair(0, 0, RING)
            with sp.Fori(1, NPAIR) as p:
                pair(p, p)
            sp.wait_ge(pairs_ready, 1)
            pairs = sp.value_load(pairs_i[0:1, 0:1], min_val=NPAIR, max_val=NPAIR * NPASS)
            with sp.Fori(1, NPASS) as r:
                with sp.If(pairs > r * NPAIR):
                    with sp.Fori(0, NPAIR) as p:
                        pair(r * NPAIR + p, p)
            for t, (c0, n) in enumerate(TILES):
                sp.wait_ge(y_ready, t + 1)
                dst = y_sample.rearrange("b s d -> (b s) d") if t == 2 else y_prompt[0, c0:c0 + n, :]
                sp.dma_start(dst, normed[0:n, t, :]).then_inc(y_out, 16)
            sp.wait_ge(y_out, 16 * 3)
            sp.wait_ge(stored, 16 * 3)
            sp.wait_ge(ret_out, 16)
            for s in range(4):
                sp.wait_ge(state_out[s], 32)

        @block.gpsimd
        def _(pool):
            step = Steps(pool, pool_step)
            nc.gpsimd.memset(tok[0:64, 2, :], 0.0).then_inc(cleared, 1)
            for o, name, n in ((0, "norm_mix", 8), (8, "ret_gn", 8), (16, "pool_scale", 4), (20, "norm_ffn", 8)):
                pool.dma_start(rows[o:o + n, 0:P], ins[name].rearrange("l (a p) -> (l a) p", p=P)).then_inc(rows_in, 16)
            bg = ins["b_gate_up"].rearrange("l e (m p) -> (l e m) p", p=P)
            pool.dma_start(rows[:, P:5 * P].rearrange("r (c p) -> r c p", c=4),
                           bg.rearrange("(c r) p -> r c p", r=P)).then_inc(b_gu_in, 16)
            pool.dma_start(hist[0:NS * PBUF, :], state_pool.rearrange("l b t c -> (l b t) c")).then_inc(hist_in, 16)
            for b in range(4):
                pool.dma_start(state_s[:, b], state_ret[0, b].rearrange("h d v -> d h v")).then_inc(state_in[b], 16)
            pool.dma_start(pool_w, ins["pool_w"].rearrange("l g c e -> c (l g) e")).then_inc(misc_in, 16)
            pool.dma_start(w_router, ins["w_router"].rearrange("l (k p) e -> p (l k) e", p=P)).then_inc(misc_in, 16)
            pool.dma_start(b_router[:, :], ins["b_router"].broadcast_to([P, NE])).then_inc(misc_in, 16)
            pool.dma_start(pool_sample[0, :, 0:PBUF - 1, :], state_pool[0, :, 1:PBUF, :]).then_inc(stored, 16)

            def only_k(b):
                if b >= 2:
                    pool.wait_ge(aux_done, AUX_AT[("outer", b - 2)] + 1)
                nc.gpsimd.tensor_scalar(k_only[0:NS, b % 2].rearrange("p h d -> p (h d)"), k_sm[0:NS, :],
                                        ident[0:NS, b:b + 1], None, ALU.mult).then_inc(k_only_ready, 1)

            def decay_state(b):
                pool.wait_ge(state_in[b % 4], 16 * (b // 4 + 1))
                for h in range(H):
                    last = nc.gpsimd.tensor_scalar(state_s[:, b % 4, h], state_s[:, b % 4, h], STEP_DEC[h], None,
                                                   ALU.mult)
                last.then_inc(state_decayed, 1)

            for b in range(4):
                decay_state(b)

            n = NM + NPR
            for g, w in enumerate(WINDOWS):
                pool.wait_ge(act_took, P0 + g + 1)
                src, lag = p_ext[:, g], 1
                for i in range(g + 1):
                    dst = win[:, i % 2]
                    step(nc.gpsimd.tensor_tensor(dst[:, 2 * lag - 1:n], src[:, 2 * lag - 1:n],
                                                 src[:, lag - 1:n - lag], ALU.add))
                    step.wait()
                    src, lag = dst, 2 * lag
                step(nc.gpsimd.tensor_scalar(src[:, NM:n], src[:, NM:n], 1.0 / w, None, ALU.mult))
                pool.wait_ge(aux_took, AUX_AT[("hist",)] + 1)
                step(nc.gpsimd.tensor_tensor(hist_sum[:, g], hist_sum[:, g], p_s[:, g], ALU.add))
                step.wait()
                step(nc.gpsimd.tensor_scalar(hist_sum[:, g], hist_sum[:, g], 1.0 / w, None, ALU.mult))
                step(nc.gpsimd.tensor_tensor(pooled[:, g, 0:NPR], src[:, NM:n], p_ext[:, g, NM:n], ALU.subtract))
                step.wait()
                nc.gpsimd.tensor_tensor(pooled[:, g, NPR:NT], hist_sum[:, g], p_s[:, g],
                                        ALU.subtract).then_inc(pooled_ready, 1)

            only_k(0)
            only_k(1)
            pool.wait_ge(aux_took, AUX_AT[("o", 1)] + 1)
            pool.dma_start(w_ffn, ins["norm_ffn"].broadcast_to([P, D])).then_inc(ffn_in, 16)
            for b in range(NS):
                pool.wait_ge(aux_took, AUX_AT[("outer", b)] + 1)
                pool.dma_start(ret_sample[0, b].rearrange("h d v -> d h v"), state_s[:, b % 4]).then_inc(
                    state_out[b % 4], 16)
                if b + 2 < NS:
                    only_k(b + 2)
                if 1 <= b <= 4:
                    s = b - 1
                    pool.wait_ge(state_out[s], 16)
                    pool.wait_ge(outer_read, s + 1)
                    pool.dma_start(state_s[:, s], state_ret[0, s + 4].rearrange("h d v -> d h v")).then_inc(
                        state_in[s], 16)
                if 2 <= b <= 5:
                    decay_state(b + 2)
            pool.dma_start(ret_prompt[0, 0].rearrange("h d v -> d h v"), ret_s[:, 0]).then_inc(ret_out, 16)
            pool.dma_start(pool_prompt[0, 0], p_rows[0:PBUF, :]).then_inc(stored, 16)
            pool.dma_start(pool_sample[0, :, PBUF - 1, :], p_rows[32:32 + NS, :]).then_inc(stored, 16)
            nc.gpsimd.memset(route[:, :, :, :], 0.0).then_inc(zeroed, 1)
            nc.gpsimd.memset(top_f[:, :, :], float(NE)).then_inc(zeroed, 1)
            pool.wait_ge(chosen_ready, 1)
            pool.wait_ge(xn_ready, 4)
            pool.dma_start(w_final[0:NE, :], ins["b_down"].rearrange("l e d -> (l e) d")).then_inc(bias_in, 16)
            nc.gpsimd.memset(g_T[:, :, :], 0.0).then_inc(half_used, STAGE)
            nc.gpsimd.memset(out_sb[:, 0, :], 0.0).then_inc(out_ready, 2)
            pool.wait_ge(down_done, 2)
            pool.dma_start(w_final[:, :], ins["norm_final"].rearrange("(a d) -> a d", a=1).broadcast_to([P, D])).then_inc(
                final_in, 16)

        @block.tensor
        def _(pe):
            mm = pe.matmul

            def aux(a):
                i = AUX_AT[a]
                if bank_owner(i):
                    pe.wait_ge(aux_took, bank_owner(i))
                kind, bank = a[0], AUX_BANKS[a][0]
                if kind == "v":
                    j = a[1]
                    pe.wait_ge(act_took, V0 + j + 1)
                    src = v_T[:, j % 2]
                    pe.transpose(banks(bank)[:, 0:P], src[:, 0:P], ident)
                    pe.transpose(banks(bank)[:, P:2 * P], src[:, P:2 * P], ident)
                    pe.transpose(banks(bank)[0:NS, 2 * P:3 * P], src[:, NPR:NT], ident)
                    last = pe.transpose(banks(bank)[0:NM, 3 * P:4 * P], src[:, NT:NA], ident)
                elif kind == "k":
                    j = a[1]
                    pe.wait_ge(roped, j + 1)
                    src = k_T[:, j]
                    pe.transpose(banks(bank)[:, 0:P], src[:, 0:P], ident)
                    pe.transpose(banks(bank)[:, P:2 * P], src[:, P:2 * P], ident)
                    pe.transpose(banks(bank)[0:NS, 2 * P:3 * P], src[:, NPR:NT], ident)
                    last = pe.transpose(banks(bank)[0:NM, 3 * P:4 * P], src[:, NT:NA], ident)
                elif kind == "hist":
                    pe.wait_ge(hist_in, 16)
                    n = NS * PBUF
                    for g in range(PG):
                        last = pe.transpose(banks(bank)[:, g * P:g * P + n], hist[0:n, g * P:(g + 1) * P],
                                            ident[0:n, 0:n])
                elif kind == "s_meta":
                    pe.wait_ge(aux_took, AUX_AT[("k", 3)] + 1)
                    for h in range(H):
                        last = mm(banks(bank, 2)[:, h * DV:(h + 1) * DV], k_sm[32:32 + NM, h * DK:(h + 1) * DK],
                                  v_sm[32:32 + NM, h * DV:(h + 1) * DV], start=True, stop=True)
                elif kind == "score":
                    c = a[1]
                    pe.wait_ge(roped, 8)
                    for h in range(H):
                        last = mm(banks(bank)[:, h * P:(h + 1) * P], k_T[:, h, c * P:(c + 1) * P],
                                  q_T[:, h, c * P:(c + 1) * P], start=True, stop=True)
                elif kind == "s_next":
                    c = a[1]
                    for h in range(H):
                        last = mm(banks(bank, 2)[:, h * DV:(h + 1) * DV], k_tok[:, c, h * DK:(h + 1) * DK],
                                  v_tok[:, c, h * DV:(h + 1) * DV], start=True, stop=True)
                elif kind == "o":
                    c = a[1]
                    before = ("s_meta",) if c == 0 else ("s_next", 0)
                    pe.wait_ge(aux_took, max(AUX_AT[("score", c)], AUX_AT[before]) + 1)
                    for h in range(H):
                        o = banks(bank, 2)[:, h * DV:(h + 1) * DV]
                        mm(o, scores[:, c, h], v_tok[:, c, h * DV:(h + 1) * DV], start=True, stop=False)
                        last = mm(o, qd[:, c, h], ret_s[:, c, h], start=False, stop=True)
                elif kind == "ptok":
                    pe.wait_ge(act_took, P0 + PG)
                    for g in range(PG):
                        pe.transpose(banks(bank)[0:PBUF, g * P:(g + 1) * P], p_ext[:, g, NM + NPR - PBUF:], ident)
                    for g in range(PG):
                        last = pe.transpose(banks(bank + 1)[0:NS, g * P:(g + 1) * P], p_s[:, g], ident)
                elif kind == "outer":
                    b = a[1]
                    pe.wait_ge(k_only_ready, b + 1)
                    for h in range(H):
                        last = mm(banks(bank, 2)[:, h * DV:(h + 1) * DV], k_only[0:NS, b % 2, h],
                                  v_sm[0:NS, h * DV:(h + 1) * DV], start=True, stop=True)
                elif kind == "o_turn":
                    pe.wait_ge(o_s_ready, 1)
                    for m in range(8):
                        last = pe.transpose(banks(bank, 2)[0:NS, m * P:(m + 1) * P], hs_T[:, m], ident)
                elif kind == "z":
                    j = a[1]
                    pe.wait_ge(aux_took, AUX_AT[("o_turn",)] + 1)
                    for t, (c0, n) in enumerate(TILES):
                        last = pe.transpose(banks(bank)[:, c0:c0 + n], normed[0:n, t, j * P:(j + 1) * P],
                                            ident[0:n, 0:n])
                last.then_inc(aux_done, 1)

            def read_state(b):
                if b == 0:
                    pe.wait_ge(params_ready, 2)
                pe.wait_ge(aux_took, AUX_AT[("outer", b)] + 1)
                for h in range(H):
                    for v in range(2):
                        m = 2 * h + v
                        last = mm(psum[:, 3, m * NS + b:m * NS + b + 1], state_s[:, b % 4, h, v * P:(v + 1) * P],
                                  q_s[:, h, b:b + 1], start=True, stop=True)
                last.then_inc(outer_read, 1)

            pe.wait_ge(consts_in, 16)
            pe.wait_ge(rows_in, 4 * 16)
            pe.transpose(psum[:, 0, 0:28], rows[0:28, 0:P], ident[0:28, 0:28]).then_inc(params_turned, 1)
            for k in range(KD):
                if k == 0:
                    pe.wait_ge(x_scaled, 3)
                if k >= 4:
                    pe.wait_ge(u_ready, 2 * (k - 3))
                for t, n in enumerate((P, P, 48)):
                    last = pe.transpose(psum[:, 4 + k % 4, t * P:t * P + n], normed[0:n, t, k * P:(k + 1) * P],
                                        ident[0:n, 0:n])
                last.then_inc(x_turned, 1)
            pe.wait_ge(b_gu_in, 16)
            for c in range(4):
                last = pe.transpose(psum[:, 3, c * P:(c + 1) * P], rows[:, (1 + c) * P:(2 + c) * P], ident)
            last.then_inc(params_turned, 1)
            pe.wait_ge(u_ready, 2 * KD)

            for n in range(T_END):
                if n >= 3:
                    wait_taken(pe, n - 3)
                o = psum[:, n % 3]
                if n < N_IN:
                    i, width = n // 2, (NA if n < G0 else NT)
                    w = slot(8 + i % MIX_SLOTS).rearrange("p (k n) -> p k n", k=KD)
                    cols = (n % 2) * P
                    x, nk = u_T, KD
                elif n < T_YB:
                    width, nk = NT, 1
                    if n == T_POOL:
                        pe.wait_ge(misc_in, 3 * 16)
                    g = n - T_POOL
                    pe.wait_ge(pooled_ready, g + 1)
                    mm(o[:, 0:NT], pool_w[:, g], pooled[:, g], start=True, stop=True).then_inc(tile_done, 1)
                    continue
                elif n < T_YA:
                    d = n - T_YB
                    i, cols, x, width, nk = C_PB + d // 4, (d % 4) * P, pooled, NT, PG
                    w = slot(8 + i % MIX_SLOTS).rearrange("p (k n) -> p k n", k=PG)
                    if d == 0:
                        pe.wait_ge(act_took, T_YB)
                else:
                    d = n - (T_YA if n < T_OUT else T_OUT)
                    i = (C_RET if n < T_OUT else C_OUT) + d // 2
                    cols, width, nk = (d % 2) * P, NT, KD
                    x = z_T if n < T_OUT else gate_a
                    w = slot(8 + i % MIX_SLOTS).rearrange("p (k n) -> p k n", k=KD)
                    if n == T_YA:
                        pe.wait_ge(aux_took, AUX_AT[("z", 7)] + 1)
                    if n == T_OUT:
                        pe.wait_ge(dve_took, T_OUT - T_YB)
                pe.wait_ge(wmix_in[i % MIX_SLOTS], 16 * (i // MIX_SLOTS + 1))
                for k in range(nk):
                    last = mm(o[:, 0:width], w[:, k, cols:cols + P], x[:, k, 0:width], start=k == 0, stop=k == nk - 1)
                    if n >= T_OUT and k == 0:
                        for t, (c0, m) in enumerate(TILES):
                            mm(o[:, c0:c0 + m], tok[0:m, t, d * P:(d + 1) * P], ident[0:m, 0:m], start=False,
                               stop=False)
                last.then_inc(tile_done, 1)
                for a in AUX_AFTER[n]:
                    aux(a)
                if 25 <= n < 25 + NS:
                    read_state(n - 25)

            for t, (c0, n) in enumerate(TILES):
                bank = (4, 6, 3)[t]
                if t == 0:
                    wait_taken(pe, T_END - 1)
                for d in range(KD):
                    o = banks(bank, 2)[0:n, d * P:(d + 1) * P] if t < 2 else psum[0:n, 3 if d < 4 else 0,
                                                                                 (d % 4) * P:(d % 4 + 1) * P]
                    last = pe.transpose(o, y_T[:, d, c0:c0 + n], ident)
                last.then_inc(h_turned, 1)
            pe.wait_ge(dve_took, T_END - T_YB)
            for t, (c0, n) in enumerate(TILES):
                for k in range(KD):
                    last = mm(psum[0:n, 1, t * NE:(t + 1) * NE], xn_T[:, k, c0:c0 + n], w_router[:, k],
                              start=k == 0, stop=k == KD - 1)
            last.then_inc(logits_done, 1)
            pe.wait_ge(chosen_ready, 1)
            before = const("before")
            for t, (_, n) in enumerate(TILES):
                for s in range(t):
                    mm(psum[0:n, 2, t * NE:(t + 1) * NE], ones[:, 0:n], chosen[:, s], start=s == 0, stop=False)
                mm(psum[0:n, 2, t * NE:(t + 1) * NE], before[0:n, 0:n], chosen[0:n, t], start=t == 0, stop=True)
            for t, (_, n) in enumerate(TILES):
                last = mm(psum[:, 2, 3 * NE:4 * NE], ones[0:n, :], chosen[0:n, t], start=t == 0, stop=t == 2)
            last.then_inc(placed, 1)

            pe.wait_ge(gates_ready, 1)
            for t, (c0, n) in enumerate(TILES):
                last = pe.transpose(psum[0:NE, 3, c0:c0 + n], gates[0:n, t], ident[0:n, 0:n])
            last.then_inc(gates_turned, 1)

            def scatter(it, d):
                if d == 0:
                    pe.wait_ge(out_ready, 4 * it + 4)
                    pe.wait_ge(g_T_ready, 2 * it + 2)
                if d >= 2:
                    pe.wait_ge(y_added, KD * it + d - 1)
                for j in range(2):
                    last = mm(psum[:, 6 + d % 2, 0:NT], out_sb[:, j, d * P:(d + 1) * P], g_T[:, j], start=j == 0,
                              stop=j == 1)
                last.then_inc(scattered, 1)

            def gather(it):
                pe.wait_ge(one_hot_ready, it + 1)
                for k in range(KD):
                    for t, (_, n) in enumerate(TILES):
                        last = mm(psum[:, k // 4, (k % 4) * P:(k % 4 + 1) * P], normed[0:n, t, k * P:(k + 1) * P],
                                  one_hot[0:n, t].rearrange("p j c -> p (j c)"), start=t == 0, stop=t == 2)
                last.then_inc(gathered, 1)

            def use(it, u):
                j, part, k, h = UNITS[u]
                if part == "gu":
                    x = x_parts[:, k, j].rearrange("p s c -> p (s c)")
                    if u == 0:
                        pe.wait_ge(x_lo, it + 1)
                    bank, first, last_k, done = 2 * h, k == 0, k == KD - 1, gu_done
                else:
                    f = 2 * k + h
                    if f == 0:
                        pe.wait_ge(act_ready, 2 * it + j + 1)
                        if j == 1:
                            pe.wait_ge(g_T_ready, 2 * it + 4)
                    x = act_parts[:, f].rearrange("p s c -> p (s c)")
                    bank, first, last_k, done = 4, f == 0, f == KD - 1, down_done
                hi, lo = stage_hi[u % STAGE], lo_half(u)
                pe.wait_ge(split_lo, NU * it + u + 1)
                for n in range(2):
                    mm(psum[:, bank + n], x, hi[:, n * 512:(n + 1) * 512], start=first, stop=False)
                    last = mm(psum[:, bank + n], x, lo[:, n * 512:(n + 1) * 512], start=False, stop=last_k)
                    if last_k:
                        last.then_inc(done, 1)
                if not last_k:
                    last.then_inc(half_used, 1)

            def turn_hidden(it, j):
                e = 2 * it + j
                if j == 0:
                    pe.wait_ge(y_added, KD * it + KD)
                for m in range(16):
                    if m % 4 == 0:
                        pe.wait_ge(raw_ready, 4 * e + 1 + m // 4)
                    last = mm(psum[:, 6 + m // 8, (m % 8) * CAP:(m % 8 + 1) * CAP], h_raw[:, m * P:(m + 1) * P],
                              const("twin"), start=True, stop=True)
                    if m % 8 == 7:
                        last.then_inc(hidden_turned, 1)

            def pair(it):
                for u in range(NU):
                    if UNITS[u] == (1, "gu", 0, 0):
                        turn_hidden(it, 0)
                    if UNITS[u] == (1, "dn", 0, 0):
                        turn_hidden(it, 1)
                        pe.wait_ge(gated_ready, it + 1)
                        pe.wait_ge(out_ready, 4 * it + 6)
                        for j in range(2):
                            for t, (c0, n) in enumerate(TILES):
                                last = pe.transpose(psum[:, 4 + j, c0:c0 + n],
                                                    gated[0:n, t, j].rearrange("p s c -> p (s c)"), ident[0:n, 0:n])
                        last.then_inc(gates_turned, 1)
                        gather(it + 1)
                    use(it, u)
                    if u in SCATTER_AFTER:
                        scatter(it, SCATTER_AFTER.index(u))

            pe.wait_ge(pairs_ready, 1)
            gather(0)
            pe.wait_ge(bias_in, 16)
            for n in range(2):
                mm(psum[:, 4 + n], ident[0:NE, :], w_final[0:NE, n * 512:(n + 1) * 512], start=True,
                   stop=True).then_inc(down_done, 1)
            pe.wait_ge(g_T_ready, 2)
            pairs = pe.value_load(pairs_i[0:1, 0:1], min_val=NPAIR, max_val=NPAIR * NPASS)
            with pe.Fori(0, NPASS) as r:
                with pe.If(pairs > r * NPAIR):
                    with pe.Fori(0, NPAIR) as p:
                        pair(r * NPAIR + p)
            for d in range(KD):
                scatter(pairs, d)

            pe.wait_ge(y_added, KD * pairs + KD)
            for t, (c0, n) in enumerate(TILES):
                for d in range(KD):
                    last = pe.transpose(banks(2 * t, 2)[0:n, d * P:(d + 1) * P], y_T[:, d, c0:c0 + n], ident)
                last.then_inc(y_turned, 1)

        @block.scalar
        def _(act_e):
            step = Steps(act_e, act_step)
            A = nc.scalar.activation
            act_e.wait_ge(x_in, 48)
            for t, n in enumerate((P, P, 48)):
                step(A(squares[0:n], tok[0:n, t], ACT.Square, accum_out=sumsq[0:n, t:t + 1]))
                step.wait()
            act_e.wait_ge(consts_in, 16)
            for t, n in enumerate((P, P, 48)):
                A(rms[0:n, t:t + 1], sumsq[0:n, t:t + 1], ACT.Sqrt, bias=const("eps")[0:n], scale=1.0 / D).then_inc(
                    rms_done, 1)
            act_e.wait_ge(params_ready, 1)
            for k in range(KD):
                act_e.wait_ge(x_turned, k + 1)
                A(u_T[:, k, 0:NT], psum[:, 4 + k % 4, 0:NT], ACT.Copy, scale=norm_mix[:, k:k + 1]).then_inc(u_ready, 1)
                A(u_T[:, k, NT:NA], psum[:, 4 + k % 4, 288:304], ACT.Copy, scale=norm_mix[:, k:k + 1]).then_inc(
                    u_ready, 1)
            for n in range(T_YB):
                act_e.wait_ge(tile_done, n + 1)
                ps = psum[:, n % 3]
                if n < K0:
                    if n >= 2:
                        act_e.wait_ge(aux_done, AUX_AT[("v", n - 2)] + 1)
                    last = nc.scalar.copy(v_T[:, n % 2], ps[:, 0:NA])
                elif n < P0:
                    j = n - K0
                    if j >= 2:
                        act_e.wait_ge(roped, j - 1)
                    nc.scalar.copy(rope_y[0:64, j % 2], ps[64:128, 0:NA])
                    nc.scalar.copy(rope_y[64:128, j % 2], ps[0:64, 0:NA])
                    last = nc.scalar.copy(rope_x[:, j % 2], ps[:, 0:NA])
                elif n < G0:
                    g = n - P0
                    nc.scalar.copy(p_ext[:, g, 0:NM], ps[:, NT:NA])
                    nc.scalar.copy(p_s[:, g], ps[:, NPR:NT])
                    last = nc.scalar.copy(p_ext[:, g, NM:], ps[:, 0:NPR])
                elif n < GA0:
                    last = A(z_T[:, n - G0], ps[:, 0:NT], ACT.Silu)
                elif n < GB0:
                    if n == GA0:
                        act_e.wait_ge(aux_took, AUX_AT[("o", 1)] + 1)
                    last = A(gate_a[:, n - GA0], ps[:, 0:NT], ACT.Sigmoid)
                elif n < N_IN:
                    if n == GB0:
                        act_e.wait_ge(aux_done, AUX_AT[("outer", NS - 1)] + 1)
                    last = A(gate_b[:, n - GB0], ps[:, 0:NT], ACT.Sigmoid)
                else:
                    g = n - T_POOL
                    last = A(pooled[:, g], ps[:, 0:NT], ACT.Copy, scale=pool_scale[:, g:g + 1])
                last.then_inc(act_took, 1)
                if n in ROOT_AFTER:
                    i = ROOT_AFTER[n]
                    rows_n = NS if i == 2 else P
                    act_e.wait_ge(spread_ready, i + 1)
                    A(spread[0:rows_n], moments[0:rows_n, :, 1], ACT.Sqrt, bias=const("eps")[0:rows_n]).then_inc(
                        spread_rooted, 1)
            for n in range(T_OUT, T_END):
                act_e.wait_ge(tile_done, n + 1)
                nc.scalar.copy(y_T[:, n - T_OUT], psum[:, n % 3, 0:NT]).then_inc(act_took, 1)
            act_e.wait_ge(ret_out, 16)
            for t, (_, n) in enumerate(TILES):
                act_e.wait_ge(h_turned, t + 1)
                if t:
                    act_e.wait_ge(sq_done, t)
                if t < 2:
                    A(z_sq[0:n], h_tok(t), ACT.Square, accum_out=sumsq[0:n, t:t + 1]).then_inc(sq_done, 1)
                else:
                    A(z_sq[0:n, 0:512], psum[0:n, 3], ACT.Square, accum_out=sumsq[0:n, 2:3]).then_inc(sq_done, 1)
                    A(z_sq[0:n, 512:], psum[0:n, 0], ACT.Square, accum_out=sumsq[0:n, 3:4]).then_inc(sq_done, 1)
            act_e.wait_ge(sq_done, 4)
            A(sumsq[0:NS, 2:3], sumsq[0:NS, 2:3], ACT.Identity, bias=sumsq[0:NS, 3:4]).then_inc(sq_done, 1)
            act_e.wait_ge(sq_done, 5)
            for t, (_, n) in enumerate(TILES):
                A(rms[0:n, t:t + 1], sumsq[0:n, t:t + 1], ACT.Sqrt, bias=const("eps")[0:n], scale=1.0 / D).then_inc(
                    rms_done, 1)
            act_e.wait_ge(neg_ready, 1)
            act_e.wait_ge(zeroed, 2)
            for t, (_, n) in enumerate(TILES):
                A(expd[0:n, t], logits[0:n, t], ACT.Exp, bias=neg_top[0:n, t:t + 1]).then_inc(exp_ready, 1)

            act_e.wait_ge(gates_turned, 1)
            act_e.wait_ge(half_used, STAGE)
            A(sumsq[0:1, 0:1], sumsq[0:1, 0:1], ACT.Silu)
            nc.scalar.copy(g_T[0:NE, 1], psum[0:NE, 3, 0:NT]).then_inc(g_T_ready, 2)

            def split(it, *units):
                for u in units:
                    c = u // 2
                    if u % 2 == 0:
                        act_e.wait_ge(expert_in[c % RING], 16 * (2 * it + c // RING + 1))
                    wait_used(act_e, it, u - STAGE)
                    nc.scalar.copy(stage_hi[u % STAGE][:, :], raw_half(u)).then_inc(split_hi, 1)

            def take_hidden(it, j):
                e = 2 * it + j
                for n in range(4):
                    act_e.wait_ge(gu_done, 4 * e + n + 1)
                    nc.scalar.copy(h_raw[:, n * 512:(n + 1) * 512], psum[:, n]).then_inc(raw_ready, 1)

            def take_down(n, j):
                for b in range(2):
                    act_e.wait_ge(down_done, 2 * n + 3 + b)
                    nc.scalar.copy(out_sb[:, j, b * 512:(b + 1) * 512], psum[:, 4 + b]).then_inc(out_ready, 1)

            def take_tokens(it):
                act_e.wait_ge(gathered, it + 1)
                nc.scalar.copy(x_parts[:, :, :, 0].rearrange("p k j c -> p (k j) c"),
                               banks(0, 2).rearrange("p (k c) -> p k c", c=CAP)).then_inc(x_hi, 1)

            def silu(it, j):
                act_e.wait_ge(gate_clipped, 2 * it + j + 1)
                A(hs[:, :, :], hg[:, :, :], ACT.Silu, scale=ALPHA).then_inc(silu_ready, 1)

            def gate(it, p):
                act_e.wait_ge(one_hot_ready, it + 1)
                for t in range(3):
                    for j in range(2):
                        last = A(gated[:, t, j], one_hot[:, t, j].rearrange("p (s c) -> p s c", s=1).broadcast_to(
                            [P, 2, CAP]), ACT.Copy, scale=gates_s[:, t, bass.ds(2 * p + j, 1)])
                last.then_inc(gated_ready, 1)

            def pair(r, p):
                it = r * NPAIR + p
                split(it, 0, 1, 2, 3)
                take_down(2 * it - 1, 1)
                split(it, 4, 5)
                gate(it, p)
                split(it, *range(6, AT[1, "gu", 0] + LEAD))
                take_hidden(it, 0)
                split(it, *range(AT[1, "gu", 0] + LEAD, SWIGLU_AT[0] + 2))
                silu(it, 0)
                split(it, *range(SWIGLU_AT[0] + 2, D0_END + LEAD))
                take_down(2 * it, 0)
                split(it, *range(D0_END + LEAD, AT[1, "dn", 0] + LEAD))
                take_hidden(it, 1)
                split(it, *range(AT[1, "dn", 0] + LEAD, SWIGLU_AT[1] + 2))
                silu(it, 1)
                act_e.wait_ge(gates_turned, it + 2)
                for j in range(2):
                    nc.scalar.copy(g_T[:, j], psum[:, 4 + j, 0:NT]).then_inc(g_T_ready, 1)
                split(it, *range(SWIGLU_AT[1] + 2, NU))
                take_tokens(it + 1)

            take_tokens(0)
            act_e.wait_ge(pairs_ready, 1)
            pairs = act_e.value_load(pairs_i[0:1, 0:1], min_val=NPAIR, max_val=NPAIR * NPASS)
            with act_e.Fori(0, NPASS) as r:
                with act_e.If(pairs > r * NPAIR):
                    with act_e.Fori(0, NPAIR) as p:
                        pair(r, p)

            take_down(2 * pairs - 1, 1)

            for t, (_, n) in enumerate(TILES):
                act_e.wait_ge(y_turned, t + 1)
                A(out_sq[0:n], banks(2 * t, 2)[0:n], ACT.Square, accum_out=sumsq[0:n, t:t + 1]).then_inc(y_sq, 1)
                act_e.wait_ge(y_sq, t + 1)
            for t, (_, n) in enumerate(TILES):
                A(rms[0:n, t:t + 1], sumsq[0:n, t:t + 1], ACT.Sqrt, bias=const("eps")[0:n], scale=1.0 / D).then_inc(
                    y_rms, 1)

        @block.vector
        def _(dve):
            V = nc.vector
            step = Steps(dve, dve_step)

            def aux(a):
                i = AUX_AT[a]
                dve.wait_ge(aux_done, i + 1)
                kind, bank = a[0], AUX_BANKS[a][0]
                ps = banks(bank)
                if kind == "v":
                    c = slice(a[1] * P, (a[1] + 1) * P)
                    V.tensor_copy(v_tok[:, :, c], ps[:, 0:2 * P].rearrange("p (t c) -> p t c", t=2))
                    V.tensor_copy(v_sm[0:NS, c], ps[0:NS, 2 * P:3 * P])
                    last = V.tensor_copy(v_sm[32:32 + NM, c], ps[0:NM, 3 * P:4 * P])
                elif kind == "k":
                    j = a[1]
                    c = slice(j * P, (j + 1) * P)
                    V.tensor_scalar(k_tok[:, :, c], ps[:, 0:2 * P].rearrange("p (t c) -> p t c", t=2),
                                    const("k_dec")[:, j:j + 1], None, ALU.mult)
                    V.tensor_copy(k_sm[0:NS, c], ps[0:NS, 2 * P:3 * P])
                    step(V.tensor_copy(k_sm[32:32 + NM, c], ps[0:NM, 3 * P:4 * P]))
                    step.wait()
                    last = V.tensor_scalar(k_sm[32:32 + NM, c], k_sm[32:32 + NM, c],
                                           const("k_dec_meta")[32:32 + NM, j:j + 1], None, ALU.mult)
                elif kind == "hist":
                    for g, w in enumerate(WINDOWS):
                        rows_g = ps[:, g * P:g * P + NS * PBUF].rearrange("p (b t) -> p b t", b=NS)
                        last = V.tensor_reduce(hist_sum[:, g], rows_g[:, :, PBUF - w + 1:], AX.X, ALU.add)
                elif kind == "s_meta":
                    last = V.tensor_copy(ret_s[:, 0].rearrange("p h v -> p (h v)"), banks(bank, 2))
                elif kind == "score":
                    c = a[1]
                    V.tensor_tensor(qd[:, c], q_T[:, :, c * P:(c + 1) * P],
                                    const("q_dec").rearrange("p (h i) -> p h i", h=H), ALU.mult)
                    last = V.tensor_tensor(scores[:, c].rearrange("p h i -> p (h i)"), ps, const("mask"), ALU.mult)
                elif kind == "s_next":
                    c = a[1]
                    for h in range(H):
                        last = V.scalar_tensor_tensor(ret_s[:, 1 - c, h], ret_s[:, c, h], CHUNK_DEC[h],
                                                      banks(bank, 2)[:, h * DV:(h + 1) * DV], ALU.mult, ALU.add)
                elif kind == "o":
                    group_norm(a[1], P, banks(bank, 2))
                    last = None
                elif kind == "ptok":
                    V.tensor_copy(p_rows[0:PBUF, :], ps[0:PBUF])
                    last = V.tensor_copy(p_rows[32:32 + NS, :], banks(bank + 1)[0:NS])
                elif kind == "outer":
                    b = a[1]
                    dve.wait_ge(state_decayed, b + 1)
                    s = state_s[:, b % 4].rearrange("p h v -> p (h v)")
                    last = V.tensor_tensor(s, s, banks(bank, 2), ALU.add)
                elif kind == "o_turn":
                    group_norm(2, NS, banks(bank, 2))
                    last = None
                elif kind == "z":
                    j = a[1]
                    dve.wait_ge(act_took, GA0)
                    last = V.scalar_tensor_tensor(z_T[:, j], ps[:, 0:NT], gn_w[:, j:j + 1], z_T[:, j], ALU.mult,
                                                  ALU.mult)
                if last is not None:
                    last.then_inc(aux_took, 1)

            def group_norm(i, n, ps):
                for h in range(H):
                    step(V.bn_stats(stats[0:n, h], ps[0:n, h * DV:(h + 1) * DV]))
                step.wait()
                for h in range(H):
                    last = V.bn_aggr(moments[0:n, h], stats[0:n, h])
                last.then_inc(spread_ready, 1)
                dve.wait_ge(spread_rooted, i + 1)
                step(V.reciprocal(spread[0:n], spread[0:n]))
                step.wait()
                for h in range(H):
                    last = V.tensor_scalar(normed[0:n, i, h * DV:(h + 1) * DV], ps[0:n, h * DV:(h + 1) * DV],
                                           moments[0:n, h, 0:1], spread[0:n, h:h + 1], ALU.subtract, ALU.mult)
                last.then_inc(aux_took, 1)

            dve.wait_ge(rms_done, 3)
            for t, n in enumerate((P, P, 48)):
                step(V.reciprocal(rstd[0:n, t:t + 1], rms[0:n, t:t + 1]))
            step.wait()
            for t, n in enumerate((P, P, 48)):
                V.tensor_scalar(normed[0:n, t], tok[0:n, t], rstd[0:n, t:t + 1], None, ALU.mult).then_inc(x_scaled, 1)
            dve.wait_ge(params_turned, 1)
            V.tensor_copy(params[:, 0:28], psum[:, 0, 0:28]).then_inc(params_ready, 1)
            dve.wait_ge(params_turned, 2)
            V.tensor_copy(params[:, 28:28 + 512], psum[:, 3]).then_inc(params_ready, 1)

            for n in range(T_OUT):
                if K0 <= n < P0:
                    j = n - K0
                    dve.wait_ge(act_took, n + 1)
                    s = DK ** -0.5 if j < H else 1.0
                    x, y = rope_x[:, j % 2], rope_y[:, j % 2]
                    step(V.scalar_tensor_tensor(x, x, s, const("cos"), ALU.mult, ALU.mult))
                    step(V.scalar_tensor_tensor(y, y, s, const("sin"), ALU.mult, ALU.mult))
                    step.wait()
                    if j < H:
                        V.tensor_tensor(k_T[:, j], x, y, ALU.add).then_inc(roped, 1)
                    else:
                        h = j - H
                        step(V.tensor_tensor(q_s[:, h], x[:, NPR:NT], y[:, NPR:NT], ALU.add))
                        V.tensor_tensor(q_T[:, h], x[:, 0:NT], y[:, 0:NT], ALU.add).then_inc(roped, 1)
                        if h == H - 1:
                            dve.wait_ge(roped, 8)
                elif T_YB <= n < T_YA:
                    d = n - T_YB
                    dve.wait_ge(tile_done, n + 1)
                    dve.wait_ge(act_took, N_IN)
                    V.tensor_tensor(gate_b[:, d], psum[:, n % 3, 0:NT], gate_b[:, d], ALU.mult).then_inc(dve_took, 1)
                elif T_YA <= n:
                    d = n - T_YA
                    dve.wait_ge(tile_done, n + 1)
                    if d == 0:
                        dve.wait_ge(dve_took, T_YA - T_YB)
                    step(V.tensor_tensor(gate_a[:, d], psum[:, n % 3, 0:NT], gate_a[:, d], ALU.mult))
                    step.wait()
                    V.tensor_tensor(gate_a[:, d], gate_a[:, d], gate_b[:, d], ALU.add).then_inc(dve_took, 1)
                for a in AUX_AFTER[n]:
                    aux(a)
                if n == 33:
                    dve.wait_ge(outer_read, NS)
                    V.tensor_copy(hs_T.rearrange("p m b -> p (m b)"), psum[:, 3, 0:8 * NS]).then_inc(o_s_ready, 1)

            for n in range(T_OUT, T_END):
                dve.wait_ge(act_took, T_YB + n - T_OUT + 1)
                V.tensor_scalar(xn_T[:, n - T_OUT], y_T[:, n - T_OUT], norm_ffn[:, n - T_OUT:n - T_OUT + 1], None,
                                ALU.mult).then_inc(dve_took, 1)
            dve.wait_ge(rms_done, 6)
            for t, (_, n) in enumerate(TILES):
                step(V.reciprocal(rstd[0:n, t:t + 1], rms[0:n, t:t + 1]))
            step.wait()

            dve.wait_ge(logits_done, 1)
            dve.wait_ge(zeroed, 2)
            for t, (_, n) in enumerate(TILES):
                step(V.scalar_tensor_tensor(logits[0:n, t], psum[0:n, 1, t * NE:(t + 1) * NE], rstd[0:n, t:t + 1],
                                            b_router[0:n, :], ALU.mult, ALU.add))
            step.wait()
            for t, (_, n) in enumerate(TILES):
                step(V.max(top[0:n, t], logits[0:n, t]))
            step.wait()
            for t, (_, n) in enumerate(TILES):
                last = V.tensor_scalar(neg_top[0:n, t:t + 1], top[0:n, t, 0:1], -1.0, None, ALU.mult)
            last.then_inc(neg_ready, 1)
            for t, (_, n) in enumerate(TILES):
                step(V.max_index(top_i[0:n, t], top[0:n, t], logits[0:n, t]))
            step.wait()
            for t, (_, n) in enumerate(TILES):
                step(V.tensor_copy(top_f[0:n, t], top_i[0:n, t]))
            step.wait()
            for t in range(3):
                step(V.tensor_tensor(match[:, 4 * t:4 * t + 4],
                                     const("experts").rearrange("p (a e) -> p a e", a=1).broadcast_to([P, TOPK, NE]),
                                     top_f[:, t, 0:TOPK].rearrange("p (j a) -> p j a", a=1).broadcast_to(
                                         [P, TOPK, NE]), ALU.is_equal))
            step.wait()
            for t in range(3):
                last = V.tensor_reduce(chosen[:, t], match[:, 4 * t:4 * t + 4].rearrange("p j e -> p e j"), AX.X,
                                       ALU.add)
                if t == 2:
                    last.then_inc(chosen_ready, 1)
            dve.wait_ge(ffn_in, 16)
            for t, (_, n) in enumerate(TILES):
                parts = [(h_tok(t), slice(0, D))] if t < 2 else [(psum[:, 3], slice(0, 512)), (psum[:, 0], slice(512, D))]
                for h, c in parts:
                    V.scalar_tensor_tensor(normed[0:n, t, c], h[0:n], rstd[0:n, t:t + 1], w_ffn[0:n, c], ALU.mult,
                                           ALU.mult).then_inc(xn_ready, 1)
            dve.wait_ge(exp_ready, 3)
            dve.wait_ge(chosen_ready, 1)
            step(V.tensor_tensor(gates[:, :, :], expd[:, :, :], chosen[:, :, :], ALU.mult))
            step.wait()
            step(V.tensor_reduce(gate_sum, gates[:, :, :], AX.X, ALU.add))
            step.wait()
            step(V.tensor_scalar(gate_sum, gate_sum, 1e-30, None, ALU.max))
            step.wait()
            step(V.reciprocal(gate_rec, gate_sum))
            step.wait()
            V.tensor_tensor(gates[:, :, :], gates[:, :, :],
                            gate_rec.rearrange("p (t a) -> p t a", a=1).broadcast_to([P, 3, NE]),
                            ALU.mult).then_inc(gates_ready, 1)
            dve.wait_ge(gates_ready, 1)
            step(V.tensor_scalar(gates_s[:, :, :], gates[:, :, :], 1.0 / ALPHA, None, ALU.mult))
            step(V.tensor_scalar(place[:, :, 0:NE], chosen[:, :, :], -FAR, FAR, ALU.mult, ALU.add))
            step.wait()
            dve.wait_ge(placed, 1)
            step(V.tensor_tensor(place[:, 0:2, 0:NE], place[:, 0:2, 0:NE],
                                 psum[:, 2, 0:2 * NE].rearrange("p (t e) -> p t e", t=2), ALU.add))
            step(V.tensor_tensor(place[0:NS, 2, 0:NE], place[0:NS, 2, 0:NE], psum[0:NS, 2, 2 * NE:3 * NE], ALU.add))
            step.wait()
            V.tensor_scalar(place[:, :, NE:NE + 2], place[:, :, 0:2], float(CAP), None, ALU.subtract).then_inc(
                place_ready, 1)
            step(V.tensor_reduce(most, psum[0:1, 2, 3 * NE:4 * NE], AX.X, ALU.max))
            step.wait()
            step(V.tensor_scalar(beyond, const("passes")[0:1], most, float(NPAIR), ALU.is_lt, ALU.mult))
            step.wait()
            step(V.tensor_reduce(pairs_f, beyond, AX.X, ALU.add))
            step.wait()
            V.tensor_copy(pairs_i[0:1, 0:1], pairs_f).then_inc(pairs_ready, 1)

            loop = Steps(dve, dve_loop)
            iota = const("iota").rearrange("p (t j c) -> p t j c", t=1, j=1).broadcast_to([P, 3, 2, CAP])

            def bias(e, m0):
                return b_gu[:, bass.ds(e, 1), m0:m0 + KD].rearrange("p a (m c) -> p (a m) c", c=1).broadcast_to(
                    [P, KD, CAP])

            def split(it, *units):
                for u in units:
                    dve.wait_ge(split_hi, NU * it + u + 1)
                    V.tensor_tensor(lo_half(u), raw_half(u), stage_hi[u % STAGE][:, :].bitcast(F32),
                                    ALU.subtract).then_inc(split_lo, 1)

            def choose(r, p2):
                dve.wait_ge(place_ready, r + 1)
                V.tensor_tensor(one_hot, iota, place[:, :, bass.ds(p2, 2)].rearrange(
                    "p t (j c) -> p t j c", c=1).broadcast_to([P, 3, 2, CAP]), ALU.is_equal).then_inc(one_hot_ready, 1)

            def take_tokens(it):
                dve.wait_ge(x_hi, it + 1)
                V.tensor_tensor(x_parts[:, :, :, 1].rearrange("p k j c -> p (k j) c"),
                                banks(0, 2).rearrange("p (k c) -> p k c", c=CAP),
                                x_parts[:, :, :, 0].bitcast(F32).rearrange("p k j c -> p (k j) c"),
                                ALU.subtract).then_inc(x_lo, 1)

            def add_scattered(it, tiles):
                for d in tiles:
                    dve.wait_ge(scattered, KD * it + d + 1)
                    V.tensor_tensor(y_T[:, d], y_T[:, d], psum[:, 6 + d % 2, 0:NT], ALU.add).then_inc(y_added, 1)

            def swiglu(it, j, p):
                e, n = 2 * p + j, 2 * it + j
                dve.wait_ge(hidden_turned, 2 * n + 1)
                V.tensor_tensor(hg, psum[:, 6].rearrange("p (m c) -> p m c", m=KD), bias(e, 0),
                                ALU.add).then_inc(hidden_took, 1)
                dve.wait_ge(hidden_took, 2 * n + 1)
                V.tensor_scalar(hg, hg, LIMIT, None, ALU.min).then_inc(gate_clipped, 1)
                split(it, SWIGLU_AT[j])
                dve.wait_ge(hidden_turned, 2 * n + 2)
                V.tensor_tensor(hu, psum[:, 7].rearrange("p (m c) -> p m c", m=KD), bias(e, KD),
                                ALU.add).then_inc(hidden_took, 1)
                dve.wait_ge(hidden_took, 2 * n + 2)
                loop(V.tensor_scalar(hu, hu, LIMIT, -LIMIT, ALU.min, ALU.max))
                split(it, SWIGLU_AT[j] + 1)
                loop.wait()
                dve.wait_ge(silu_ready, n + 1)
                loop(V.scalar_tensor_tensor(hg, hu, 1.0, hs, ALU.add, ALU.mult))
                loop.wait()
                loop(V.tensor_copy(act_parts[:, :, 0], hg))
                loop.wait()
                V.tensor_tensor(act_parts[:, :, 1], hg, act_parts[:, :, 0].bitcast(F32), ALU.subtract).then_inc(
                    act_ready, 1)

            LOOP_STEPS = 6

            def pair(r, p):
                it = r * NPAIR + p
                loop.base, loop.n = it * LOOP_STEPS, 0
                split(it, 0, 1, 2, 3)
                for u in range(4, SWIGLU_AT[0]):
                    split(it, u)
                    if u - 2 in SCATTER_AFTER:
                        add_scattered(it, (SCATTER_AFTER.index(u - 2),))
                swiglu(it, 0, p)
                dve.wait_ge(gated_ready, it + 1)
                choose(r, 2 * p + 2)
                split(it, *range(SWIGLU_AT[0] + 2, SWIGLU_AT[1]))
                swiglu(it, 1, p)
                split(it, *range(SWIGLU_AT[1] + 2, NU))
                take_tokens(it + 1)
                assert loop.n == LOOP_STEPS

            choose(0, 0)
            take_tokens(0)
            dve.wait_ge(pairs_ready, 1)
            pairs = dve.value_load(pairs_i[0:1, 0:1], min_val=NPAIR, max_val=NPAIR * NPASS)
            with dve.Fori(0, NPASS) as r:
                with dve.If(pairs > r * NPAIR):
                    with dve.Fori(0, NPAIR) as p:
                        pair(r, p)
                    dve.wait_ge(one_hot_ready, (r + 1) * NPAIR + 1)
                    V.tensor_scalar(place[:, :, :], place[:, :, :], float(CAP), None, ALU.subtract).then_inc(
                        place_ready, 1)
            add_scattered(pairs, range(KD))

            dve.wait_ge(y_rms, 3)
            for t, (_, n) in enumerate(TILES):
                V.reciprocal(rstd[0:n, t:t + 1], rms[0:n, t:t + 1]).then_inc(y_rstd, 1)
            dve.wait_ge(y_rstd, 3)
            dve.wait_ge(final_in, 16)
            for t, (_, n) in enumerate(TILES):
                V.scalar_tensor_tensor(normed[0:n, t], banks(2 * t, 2)[0:n], rstd[0:n, t:t + 1], w_final[0:n], ALU.mult,
                                       ALU.mult).then_inc(y_ready, 1)


_INS = ["x_prompt", "x_sample", "state_ret", "state_pool", "meta_tokens", "norm_mix", "w_in", "ret_gn", "pool_w",
        "pool_scale", "w_ret_branch", "w_pool_branch", "w_out", "norm_ffn", "w_router", "b_router", "w_gate_up",
        "b_gate_up", "w_down", "b_down", "norm_final"]
_OUTS = [(1, NPR, D), (NS, 1, D), (1, 1, H, DK, DV), (1, 1, PBUF, PG * P), (1, NS, H, DK, DV), (1, NS, PBUF, PG * P)]


def kernel(**inputs):
    import numpy as _np
    import concourse.bacc as _bacc
    from concourse.bass_utils import run_bass_kernel_spmd as _run

    nc = _bacc.Bacc("TRN2", target_bir_lowering=False, num_devices=1)
    arrays = {f"in_{n}": _np.ascontiguousarray(inputs[n]) for n in _INS}
    arrays["in_consts"] = constants()
    ins = {n[3:]: nc.dram_tensor(n, a.shape, F32, kind="ExternalInput").ap() for n, a in arrays.items()}
    outs = [nc.dram_tensor(f"out_{i}", s, F32, kind="ExternalOutput").ap() for i, s in enumerate(_OUTS)]
    build(nc, ins, outs)
    r = _run(nc, [arrays], core_ids=[0])
    return tuple(r.results[0][f"out_{i}"] for i in range(len(_OUTS)))
```
